# Optimizing a Trainium2 kernel written in Bass

```python
import math
import jax
import jax.numpy as jnp
from jax import lax
import numpy as np

'''One post-norm DeepNorm hybrid layer of a chunk-causal streaming encoder.

Mixing sub-layer: Hymba-style parallel head groups. A single combined input projection
feeds a GLA head group (gated low-rank linear attention) and a RetNet head group
(multi-scale retention with rotary phases). Each group is per-head normalised and
swish-gated, the groups are concatenated and passed through one output projection.
Channel sub-layer: PEER product-key retrieval over n_keys^2 single-neuron experts.
Each sub-layer is followed by x <- LayerNorm(alpha * x + sublayer(x)).

Inputs: x (BATCH, SEQ, D_MODEL) float32 plus per-layer weights stacked on a leading DEPTH axis.
Output: (BATCH, SEQ, D_MODEL).
'''

D_MODEL = 2048
BATCH = 1
SEQ = 256
DEPTH = 1

CHUNK = 64
MIX_WIDTH = D_MODEL
GLA_HEADS = 4
GLA_DV = MIX_WIDTH // 2 // GLA_HEADS
GLA_DK = GLA_DV // 2
GLA_GATE_RANK = 16
GLA_TAU = 16.0
RET_HEADS = 4
RET_DV = MIX_WIDTH // 2 // RET_HEADS
RET_DK = RET_DV
ROPE_BASE = 10000.0
PEER_HEADS = 8
PEER_NKEYS = 128
PEER_N = PEER_NKEYS * PEER_NKEYS
PEER_QDIM = 256
PEER_TOPK = 16
PEER_TOKEN_BLOCK = 128
LN_EPS = 1e-5
DEEPNORM_ALPHA = (2 * DEPTH) ** 0.25
DEEPNORM_BETA = (8 * DEPTH) ** -0.25
PROJ_SIZES = (GLA_HEADS * GLA_DK, GLA_HEADS * GLA_DK, GLA_HEADS * GLA_DV, GLA_HEADS * GLA_DV, GLA_GATE_RANK,
              RET_HEADS * RET_DK, RET_HEADS * RET_DK, RET_HEADS * RET_DV, RET_HEADS * RET_DV)
PROJ_COLS = sum(PROJ_SIZES)
VALUE_SLOTS = (2, 7)

kernel_name = "hybrid_gla_retention_peer_block"

def _layer_norm(x, g, b):
    xf = x.astype(jnp.float32)
    mu = jnp.mean(xf, -1, keepdims=True)
    var = jnp.mean(jnp.square(xf - mu), -1, keepdims=True)
    return ((xf - mu) * lax.rsqrt(var + LN_EPS) * g + b).astype(x.dtype)

def _head_norm(o, gain, center):
    of = o.astype(jnp.float32)
    if center:
        of = of - jnp.mean(of, -1, keepdims=True)
    y = of * lax.rsqrt(jnp.mean(jnp.square(of), -1, keepdims=True) + LN_EPS)
    return y.reshape(o.shape[0], o.shape[1], -1) * gain

def _to_chunks(t):
    b, s, h, d = t.shape
    return t.reshape(b, s // CHUNK, CHUNK, h, d).transpose(1, 0, 3, 2, 4)

def _from_chunks(t):
    nc, b, h, c, d = t.shape
    return t.transpose(1, 0, 3, 2, 4).reshape(b, nc * c, h, d)

def _scan_states(decay, u):
    def step(s, inp):
        d_i, u_i = inp
        return d_i * s + u_i, s
    _, s_prev = lax.scan(step, jnp.zeros(u.shape[1:], u.dtype), (decay, u))
    return s_prev

def _rotary(t, pos):
    half = t.shape[-1] // 2
    inv = ROPE_BASE ** (-jnp.arange(half, dtype=jnp.float32) / half)
    ang = pos.astype(jnp.float32)[:, None] * inv[None, :]
    cos = jnp.cos(ang)[None, :, None, :]
    sin = jnp.sin(ang)[None, :, None, :]
    t1, t2 = t[..., :half], t[..., half:]
    return jnp.concatenate([t1 * cos - t2 * sin, t1 * sin + t2 * cos], -1).astype(t.dtype)

def _gla_chunk_causal(q, k, v, log_a):
    dk = q.shape[-1]
    qc = _to_chunks(q * dk ** -0.5)
    kc = _to_chunks(k)
    vc = _to_chunks(v)
    bc = jnp.cumsum(_to_chunks(log_a), axis=3)
    b_last = bc[:, :, :, -1:, :]
    u = jnp.einsum('nbhcd,nbhce->nbhde', kc * jnp.exp(b_last - bc), vc).astype(jnp.float32)
    s_prev = _scan_states(jnp.exp(b_last[:, :, :, 0, :])[..., None], u)
    o_inter = jnp.einsum('nbhcd,nbhde->nbhce', qc * jnp.exp(bc), s_prev)

    def intra(args):
        q_i, k_i, v_i, b_i = args
        dec = jnp.exp(-jnp.abs(b_i[:, :, :, None, :] - b_i[:, :, None, :, :]))
        a = jnp.einsum('bhnd,bhmd,bhnmd->bhnm', q_i, k_i, dec)
        return jnp.einsum('bhnm,bhme->bhne', a, v_i)

    o_intra = lax.map(intra, (qc, kc, vc, bc))
    return _from_chunks(o_inter + o_intra)

def _retention_chunk_causal(q, k, v):
    dk = q.shape[-1]
    h = q.shape[2]
    log_gamma = jnp.log(1.0 - 2.0 ** (-5.0 - jnp.arange(h, dtype=jnp.float32)))
    idx = jnp.arange(CHUNK, dtype=jnp.float32)
    qc = _to_chunks(q)
    kc = _to_chunks(k * dk ** -0.5)
    vc = _to_chunks(v)
    k_dec = jnp.exp(log_gamma[:, None] * (CHUNK - 1.0 - idx)[None, :])[None, None, :, :, None]
    q_dec = jnp.exp(log_gamma[:, None] * (idx + 1.0)[None, :])[None, None, :, :, None]
    d_intra = jnp.exp(log_gamma[:, None, None] * jnp.abs(idx[:, None] - idx[None, :]))
    u = jnp.einsum('nbhcd,nbhce->nbhde', kc * k_dec, vc).astype(jnp.float32)
    nc = qc.shape[0]
    chunk_decay = jnp.broadcast_to(jnp.exp(log_gamma * CHUNK)[None, None, :, None, None], (nc, 1, h, 1, 1))
    s_prev = _scan_states(chunk_decay, u)
    o_inter = jnp.einsum('nbhcd,nbhde->nbhce', qc, s_prev) * q_dec
    a = jnp.einsum('nbhcd,nbhmd->nbhcm', qc, kc) * d_intra
    o_intra = jnp.einsum('nbhcm,nbhme->nbhce', a, vc)
    return _from_chunks(o_inter + o_intra)

def _hybrid_mixer(h, w_in, w_gate_up, b_gate, gla_g, ret_g, w_out):
    b, s, _ = h.shape
    proj = jnp.einsum('bsd,dn->bsn', h, w_in)
    splits = np.cumsum(PROJ_SIZES)[:-1].tolist()
    gq, gk, gv, gr, glr, rq, rk, rv, rr = jnp.split(proj, splits, axis=-1)
    log_a = jax.nn.log_sigmoid((glr @ w_gate_up + b_gate).astype(jnp.float32)) / GLA_TAU
    o_gla = _gla_chunk_causal(gq.reshape(b, s, GLA_HEADS, GLA_DK), gk.reshape(b, s, GLA_HEADS, GLA_DK),
                              gv.reshape(b, s, GLA_HEADS, GLA_DV), log_a.reshape(b, s, GLA_HEADS, GLA_DK))
    o_gla = _head_norm(o_gla, gla_g, False) * jax.nn.silu(gr)
    pos = jnp.arange(s)
    o_ret = _retention_chunk_causal(_rotary(rq.reshape(b, s, RET_HEADS, RET_DK), pos),
                                    _rotary(rk.reshape(b, s, RET_HEADS, RET_DK), pos),
                                    rv.reshape(b, s, RET_HEADS, RET_DV))
    o_ret = _head_norm(o_ret, ret_g, True) * jax.nn.silu(rr)
    out = jnp.concatenate([o_gla, o_ret], axis=-1) @ w_out
    return out.astype(h.dtype)

def _peer(h, w_q, subkeys, u_tab, v_tab):
    b, s, d = h.shape
    t = b * s
    tb = PEER_TOKEN_BLOCK
    xt = h.reshape(t, d)
    q = (xt @ w_q).reshape(t, PEER_HEADS, 2, PEER_QDIM // 2)
    scores = jnp.einsum('thpd,hpkd->thpk', q, subkeys).astype(jnp.float32)
    vals, idx = lax.top_k(scores, PEER_TOPK)
    cand_s = (vals[:, :, 0, :, None] + vals[:, :, 1, None, :]).reshape(t, PEER_HEADS, -1)
    cand_i = (idx[:, :, 0, :, None] * PEER_NKEYS + idx[:, :, 1, None, :]).reshape(t, PEER_HEADS, -1)
    top_s, sel = lax.top_k(cand_s, PEER_TOPK)
    experts = jnp.take_along_axis(cand_i, sel, axis=-1).reshape(t // tb, tb, -1)
    gates = jax.nn.softmax(top_s, axis=-1).reshape(t // tb, tb, -1)

    def block(args):
        xb, eb, gb = args
        act = jax.nn.gelu(jnp.einsum('tkd,td->tk', u_tab[eb], xb).astype(jnp.float32), approximate=False)
        return jnp.einsum('tk,tkd->td', (gb * act).astype(xb.dtype), v_tab[eb])

    out = lax.map(block, (xt.reshape(t // tb, tb, d), experts, gates))
    return out.reshape(b, s, d).astype(h.dtype)

def setup_inputs(seed: int = 0) -> dict:
    key = jax.random.key(seed)
    ks = jax.random.split(key, 16)
    f32 = jnp.float32

    def nrm(k, shape, scale):
        return jax.random.normal(k, shape, f32) * scale

    col_scale = jnp.concatenate([jnp.full((n,), DEEPNORM_BETA if i in VALUE_SLOTS else 1.0, f32)
                                 for i, n in enumerate(PROJ_SIZES)])
    return {
        "x": nrm(ks[0], (BATCH, SEQ, D_MODEL), 1.0),
        "w_in": nrm(ks[1], (DEPTH, D_MODEL, PROJ_COLS), D_MODEL ** -0.5) * col_scale,
        "w_gla_gate_up": nrm(ks[2], (DEPTH, GLA_GATE_RANK, GLA_HEADS * GLA_DK), GLA_GATE_RANK ** -0.5),
        "b_gla_gate": nrm(ks[3], (DEPTH, GLA_HEADS * GLA_DK), 0.1),
        "gla_norm_g": 1.0 + nrm(ks[4], (DEPTH, GLA_HEADS * GLA_DV), 0.02),
        "ret_norm_g": 1.0 + nrm(ks[5], (DEPTH, RET_HEADS * RET_DV), 0.02),
        "w_out": nrm(ks[6], (DEPTH, MIX_WIDTH, D_MODEL), MIX_WIDTH ** -0.5 * DEEPNORM_BETA),
        "ln1_g": 1.0 + nrm(ks[7], (DEPTH, D_MODEL), 0.02),
        "ln1_b": nrm(ks[8], (DEPTH, D_MODEL), 0.02),
        "w_peer_q": nrm(ks[9], (DEPTH, D_MODEL, PEER_HEADS * PEER_QDIM), D_MODEL ** -0.5),
        "peer_subkeys": nrm(ks[10], (DEPTH, PEER_HEADS, 2, PEER_NKEYS, PEER_QDIM // 2), (PEER_QDIM // 2) ** -0.5),
        "peer_u": nrm(ks[11], (DEPTH, PEER_N, D_MODEL), D_MODEL ** -0.5),
        "peer_v": nrm(ks[12], (DEPTH, PEER_N, D_MODEL), DEEPNORM_BETA),
        "ln2_g": 1.0 + nrm(ks[13], (DEPTH, D_MODEL), 0.02),
        "ln2_b": nrm(ks[14], (DEPTH, D_MODEL), 0.02),
    }

def reference(x, w_in, w_gla_gate_up, b_gla_gate, gla_norm_g, ret_norm_g, w_out, ln1_g, ln1_b,
              w_peer_q, peer_subkeys, peer_u, peer_v, ln2_g, ln2_b):
    h = x
    for l in range(DEPTH):
        mix = _hybrid_mixer(h, w_in[l], w_gla_gate_up[l], b_gla_gate[l], gla_norm_g[l], ret_norm_g[l], w_out[l])
        h = _layer_norm(DEEPNORM_ALPHA * h + mix, ln1_g[l], ln1_b[l])
        ffn = _peer(h, w_peer_q[l], peer_subkeys[l], peer_u[l], peer_v[l])
        h = _layer_norm(DEEPNORM_ALPHA * h + ffn, ln2_g[l], ln2_b[l])
    return h


_drawn_inputs = setup_inputs


def setup_inputs(seed=0):
    import zlib

    import numpy as np

    out = dict(_drawn_inputs(seed))
    spreads = {}
    factors = {'gla_norm_g': 3.24, 'ret_norm_g': 3.302, 'ln2_g': 2.781, 'ln2_b': 2.788}
    for name, (base, spread) in spreads.items():
        noise = np.random.default_rng([zlib.crc32(name.encode()), seed]).standard_normal(out[name].shape)
        drawn = base * np.exp(spread * noise) if base else spread * noise
        out[name] = jnp.asarray(drawn.astype(out[name].dtype))
    for name, factor in factors.items():
        out[name] = (out[name] * factor).astype(out[name].dtype)
    return out
```

```python
import numpy as np
from contextlib import ExitStack
import concourse.bass as bass
from concourse import mybir

F32 = mybir.dt.float32
F32R = mybir.dt.float32r
U32 = mybir.dt.uint32
ALU = mybir.AluOpType
ACT = mybir.ActivationFunctionType
AX = mybir.AxisListType

P = 128
T, D = 256, 2048
TT, KT = T // P, D // P
CH = 64
NCH = T // CH
GH, GDK, GDV = 4, 128, 256
RH, RDK, RDV = 4, 256, 256
RANK = 16
PH, NK, TOPK = 8, 128, 16
COL = 512
EPS = 1e-5
ALPHA = 2 ** 0.25
LOW = -3.0e38

GQ, GV, GLR = 0, 1024, 3072
RQ, RV = GLR + RANK, GLR + RANK + 2048
U_ROUTE, U_ONES = 48, 64
A_END, B_END, O_END, Q_END = 6, 14, 18, 22
LEVELS = 6
SLOT = (0, 2, 1)

LOG_GAMMA = np.log(1.0 - 2.0 ** (-5.0 - np.arange(RH, dtype=np.float32))).astype(np.float32)
CHUNK_DECAY = np.exp(LOG_GAMMA * CH).astype(np.float32)

KEEP = {"ident": P, "iota": P, "iota16": TOPK, "one": 1}
MIX = {"cos": T, "sin": T, "scan": T, "masks": (LEVELS + 1) * P, "dintra": RH * P, "qdec": RH * T, "kdec": RH}


def constants():
    c = {}
    c["ident"] = np.eye(P, dtype=np.float32)
    c["iota"] = np.broadcast_to(np.arange(P, dtype=np.float32), (P, P))
    c["iota16"] = np.broadcast_to(np.arange(TOPK, dtype=np.float32), (P, TOPK))
    c["one"] = np.ones((P, 1))
    half = RDK // 2
    inv = np.float32(10000.0) ** (-np.arange(half, dtype=np.float32) / np.float32(half))
    ang = np.arange(T, dtype=np.float32)[None, :] * inv.astype(np.float32)[:, None]
    c["cos"], c["sin"] = np.cos(ang), np.sin(ang)
    t = np.arange(T)
    c["scan"] = np.broadcast_to((t % CH != 0).astype(np.float32), (P, T))
    m, n = np.meshgrid(np.arange(P), np.arange(P), indexing="ij")
    masks = [(m // (CH >> l) == n // (CH >> l)) & (m // (CH >> (l + 1)) != n // (CH >> (l + 1))) for l in range(LEVELS)]
    c["masks"] = np.concatenate([*masks, m == n], axis=1)
    same = m // CH == n // CH
    scale = np.float32(RDK ** -0.5)
    c["dintra"] = np.concatenate([np.where(same, np.exp(g * np.abs(m - n).astype(np.float32)), 0) * scale for g in LOG_GAMMA], axis=1)
    i = (t % CH).astype(np.float32)
    c["qdec"] = np.concatenate([np.broadcast_to(np.exp(g * (i + 1)), (P, T)) for g in LOG_GAMMA], axis=1)
    c["kdec"] = np.stack([np.exp(g * (CH - 1 - i[:P])) * scale for g in LOG_GAMMA], axis=1)
    pack = lambda names: np.ascontiguousarray(np.concatenate([c[k].astype(np.float32) for k in names], axis=1))
    return pack(KEEP), pack(MIX)


def build(nc, x, w_in, w_up, b_gate, gla_g, ret_g, w_out, ln1_g, ln1_b, w_q, subkeys, peer_u, peer_v,
          ln2_g, ln2_b, keep_c, mix_c, out):
    ctx = ExitStack()
    with ctx:
        sem = lambda name: ctx.enter_context(nc.semaphore(name))

        base = -(-nc.sbuf_base // 64) * 64
        K = 1024

        def at(name, off, shape, dt=F32):
            return nc.alloc_sbuf_tensor_at(name, shape, dt, offset=base + off)

        BIG, HT, WRK, CST = 0, 128 * K, 160 * K, 200 * K
        act_w = at("act_w", BIG, [P, P, T])
        xT_hi, xT_lo = at("xT_hi", HT, [P, KT, T], F32R), at("xT_lo", HT + 16 * K, [P, KT, T], F32R)
        raw = at("raw", BIG, [P, 4, 4 * COL])
        w_hi = at("w_hi", BIG + 32 * K, [P, 2, 4 * COL], F32R)
        w_lo = at("w_lo", BIG + 48 * K, [P, 2, 4 * COL], F32R)
        proj_t = at("proj_t", BIG + 64 * K, [P, TT, 8 * COL])
        proj_n = at("proj_n", BIG + 96 * K, [P, 24, T])
        states = at("states", BIG + 120 * K, [P, 2, NCH, GDV])
        mixc = at("mixc", WRK, [P, sum(MIX.values())])
        x_sb = at("x_sb", WRK + 13 * K, [P, TT, D])
        o_sb = at("o_sb", WRK + 13 * K, [P, TT, D])
        gains = at("gains", WRK + 29 * K, [P, D])
        glr_raw = at("glr_raw", WRK + 29 * K, [P, KT, P])
        glr_hi = at("glr_hi", BIG + 64 * K, [P, KT, P], F32R)
        glr_lo = at("glr_lo", BIG + 72 * K, [P, KT, P], F32R)
        wup = at("wup", WRK + 37 * K, [P, GH * GDK])
        small = at("small", CST + 17 * K // 4, [P, 256])
        keepc = at("keepc", CST, [P, sum(KEEP.values())])
        HL = BIG + 32 * K
        b_cum, lvl_e, lvl_q, lvl_k, q_in, k_out, k_outT, a_gla = (
            at(n, HL + 4 * K * i, [P, 4, T]) for i, n in enumerate(("b_cum", "lvl_e", "lvl_q", "lvl_k", "q_in", "k_out", "k_outT", "a_gla")))
        lvl_tmp = at("lvl_tmp", WRK + 29 * K, [P, 8, P])
        rot = at("rot", HT, [P, 8, 2, T])
        rq_dec = at("rq_dec", HT + 16 * K, [P, RH, 2, T])
        rkT = at("rkT", HT + 24 * K, [P, RH, TT, RDK])
        rot_tmp = at("rot_tmp", WRK + 13 * K, [P, 8, 2, T])
        a_ret = at("a_ret", HL + 8 * K, [P, RH * TT, P])
        silu_sb = at("silu_sb", BIG + 96 * K, [P, TT, D])
        y_sb = o_sb
        ln_g = at("ln_g", BIG + 64 * K, [P, D])
        ln_b = at("ln_b", BIG + 72 * K, [P, D])
        x_again = at("x_again", BIG + 80 * K, [P, TT, D])
        h1_perm = at("h1_perm", BIG + 80 * K, [P, TT, D])
        qT = at("qT", BIG + 64 * K, [P, 2 * PH, T])
        sk_raw = at("sk_raw", BIG + 96 * K, [P, 2 * PH, P])
        skT = at("skT", BIG + 104 * K, [P, 2 * PH, P])
        scores = at("scores", BIG + 80 * K, [P, TT, 2 * PH, NK])
        scores2 = at("scores2", BIG + 64 * K, [P, TT, 2 * PH, NK])
        cand = at("cand", BIG + 96 * K, [P, TT * PH, TOPK * TOPK])
        cand2 = at("cand2", BIG + 80 * K, [P, TT * PH, TOPK * TOPK])
        pick = at("pick", BIG + 64 * K, [P, TT * PH * TOPK, TOPK])
        vals = at("vals", BIG + 112 * K, [P, TT, 2 * PH, TOPK])
        idx_u = at("idx_u", BIG + 114 * K, [P, TT, 2 * PH, TOPK], U32)
        idx_f = at("idx_f", BIG + 116 * K, [P, TT, PH, 2, TOPK])
        tops = at("tops", BIG + 118 * K, [P, TT * PH, TOPK])
        sel_u = at("sel_u", BIG + 119 * K, [P, TT * PH, TOPK], U32)
        sel_ab = at("sel_ab", BIG + 120 * K, [P, 2, TT * PH, TOPK], U32)
        sel_f = at("sel_f", BIG + 122 * K, [P, 2, TT * PH, TOPK])
        ijg = at("ijg", BIG + 124 * K, [P, 3, TT, P])
        ijgT = at("ijgT", CST + 5 * K // 4, [P, 3, T])
        u_raw = at("u_raw", WRK, [P, 2, 4 * COL])
        u_t = at("u_t", WRK + 16 * K, [P, 4, 4 * P])
        u_lo = at("u_lo", WRK + 16 * K, [P, 4, 4 * P], F32R)
        u_hi = at("u_hi", WRK + 24 * K, [P, 4, 4 * P], F32R)
        gelu_sb = at("gelu_sb", CST + 21 * K // 4, [P, 2, T])
        hot_j = at("hot_j", WRK + 32 * K, [P, 2, 4, P])
        hot_i = at("hot_i", WRK + 36 * K, [P, 2, 4, P])
        v_raw = at("v_raw", HT, [P, 4, D])
        v_hi = at("v_hi", HT + 32 * K, [P, 2, D], F32R)
        v_lo = at("v_lo", HT + 48 * K, [P, 2, D], F32R)
        m_hi = at("m_hi", HT + 64 * K, [P, 2, T], F32R)
        m_lo = at("m_lo", HT + 66 * K, [P, 2, T], F32R)
        h1_again = at("h1_again", BIG, [P, TT, D])
        ln2g_sb = at("ln2g_sb", BIG + 16 * K, [P, D])
        ln2b_sb = at("ln2b_sb", BIG + 24 * K, [P, D])
        h1_dram = nc.dram_tensor("h1_dram", [T, D], F32, kind="Internal").ap()

        def cols(tensor, table, name):
            off = 0
            for k, n in table.items():
                if k == name:
                    return tensor[:, off:off + n]
                off += n

        ident = cols(keepc, KEEP, "ident")
        iota = cols(keepc, KEEP, "iota")
        one = cols(keepc, KEEP, "one")
        iota16 = cols(keepc, KEEP, "iota16")
        mc = lambda name: cols(mixc, MIX, name)

        bias4 = small[:, 0:4]
        stat6 = small[:, 8:8 + 96].rearrange("p (n s) -> p n s", s=6)
        mv = small[:, 104:136].rearrange("p (n s) -> p n s", s=2)
        rstd = small[:, 136:152]
        power = small[:, 152:168]
        var16 = small[:, 168:184]
        last_e = small[:, 184:200]
        gmax = small[:, 200:216]
        wup_sb = wup[0:RANK, :]
        glrT = at("glrT", CST + 5 * K // 4, [P, T])

        ps = ctx.enter_context(nc.psum_tensor("ps", [P, 8, 512], F32))

        def bank(i, n=1):
            return ps[:, i:i + n, :].rearrange("p a b -> p (a b)")

        const_in, x_in, glrw_in, wup_in = sem("const_in"), sem("x_in"), sem("glrw_in"), sem("wup_in")
        raw_in = [sem(f"raw_in{i}") for i in range(4)]
        raw_free, hi_done, lo_done, parts_free, acc_free = sem("raw_free"), sem("hi_done"), sem("lo_done"), sem("parts_free"), sem("acc_free")
        tr_done, tr_hi, tr_lo = sem("tr_done"), sem("tr_hi"), sem("tr_lo")
        glrw_hi, glrw_lo, glr_done, glrT_done, logit_done = (sem(n) for n in ("glrw_hi", "glrw_lo", "glr_done", "glrT_done", "logit_done"))
        neg_min, logsig_act, b_done, decay_act, decay_d, decay_done = (sem(n) for n in ("neg_min", "logsig_act", "b_done", "decay_act", "decay_d", "decay_done"))
        lvl_diff, lvl_exp, lvl_ready, lvl_mm, lvl_acc = (sem(n) for n in ("lvl_diff", "lvl_exp", "lvl_ready", "lvl_mm", "lvl_acc"))
        kt_mm, kt_sb, u_mm, s_done, o_mm, o_evac = (sem(n) for n in ("kt_mm", "kt_sb", "u_mm", "s_done", "o_mm", "o_evac"))
        rot_done, rkt_mm, rkt_sb, rs_mm, ra_done, ru_mm, rs_done, ro_mm, ro_evac = (
            sem(n) for n in ("rot_done", "rkt_mm", "rkt_sb", "rs_mm", "ra_done", "ru_mm", "rs_done", "ro_mm", "ro_evac"))
        stat_done, rstd_done, silu_done, mix_done, gains_in = (sem(n) for n in ("stat_done", "rstd_done", "silu_done", "mix_done", "gains_in"))
        x2_in, ln1_in, h1_done, h1_out = sem("x2_in"), sem("ln1_in"), sem("h1_done"), sem("h1_out")
        h1p_done = sem("h1p_done")
        sk_in, sk_mm, sk_sb, score_mm, score_sb = (sem(n) for n in ("sk_in", "sk_mm", "sk_sb", "score_mm", "score_sb"))
        soft_d, soft_e, ijg_done, ijg_mm, ijg_sb = (sem(n) for n in ("soft_d", "soft_e", "ijg_done", "ijg_mm", "ijg_sb"))
        u_in = [sem("u_in0"), sem("u_in1")]
        ut_done, uhi_done, ulo_done, uparts_free, gelu_done, gelu_free = (
            sem(n) for n in ("ut_done", "uhi_done", "ulo_done", "uparts_free", "gelu_done", "gelu_free"))
        hot_done, spread_mm, spread_free = sem("hot_done"), sem("spread_mm"), sem("spread_free")
        v_in = [sem(f"v_in{i}") for i in range(4)]
        v_hi_done, vraw_free, vparts_free = sem("v_hi_done"), sem("vraw_free"), sem("vparts_free")
        last_in, y_done, out_done = sem("last_in"), sem("y_done"), sem("out_done")
        ln_stat, ln_rstd = sem("ln_stat"), sem("ln_rstd")

        win = w_in[0]
        w_rows = lambda w, kq: w[kq * 4 * P:(kq + 1) * 4 * P, :].rearrange("(k p) n -> p k n", p=P)
        wq_rows = w_q[0].rearrange("(q f l) n -> q l f n", q=4, f=KT)
        u_rows = peer_u[0].rearrange("(i b l) (q d) -> i q l b d", b=4, l=32, q=4)
        v_rows = peer_v[0].rearrange("(i j) d -> i j d", j=P)

        def raw_count(g):
            return 16 * (g + 1) if not isinstance(g, int) or g < O_END else 16 * O_END + 64 * (g + 1 - O_END)

        block = ctx.enter_context(nc.Block())

        @block.sync
        def _(sp):
            sp.sem_inc(raw_free, 4)
            sp.dma_start(x_sb[:], x[0].rearrange("(a p) d -> p a d", p=P)).then_inc(x_in, 16)
            sp.dma_start(keepc[:], keep_c).then_inc(const_in, 16)
            sp.dma_start(glr_raw[:], win[:, GLR:GLR + P].rearrange("(k p) n -> p k n", p=P)).then_inc(glrw_in, 16)
            sp.dma_start(mixc[:], mix_c).then_inc(const_in, 16)
            sp.dma_start(wup_sb, w_up[0]).then_inc(wup_in, 16)
            with nc.allow_non_contiguous_dma(reason="512 bias values, one channel a partition"):
                sp.dma_start(bias4, b_gate[0].rearrange("(h p) -> p h", p=P)).then_inc(wup_in, 16)

            def load(g, w, col):
                for kq in range(4):
                    sp.wait_ge(raw_free, 4 * g + kq + 1)
                    sp.dma_start(raw[:, kq, :].rearrange("p (k n) -> p k n", k=4),
                                 w_rows(w, kq)[:, :, bass.ds(col, COL)]).then_inc(raw_in[kq], 16)

            for g in range(2):
                load(g, win, GQ + g * COL)
            with sp.Fori(2, A_END) as g:
                load(g, win, RQ + (g - 2) * COL)
            with sp.Fori(A_END, A_END + 4) as g:
                load(g, win, GV + (g - A_END) * COL)
            with sp.Fori(A_END + 4, B_END) as g:
                load(g, win, RV + (g - (A_END + 4)) * COL)
            sp.wait_ge(lvl_acc, LEVELS + 1)
            sp.dma_start(gains[:, 0:D // 2], gla_g[0:1, :].to_broadcast([P, D // 2])).then_inc(gains_in, 16)
            sp.dma_start(gains[:, D // 2:], ret_g[0:1, :].to_broadcast([P, D // 2])).then_inc(gains_in, 16)
            for g in range(B_END, O_END):
                load(g, w_out[0], (g - B_END) * COL)
                if g == B_END:
                    sp.wait_ge(mix_done, 2)
                    sp.dma_start(x_again[:], x[0].rearrange("(a p) d -> p a d", p=P)).then_inc(x2_in, 16)
                    sp.dma_start(ln_g[:], ln1_g[0:1, :].to_broadcast([P, D])).then_inc(ln1_in, 16)
                    sp.dma_start(ln_b[:], ln1_b[0:1, :].to_broadcast([P, D])).then_inc(ln1_in, 16)
            for g in range(O_END, Q_END):
                col = (g - O_END) * COL
                for kq in range(4):
                    sp.wait_ge(raw_free, 4 * g + kq + 1)
                    for q in range(4):
                        sp.dma_start(raw[32 * q:32 * q + 32, kq, :].rearrange("p (k n) -> p k n", k=4),
                                     wq_rows[q][:, 4 * kq:4 * kq + 4, col:col + COL]).then_inc(raw_in[kq], 16)
                if g == O_END:
                    sp.wait_ge(h1_done, 2)
                    sp.dma_start(sk_raw[:], subkeys[0].rearrange("h s k d -> k (h s) d")).then_inc(sk_in, 16)
                    sp.dma_start(h1_dram.rearrange("(a p) d -> p a d", p=P), y_sb[:]).then_inc(h1_out, 16)
            sp.wait_ge(h1_out, 16)
            sp.wait_ge(tr_lo, 24)
            def load_u(ii, s):
                for q in range(4):
                    sp.dma_start(u_raw[32 * q:32 * q + 32, s, :].rearrange("p (b d) -> p b d", b=4),
                                 u_rows[bass.ds(ii * 2 + s, 1), q].rearrange("i l b d -> l (i b) d")).then_inc(u_in[s], 16)

            load_u(0, 0)
            load_u(0, 1)
            with sp.Fori(1, P // 2) as ii:
                for s in range(2):
                    sp.wait_ge(ut_done, ii * 8 + 4 * s - 4)
                    load_u(ii, s)
            sp.sem_inc(vraw_free, 4)
            sp.wait_ge(uparts_free, 4 + 4 * P)
            with sp.Fori(0, P // 4) as ii:
                for s in range(4):
                    sp.wait_ge(vraw_free, ii * 4 + s + 1)
                    sp.dma_start(v_raw[:, s, :], v_rows[bass.ds(ii * 4 + s, 1)].rearrange("i j d -> j (i d)")).then_inc(v_in[s], 16)
            sp.wait_ge(vparts_free, 2 + 64)
            sp.dma_start(h1_again[:], h1_dram.rearrange("(a p) d -> p a d", p=P)).then_inc(last_in, 16)
            sp.dma_start(ln2g_sb[:], ln2_g[0:1, :].to_broadcast([P, D])).then_inc(last_in, 16)
            sp.dma_start(ln2b_sb[:], ln2_b[0:1, :].to_broadcast([P, D])).then_inc(last_in, 16)
            for a in range(TT):
                sp.wait_ge(y_done, a + 1)
                sp.dma_start(out[0, a * P:(a + 1) * P, :], h1_again[:, a, :]).then_inc(out_done, 16)
            sp.wait_ge(out_done, 16 * TT)

        def act_transposed(act, use):
            for c in range(KT // 2):
                q = use * 8 + c
                act.wait_ge(tr_done, q + 1)
                act.activation(xT_hi[:, 2 * c:2 * c + 2, :].rearrange("p a b -> p (a b)"), bank(4 + c % 4), ACT.Copy).then_inc(tr_hi, 1)

        def silu_sb_of(s):
            return silu_sb[:, :, s * K:(s + 1) * K]

        @block.scalar
        def _(act):
            act_transposed(act, 0)
            act.wait_ge(glrw_in, 16)
            act.activation(glr_hi[:], glr_raw[:], ACT.Copy).then_inc(glrw_hi, 1)
            act.wait_ge(glr_done, 1)
            act.activation(glrT[0:RANK, :], bank(4)[0:RANK, 0:T], ACT.Copy).then_inc(glrT_done, 1)

            def hi_step(g, kq):
                act.wait_ge(raw_in[kq], raw_count(g))
                act.wait_ge(parts_free, 4 * g + kq + 1)
                act.activation(w_hi[:, kq % 2, :], raw[:, kq, :], ACT.Copy).then_inc(hi_done, 1)

            def evac_n(g, par, dst, tile):
                act.wait_ge(parts_free, 2 + 4 * (g + 1))
                act.activation(dst[:, bass.ds(tile, 4), :], bank(2 * par, 2).rearrange("p (a b) -> p a b", a=4), ACT.Copy).then_inc(acc_free, 1)

            def evac_t(g, par, col):
                act.wait_ge(parts_free, 2 + 4 * (g + 1))
                act.activation(proj_t[:, :, bass.ds(col, COL)], ps[:, 2 * par:2 * par + 2, :], ACT.Copy).then_inc(acc_free, 1)

            def group_n(g, par, dst, g0, evac=True):
                for kq in range(4):
                    hi_step(g, kq)
                    if kq == 0 and evac:
                        evac_n(g - 1, 1 - par, dst, 4 * (g - 1 - g0))

            def group_t(g, par, evac=True):
                for kq in range(4):
                    hi_step(g, kq)
                    if kq == 0 and evac:
                        evac_t(g - 1, 1 - par, (g - 1 - A_END) * COL)

            group_n(0, 0, proj_n, 0, evac=False)
            group_n(1, 1, proj_n, 0)
            with act.Fori(1, A_END // 2) as j:
                for par in range(2):
                    group_n(j * 2 + par, par, proj_n, 0)
            evac_n(A_END - 1, 1, proj_n, 4 * (A_END - 1))
            group_t(A_END, 0, evac=False)
            group_t(A_END + 1, 1)
            with act.Fori(A_END // 2 + 1, B_END // 2) as j:
                for par in range(2):
                    group_t(j * 2 + par, par)
            evac_t(B_END - 1, 1, (B_END - 1 - A_END) * COL)

            act.wait_ge(logit_done, 1)
            act.wait_ge(wup_in, 32)
            act.wait_ge(parts_free, 2 + 4 * B_END)
            for h in range(GH):
                act.activation(lvl_e[:, h, :], bank(5, 2)[:, h * T:(h + 1) * T], ACT.Abs, bias=bias4[:, h:h + 1])
            act.drain()
            act.activation(lvl_q[:], lvl_e[:], ACT.Exp, scale=-1.0)
            act.drain()
            act.activation(lvl_k[:], lvl_q[:], ACT.Ln, bias=1.0).then_inc(logsig_act, 1)
            act.wait_ge(b_done, 1)
            act.activation(lvl_e[:], b_cum[:], ACT.Exp).then_inc(decay_act, 1)
            act.wait_ge(decay_d, 1)
            act.activation(lvl_k[:], lvl_q[:], ACT.Exp).then_inc(decay_act, 1)
            for l in range(LEVELS):
                act.wait_ge(lvl_diff, l + 1)
                act.activation(lvl_e[:], lvl_e[:], ACT.Abs)
                act.drain()
                act.activation(lvl_e[:], lvl_e[:], ACT.Exp, scale=-1.0).then_inc(lvl_exp, 1)
            act.wait_ge(kt_mm, 1)
            act.activation(k_outT[:].rearrange("p a b -> p (a b)"), bank(0, 2), ACT.Copy).then_inc(kt_sb, 1)
            for h in range(GH):
                act.wait_ge(o_mm, h + 1)
                act.activation(o_sb[:, :, h * GDV:(h + 1) * GDV], bank(2 + h % 2).rearrange("p (a e) -> p a e", a=TT), ACT.Copy).then_inc(o_evac, 1)
            for s in range(2):
                act.activation(silu_sb_of(s), proj_t[:, :, (2 * s + 1) * K:(2 * s + 2) * K], ACT.Sigmoid).then_inc(silu_done, 1)
            for h in range(RH):
                act.wait_ge(ro_mm, h + 1)
                act.activation(o_sb[:, :, K + h * RDV:K + (h + 1) * RDV], bank(2 + h % 2).rearrange("p (a e) -> p a e", a=TT), ACT.Copy).then_inc(ro_evac, 1)

            act_transposed(act, 1)
            for g in range(B_END, O_END):
                for kq in range(4):
                    hi_step(g, kq)
            for a in range(TT):
                act.wait_ge(h1_done, a + 1)
                act.activation(h1_perm[:, a, :].rearrange("p (f q l) -> p q f l", f=KT, q=4),
                               y_sb[:, a, :].rearrange("p (q f l) -> p q f l", f=KT, q=4), ACT.Copy).then_inc(h1p_done, 1)
            act_transposed(act, 2)
            group_n(O_END, 0, qT, O_END, evac=False)
            for g in range(O_END + 1, Q_END):
                group_n(g, g % 2, qT, O_END)
            evac_n(Q_END - 1, (Q_END - 1) % 2, qT, 4 * (Q_END - 1 - O_END))
            for c in range(4):
                act.wait_ge(sk_mm, c + 1)
                act.activation(skT[:, 4 * c:4 * c + 4, :].rearrange("p a b -> p (a b)"), bank(4 + c), ACT.Copy).then_inc(sk_sb, 1)
            for a in range(TT):
                act.wait_ge(score_mm, a + 1)
                act.activation(scores[:, a].rearrange("p a b -> p (a b)"), bank(4 * a, 4), ACT.Copy).then_inc(score_sb, 1)

            def gelu(i, par, far):
                act.wait_ge(uparts_free, 4 * i + 8)
                if far:
                    act.wait_ge(gelu_free, i - U_ONES + 1)
                    act.activation(gelu_sb[:, par, :], bank(par)[:, 0:T], ACT.Gelu).then_inc(gelu_done, 1)
                else:
                    act.activation(act_w[:, bass.ds(i, 1), :].rearrange("p a t -> p (a t)"), bank(par)[:, 0:T], ACT.Gelu).then_inc(gelu_done, 1)

            def u_tile(i, par, evac=True, far=False):
                for f in range(4):
                    act.wait_ge(ut_done, 4 * i + f + 1)
                    act.activation(u_hi[:, f, :], u_t[:, f, :], ACT.Copy).then_inc(uhi_done, 1)
                if evac:
                    gelu(i - 1, 1 - par, far)

            u_tile(0, 0, evac=False)
            u_tile(1, 1)
            with act.Fori(1, (U_ROUTE - 12) // 2) as ii:
                for s in range(2):
                    u_tile(ii * 2 + s, s)
            act.wait_ge(soft_d, 1)
            act.activation(tops[:], tops[:], ACT.Exp).then_inc(soft_e, 1)
            with act.Fori((U_ROUTE - 12) // 2, U_ROUTE // 2) as ii:
                for s in range(2):
                    u_tile(ii * 2 + s, s)
            act.wait_ge(ijg_mm, 1)
            act.activation(ijgT[:].rearrange("p a b -> p (a b)"), bank(4, 2)[:, 0:3 * T], ACT.Copy).then_inc(ijg_sb, 1)
            with act.Fori(U_ROUTE // 2, U_ONES // 2) as ii:
                for s in range(2):
                    u_tile(ii * 2 + s, s)
            act.sem_inc(gelu_free, 2)
            u_tile(U_ONES, 0)
            u_tile(U_ONES + 1, 1, far=True)
            with act.Fori(U_ONES // 2 + 1, P // 2) as ii:
                for s in range(2):
                    u_tile(ii * 2 + s, s, far=True)
            gelu(P - 1, 1, True)

            act.wait_ge(gelu_free, 2 + P - U_ONES)
            with act.Fori(0, P // 4) as ii:
                for s in range(4):
                    i = ii * 4 + s
                    act.wait_ge(v_in[s], ii * 16 + 16)
                    act.wait_ge(vparts_free, i + 1)
                    act.activation(m_hi[:, s % 2, :], act_w[:, bass.ds(i, 1), :].rearrange("p a t -> p (a t)"), ACT.Copy)
                    act.activation(v_hi[:, s % 2, :], v_raw[:, s, :], ACT.Copy).then_inc(v_hi_done, 1)

        def layer_norm(dve, y, gain, shift, use, done):
            for a in range(TT):
                for c in range(4):
                    dve.bn_stats(stat6[:, 4 * a + c, :], y[:, a, c * 512:(c + 1) * 512])
            dve.drain()
            for a in range(TT):
                dve.bn_aggr(mv[:, a, :], stat6[:, 4 * a:4 * a + 4, :])
            dve.drain()
            dve.tensor_scalar(var16[:, 0:TT], mv[:, 0:TT, 1], EPS, None, ALU.add).then_inc(ln_stat, 1)
            dve.wait_ge(ln_rstd, use + 1)
            for a in range(TT):
                dve.tensor_scalar(y[:, a, :], y[:, a, :], mv[:, a, 0:1], rstd[:, a:a + 1], ALU.subtract, ALU.mult)
            dve.drain()
            for a in range(TT):
                dve.tensor_tensor(y[:, a, :], y[:, a, :], gain[:], ALU.mult)
            dve.drain()
            for a in range(TT):
                dve.tensor_tensor(y[:, a, :], y[:, a, :], shift[:], ALU.add).then_inc(done, 1)

        def dve_transposed(dve, use):
            for c in range(KT // 2):
                q = use * 8 + c
                dve.wait_ge(tr_hi, q + 1)
                sl = slice(2 * c, 2 * c + 2)
                dve.tensor_tensor(xT_lo[:, sl, :].rearrange("p a b -> p (a b)"), bank(4 + c % 4),
                                  xT_hi[:, sl, :].rearrange("p a b -> p (a b)").bitcast(F32), ALU.subtract).then_inc(tr_lo, 1)

        @block.vector
        def _(dve):
            dve.memset(power[:], -0.5)
            dve_transposed(dve, 0)
            dve.wait_ge(glrw_hi, 1)
            dve.tensor_tensor(glr_lo[:], glr_raw[:], glr_hi[:].bitcast(F32), ALU.subtract).then_inc(glrw_lo, 1)

            def lo_step(g, kq):
                dve.wait_ge(hi_done, 4 * g + kq + 1)
                dve.tensor_tensor(w_lo[:, kq % 2, :], raw[:, kq, :], w_hi[:, kq % 2, :].bitcast(F32), ALU.subtract).then_inc(raw_free, 1)

            with dve.Fori(0, B_END) as g:
                for kq in range(4):
                    lo_step(g, kq)

            dve.wait_ge(acc_free, 2 + B_END)
            dve.wait_ge(const_in, 32)
            both = proj_n[:, 8:24, :].rearrange("p (h s) t -> p h s t", s=2)
            cos8 = mc("cos").unsqueeze(1).to_broadcast([P, 8, T])
            sin8 = mc("sin").unsqueeze(1).to_broadcast([P, 8, T])
            dve.wait_ge(parts_free, 2 + 4 * B_END)
            dve.tensor_tensor(rot[:, :, 0, :], both[:, :, 0, :], cos8, ALU.mult)
            dve.tensor_tensor(rot[:, :, 1, :], both[:, :, 0, :], sin8, ALU.mult)
            dve.tensor_tensor(rot_tmp[:, :, 0, :], both[:, :, 1, :], sin8, ALU.mult)
            dve.tensor_tensor(rot_tmp[:, :, 1, :], both[:, :, 1, :], cos8, ALU.mult)
            dve.drain()
            dve.tensor_tensor(rot[:, :, 0, :], rot[:, :, 0, :], rot_tmp[:, :, 0, :], ALU.subtract)
            dve.tensor_tensor(rot[:, :, 1, :], rot[:, :, 1, :], rot_tmp[:, :, 1, :], ALU.add).then_inc(rot_done, 1)
            dve.drain()
            qdec = mc("qdec").rearrange("p (h t) -> p h t", h=RH).unsqueeze(2).to_broadcast([P, RH, 2, T])
            dve.tensor_tensor(rq_dec[:], rot[:, 0:RH], qdec, ALU.mult).then_inc(rot_done, 1)

            dve.wait_ge(logit_done, 1)
            dve.wait_ge(wup_in, 32)
            dve.wait_ge(logsig_act, 1)
            for h in range(GH):
                dve.tensor_scalar(k_out[:, h, :], bank(5, 2)[:, h * T:(h + 1) * T], bias4[:, h:h + 1], 0.0, ALU.add, ALU.min)
            dve.drain()
            dve.tensor_tensor(k_out[:], k_out[:], lvl_k[:], ALU.subtract)
            dve.drain()
            for h in range(GH):
                dve.tensor_tensor_scan(b_cum[:, h, :], mc("scan"), k_out[:, h, :], 0.0, ALU.mult, ALU.add)
            dve.drain()
            dve.tensor_scalar(b_cum[:], b_cum[:], 1.0 / 16.0, None, ALU.mult).then_inc(b_done, 1)
            dve.drain()
            chunks = lambda t: t[:].rearrange("p h (c n) -> p (h c) n", n=CH)
            dve.tensor_tensor(chunks(lvl_q), chunks(b_cum)[:, :, CH - 1:CH].to_broadcast([P, GH * NCH, CH]), chunks(b_cum), ALU.subtract).then_inc(decay_d, 1)
            gq, gk = proj_n[:, 0:4, :], proj_n[:, 4:8, :]
            dve.tensor_scalar(gq, gq, float(np.float32(GDK ** -0.5)), None, ALU.mult)
            dve.wait_ge(decay_act, 2)
            dve.drain()
            dve.tensor_copy(last_e, chunks(lvl_e)[:, :, CH - 1])
            dve.tensor_tensor(q_in[:], gq, lvl_e[:], ALU.mult)
            dve.tensor_tensor(k_out[:], gk, lvl_k[:], ALU.mult).then_inc(decay_done, 1)
            dve.drain()
            masks = mc("masks").rearrange("p (l n) -> p l n", l=LEVELS + 1)

            def gather_level(l):
                dve.wait_ge(lvl_mm, l + 1)
                m8 = masks[:, l:l + 1, :].to_broadcast([P, 8, P])
                s = bank(4 + 2 * (l % 2), 2).rearrange("p (a b) -> p a b", a=8)
                a8 = a_gla[:].rearrange("p h (a b) -> p (h a) b", b=P)
                if l == 0:
                    dve.tensor_tensor(a8, s, m8, ALU.mult).then_inc(lvl_acc, 1)
                else:
                    dve.wait_ge(lvl_acc, l)
                    dve.tensor_tensor(lvl_tmp[:], s, m8, ALU.mult)
                    dve.drain()
                    dve.tensor_tensor(a8, a8, lvl_tmp[:], ALU.add).then_inc(lvl_acc, 1)

            for l in range(LEVELS):
                m = CH >> (l + 1)
                blocks = lambda t: t[:].rearrange("p h (c n) -> p (h c) n", n=2 * m)
                bb = blocks(b_cum)
                if l:
                    dve.wait_ge(lvl_ready, l)
                dve.tensor_tensor(blocks(lvl_e), bb, bb[:, :, m - 1:m].to_broadcast([P, GH * T // (2 * m), 2 * m]), ALU.subtract).then_inc(lvl_diff, 1)
                if l:
                    gather_level(l - 1)
                dve.wait_ge(lvl_exp, l + 1)
                dve.tensor_tensor(lvl_q[:], gq, lvl_e[:], ALU.mult)
                dve.tensor_tensor(lvl_k[:], gk, lvl_e[:], ALU.mult).then_inc(lvl_ready, 1)
            gather_level(LEVELS - 1)
            gather_level(LEVELS)

            kdec = mc("kdec")
            for h in range(RH):
                dve.wait_ge(rkt_mm, h + 1)
                dve.tensor_scalar(rkT[:, h].rearrange("p a d -> p (a d)"), bank(4 + h), kdec[:, h:h + 1], None, ALU.mult).then_inc(rkt_sb, 1)

            dve.memset(states[:, :, 0, :], 0.0)
            for h in range(GH):
                dve.wait_ge(u_mm, h + 1)
                if h >= 2:
                    dve.wait_ge(o_mm, h - 1)
                s = states[:, h % 2]
                u = lambda c: bank(0, 2)[:, SLOT[c] * GDV:(SLOT[c] + 1) * GDV]
                dve.tensor_copy(s[:, 1, :], u(0))
                for c in (1, 2):
                    dve.drain()
                    ins = dve.scalar_tensor_tensor(s[:, c + 1, :], s[:, c, :], last_e[:, h * NCH + c:h * NCH + c + 1], u(c), ALU.mult, ALU.add)
                ins.then_inc(s_done, 1)

            dintra = mc("dintra").rearrange("p (h n) -> p h n", h=RH)
            dve.wait_ge(rs_mm, 1)
            a4 = a_ret[:].rearrange("p (h a) n -> p h a n", h=RH)
            dve.tensor_tensor(a4, bank(0, 2).rearrange("p (h a n) -> p h a n", h=RH, a=TT), dintra.unsqueeze(2).to_broadcast([P, RH, TT, P]), ALU.mult).then_inc(ra_done, 1)
            for h in range(RH):
                dve.wait_ge(ru_mm, h + 1)
                dve.wait_ge(o_mm if h == 0 else ro_mm, GH if h == 0 else h)
                u6 = bank(4, 3).rearrange("p (c s e) -> p c s e", c=3, s=2)
                dve.tensor_copy(states[:, :, 1, :], u6[:, SLOT[0]])
                for c in (1, 2):
                    dve.drain()
                    ins = dve.scalar_tensor_tensor(states[:, :, c + 1, :], states[:, :, c, :], float(CHUNK_DECAY[h]), u6[:, SLOT[c]], ALU.mult, ALU.add)
                ins.then_inc(rs_done, 1)

            dve.wait_ge(o_evac, GH)
            dve.wait_ge(ro_evac, RH)
            for a in range(TT):
                for h in range(8):
                    dve.bn_stats(stat6[:, a * 8 + h, :], o_sb[:, a, h * GDV:(h + 1) * GDV])
            dve.drain()
            for n in range(16):
                dve.bn_aggr(mv[:, n, :], stat6[:, n:n + 1, :])
            dve.drain()
            v16 = var16[:].rearrange("p (a h) -> p a h", a=TT)
            mva = mv[:].rearrange("p (a h) s -> p a h s", a=TT)
            dve.tensor_tensor(v16[:, :, 0:4], mva[:, :, 0:4, 0], mva[:, :, 0:4, 0], ALU.mult)
            dve.tensor_copy(v16[:, :, 4:8], mva[:, :, 4:8, 1])
            dve.drain()
            dve.tensor_tensor(v16[:, :, 0:4], v16[:, :, 0:4], mva[:, :, 0:4, 1], ALU.add)
            dve.drain()
            dve.tensor_scalar(var16[:], var16[:], EPS, None, ALU.add).then_inc(stat_done, 1)
            dve.wait_ge(rstd_done, 1)
            for a in range(TT):
                for h in range(8):
                    n = a * 8 + h
                    o = o_sb[:, a, h * GDV:(h + 1) * GDV]
                    if h < GH:
                        dve.tensor_scalar(o, o, rstd[:, n:n + 1], None, ALU.mult)
                    else:
                        dve.tensor_scalar(o, o, mv[:, n, 0:1], rstd[:, n:n + 1], ALU.subtract, ALU.mult)
            dve.wait_ge(silu_done, 2)
            for s in range(2):
                dve.tensor_tensor(silu_sb_of(s), silu_sb_of(s), proj_t[:, :, (2 * s + 1) * K:(2 * s + 2) * K], ALU.mult)
            dve.wait_ge(gains_in, 32)
            dve.drain()
            for a in range(TT):
                dve.tensor_tensor(o_sb[:, a, :], o_sb[:, a, :], gains[:], ALU.mult)
            dve.drain()
            for a in range(TT):
                dve.tensor_tensor(o_sb[:, a, :], o_sb[:, a, :], silu_sb[:, a, :], ALU.mult).then_inc(mix_done, 1)
            dve_transposed(dve, 1)

            def evac_y(g):
                col = (g - B_END) * COL
                dve.wait_ge(parts_free, 2 + 4 * (g + 1))
                dve.scalar_tensor_tensor(y_sb[:, :, col:col + COL], x_again[:, :, col:col + COL], float(ALPHA),
                                         ps[:, 2 * (g % 2):2 * (g % 2) + 2, :], ALU.mult, ALU.add).then_inc(acc_free, 1)

            for g in range(B_END, O_END):
                for kq in range(4):
                    lo_step(g, kq)
                    if kq == 0 and g > B_END:
                        dve.wait_ge(x2_in, 16)
                        evac_y(g - 1)
            evac_y(O_END - 1)
            dve.drain()
            dve.wait_ge(ln1_in, 32)
            layer_norm(dve, y_sb, ln_g, ln_b, 0, h1_done)
            dve_transposed(dve, 2)
            with dve.Fori(O_END, Q_END) as g:
                for kq in range(4):
                    lo_step(g, kq)

            def u_quarter(ii, s, f):
                if f == 0:
                    dve.wait_ge(u_in[s], ii * 64 + 64)
                dve.wait_ge(uparts_free, ii * 8 + 4 * s + f + 1)
                dve.transpose(u_t[:, f, :].rearrange("p (f b l) -> p b f l", f=4, b=4),
                              u_raw[:, s, :].rearrange("p (b f l) -> p b f l", b=4, l=32)[:, :, 4 * f:4 * f + 4, :]).then_inc(ut_done, 1)

            def route_best(stage, part):
                a, rows = part // 2, range(8 * (part % 2), 8 * (part % 2) + 8)
                sums = range(4 * part, 4 * part + 4)
                dve.drain()
                if stage == 0:
                    if part % 2 == 0:
                        dve.wait_ge(score_sb, a + 1)
                    for r in rows:
                        dve.max(vals[:, a, r, 0:8], scores[:, a, r, :])
                elif stage == 1:
                    for r in rows:
                        dve.max_index(idx_u[:, a, r, 0:8], vals[:, a, r, 0:8], scores[:, a, r, :])
                        dve.match_replace(scores2[:, a, r, :], vals[:, a, r, 0:8], scores[:, a, r, :], LOW)
                elif stage == 2:
                    for r in rows:
                        dve.max(vals[:, a, r, 8:16], scores2[:, a, r, :])
                elif stage == 3:
                    v = vals[:, a].rearrange("p (h s) k -> p h s k", s=2)
                    for r in rows:
                        dve.max_index(idx_u[:, a, r, 8:16], vals[:, a, r, 8:16], scores2[:, a, r, :])
                    for n in sums:
                        h = n % PH
                        dve.tensor_tensor(cand[:, n, :].rearrange("p (a b) -> p a b", a=TOPK),
                                          v[:, h, 0, :].unsqueeze(2).to_broadcast([P, TOPK, TOPK]),
                                          v[:, h, 1, :].unsqueeze(1).to_broadcast([P, TOPK, TOPK]), ALU.add)
                elif stage == 4:
                    for n in sums:
                        dve.max(tops[:, n, 0:8], cand[:, n, :])
                elif stage == 5:
                    for n in sums:
                        dve.max_index(sel_u[:, n, 0:8], tops[:, n, 0:8], cand[:, n, :])
                        dve.match_replace(cand2[:, n, :], tops[:, n, 0:8], cand[:, n, :], LOW)
                elif stage == 6:
                    for n in sums:
                        dve.max(tops[:, n, 8:16], cand2[:, n, :])
                else:
                    for n in sums:
                        dve.max_index(sel_u[:, n, 8:16], tops[:, n, 8:16], cand2[:, n, :])

            def route_split():
                dve.drain()
                dve.tensor_copy(gmax[:], tops[:, :, 0])
                dve.tensor_copy(idx_f[:].rearrange("p a h s k -> p (a h s k)"), idx_u[:].rearrange("p a r k -> p (a r k)"))
                dve.tensor_scalar(sel_ab[:, 0], sel_u[:], 4, None, ALU.logical_shift_right)
                dve.tensor_scalar(sel_ab[:, 1], sel_u[:], 15, None, ALU.bitwise_and)
                dve.drain()
                dve.tensor_tensor(tops[:], tops[:], gmax[:].unsqueeze(2).to_broadcast([P, TT * PH, TOPK]), ALU.subtract).then_inc(soft_d, 1)
                dve.tensor_copy(sel_f[:], sel_ab[:])

            def route_pick(s, a, stage):
                rows = slice(a * P, (a + 1) * P)
                dve.drain()
                if stage == 0:
                    dve.tensor_tensor(pick[:, rows], sel_f[:, s, a * PH:(a + 1) * PH].rearrange("p n k -> p (n k)").unsqueeze(2).to_broadcast([P, P, TOPK]),
                                      iota16.unsqueeze(1).to_broadcast([P, P, TOPK]), ALU.is_equal)
                elif stage == 1:
                    p4 = pick[:, rows].rearrange("p (h k) a -> p h k a", h=PH)
                    dve.tensor_tensor(p4, p4, idx_f[:, a, :, s, :].unsqueeze(2).to_broadcast([P, PH, TOPK, TOPK]), ALU.mult)
                else:
                    dve.tensor_reduce(ijg[:, s, a], pick[:, rows], AX.X, ALU.add)

            def route_gates():
                dve.wait_ge(soft_e, 1)
                dve.drain()
                dve.tensor_reduce(gmax[:], tops[:], AX.X, ALU.add)
                dve.drain()
                dve.reciprocal(rstd[:], gmax[:])
                dve.drain()
                dve.tensor_tensor(ijg[:, 2].rearrange("p a (h k) -> p (a h) k", k=TOPK), tops[:],
                                  rstd[:].unsqueeze(2).to_broadcast([P, TT * PH, TOPK]), ALU.mult).then_inc(ijg_done, 1)

            for i in range(U_ROUTE):
                for f in range(4):
                    u_quarter(i // 2, i % 2, f)
                if i < 32:
                    route_best(i // 4, i % 4)
                elif i == 32:
                    route_split()
                elif i < 45:
                    route_pick((i - 33) // 6, (i - 33) // 3 % 2, (i - 33) % 3)
                elif i == 45:
                    route_gates()
            dve.wait_ge(ijg_sb, 1)
            with dve.Fori(U_ROUTE // 2, U_ONES // 2) as ii:
                for s in range(2):
                    for f in range(4):
                        u_quarter(ii, s, f)
                    dve.tensor_copy(act_w[:, bass.ds(U_ONES + (ii * 2 + s - U_ROUTE) * 4, 4), :], one.unsqueeze(2).to_broadcast([P, 4, T]))

            grid = act_w[:].rearrange("p i t -> p t i")

            def hot(q, r, ks):
                for k in ks:
                    if k == 0:
                        dve.wait_ge(spread_mm, q + 1)
                    t = bass.ds(q * 4 + k, 1)
                    dve.tensor_scalar(hot_j[:, r, k, :], iota, ijgT[:, 1, t], None, ALU.is_equal)
                    ins = dve.tensor_scalar(hot_i[:, r, k, :], iota, ijgT[:, 0, t], ijgT[:, 2, t], ALU.is_equal, ALU.mult)
                if ks[-1] == 3:
                    ins.then_inc(hot_done, 1)

            def spread(q, r):
                dve.drain()
                dve.wait_ge(spread_mm, 2 + q + 1)
                g4 = grid[:, bass.ds(q * 4, 4), :]
                dve.tensor_tensor(g4, g4, bank(2 + r).rearrange("p (t i) -> p t i", t=4), ALU.mult).then_inc(spread_free, 1)

            def weigh(i, s):
                dve.drain()
                dve.wait_ge(gelu_done, i + 1)
                row = act_w[:, bass.ds(i, 1), :].rearrange("p a t -> p (a t)")
                dve.tensor_tensor(row, row, gelu_sb[:, s, :], ALU.mult).then_inc(gelu_free, 1)

            def u_spread_tile(ii, s, first=False):
                q = ii * 2 + s - U_ONES
                u_quarter(ii, s, 0)
                hot(q, s, (0, 1))
                u_quarter(ii, s, 1)
                hot(q, s, (2, 3))
                u_quarter(ii, s, 2)
                if first and s == 1:
                    dve.wait_ge(gelu_done, U_ONES)
                if not (first and s == 0):
                    spread(q - 1, 1 - s)
                u_quarter(ii, s, 3)
                if not first:
                    weigh(ii * 2 + s - 2, s)

            dve.sem_inc(spread_mm, 2)
            for s in range(2):
                u_spread_tile(U_ONES // 2, s, first=True)
            with dve.Fori(U_ONES // 2 + 1, P // 2) as ii:
                for s in range(2):
                    u_spread_tile(ii, s)
            spread(P - U_ONES - 1, 1)
            weigh(P - 2, 0)
            weigh(P - 1, 1)

            with dve.Fori(0, P // 4) as ii:
                for s in range(4):
                    i = ii * 4 + s
                    dve.wait_ge(v_hi_done, i + 1)
                    dve.tensor_tensor(m_lo[:, s % 2, :], act_w[:, bass.ds(i, 1), :].rearrange("p a t -> p (a t)"), m_hi[:, s % 2, :].bitcast(F32), ALU.subtract)
                    dve.tensor_tensor(v_lo[:, s % 2, :], v_raw[:, s, :], v_hi[:, s % 2, :].bitcast(F32), ALU.subtract).then_inc(vraw_free, 1)
            dve.wait_ge(last_in, 48)
            dve.wait_ge(vparts_free, 2 + P)
            for a in range(TT):
                dve.scalar_tensor_tensor(h1_again[:, a, :], h1_again[:, a, :], float(ALPHA), bank(4 * a, 4), ALU.mult, ALU.add)
            dve.drain()
            layer_norm(dve, h1_again, ln2g_sb, ln2b_sb, 1, y_done)

        @block.gpsimd
        def _(pool):
            pool.wait_ge(stat_done, 1)
            pool.tensor_tensor(rstd[:], var16[:], power[:], ALU.pow).then_inc(rstd_done, 1)
            def ln_power(use):
                pool.wait_ge(ln_stat, use + 1)
                pool.tensor_tensor(rstd[:, 0:TT], var16[:, 0:TT], power[:, 0:TT], ALU.pow).then_inc(ln_rstd, 1)

            ln_power(0)
            with pool.Fori(0, P) as i:
                for f in range(4):
                    pool.wait_ge(uhi_done, i * 4 + f + 1)
                    pool.tensor_tensor(u_lo[:, f, :], u_t[:, f, :], u_hi[:, f, :].bitcast(F32), ALU.subtract).then_inc(ulo_done, 1)
            ln_power(1)

        @block.tensor
        def _(pe):
            def transposed(src, use, tiles):
                for c in range(KT // 2):
                    q = use * 8 + c
                    if c >= 4:
                        pe.wait_ge(tr_lo, q - 3)
                    for k in range(2):
                        for a in range(TT):
                            o = (k * TT + a) * P
                            ins = pe.transpose(bank(4 + c % 4)[:, o:o + P], tiles(src, a, 2 * c + k), ident)
                    ins.then_inc(tr_done, 1)

            by_tile = lambda s, a, k: s[:, a, k * P:(k + 1) * P]

            def three(o, lh, ll, rh, rl, start, stop, lint=False):
                pe.matmul(o, lh, rh, start=start, stop=False, skip_group_check=lint)
                pe.matmul(o, lh, rl, start=False, stop=False, skip_group_check=lint)
                return pe.matmul(o, ll, rh, start=False, stop=stop, skip_group_check=lint)

            def steps_n(g, par):
                pe.wait_ge(acc_free, g + 1)
                for kq in range(4):
                    pe.wait_ge(raw_free, 4 + 4 * g + kq + 1)
                    for k in range(4):
                        kt = 4 * kq + k
                        for n in range(4):
                            c = slice(k * COL + n * P, k * COL + (n + 1) * P)
                            o = ps[:, 2 * par + n // 2, (n % 2) * T:(n % 2 + 1) * T]
                            ins = three(o, w_hi[:, kq % 2, c], w_lo[:, kq % 2, c], xT_hi[:, kt, :], xT_lo[:, kt, :],
                                        kt == 0 and n % 2 == 0, kt == KT - 1, lint=True)
                    ins.then_inc(parts_free, 1)

            def steps_t(g, par):
                pe.wait_ge(acc_free, g + 1)
                for kq in range(4):
                    pe.wait_ge(raw_free, 4 + 4 * g + kq + 1)
                    for k in range(4):
                        kt = 4 * kq + k
                        c = slice(k * COL, (k + 1) * COL)
                        for a in range(TT):
                            t = slice(a * P, (a + 1) * P)
                            ins = three(ps[:, 2 * par + a, :], xT_hi[:, kt, t], xT_lo[:, kt, t], w_hi[:, kq % 2, c], w_lo[:, kq % 2, c],
                                        kt == 0, kt == KT - 1)
                    ins.then_inc(parts_free, 1)

            pe.sem_inc(parts_free, 2)
            pe.sem_inc(acc_free, 2)
            pe.wait_ge(const_in, 32)
            pe.wait_ge(x_in, 16)
            transposed(x_sb, 0, by_tile)
            pe.wait_ge(tr_lo, 8)
            pe.wait_ge(glrw_lo, 1)
            for kt in range(KT):
                ins = three(bank(4)[:, 0:T], glr_hi[:, kt, :], glr_lo[:, kt, :], xT_hi[:, kt, :], xT_lo[:, kt, :], kt == 0, kt == KT - 1)
            ins.then_inc(glr_done, 1)
            pe.wait_ge(wup_in, 32)
            pe.wait_ge(glrT_done, 1)
            for h in range(GH):
                ins = pe.matmul(bank(5, 2)[:, h * T:(h + 1) * T], wup_sb[:, h * P:(h + 1) * P], glrT[0:RANK, :], start=True, stop=True)
            ins.then_inc(logit_done, 1)
            with pe.Fori(0, A_END // 2) as j:
                for par in range(2):
                    steps_n(j * 2 + par, par)
            with pe.Fori(A_END // 2, B_END // 2) as j:
                for par in range(2):
                    steps_t(j * 2 + par, par)

            head_t = lambda t, h, a: t[:, h, a * P:(a + 1) * P]
            pe.wait_ge(decay_done, 1)
            for h in range(GH):
                for a in range(TT):
                    o = (h * TT + a) * P
                    ins = pe.transpose(bank(0, 2)[:, o:o + P], head_t(k_out, h, a), ident)
            ins.then_inc(kt_mm, 1)
            for l in range(LEVELS + 1):
                if l < LEVELS:
                    pe.wait_ge(lvl_ready, l + 1)
                if l >= 2:
                    pe.wait_ge(lvl_acc, l - 1)
                kk, qq = (lvl_k, lvl_q) if l < LEVELS else (proj_n[:, 4:8, :], proj_n[:, 0:4, :])
                for h in range(GH):
                    for a in range(TT):
                        o = (h * TT + a) * P
                        ins = pe.matmul(bank(4 + 2 * (l % 2), 2)[:, o:o + P], head_t(kk, h, a), head_t(qq, h, a), start=True, stop=True)
                ins.then_inc(lvl_mm, 1)
            pe.wait_ge(rot_done, 2)
            pe.wait_ge(lvl_acc, LEVELS + 1)
            for h in range(RH):
                for a in range(TT):
                    for s in range(2):
                        o = (a * 2 + s) * P
                        ins = pe.transpose(bank(4 + h)[:, o:o + P], rot[:, RH + h, s, a * P:(a + 1) * P], ident)
                ins.then_inc(rkt_mm, 1)

            def values(h, a, ret):
                return proj_t[:, a, 2 * K * ret + h * GDV:2 * K * ret + (h + 1) * GDV]

            def half(c):
                return slice(CH * (c % 2), CH * (c % 2) + CH)

            pe.wait_ge(kt_sb, 1)
            for h in range(GH):
                if h:
                    pe.wait_ge(s_done, h)
                for c in range(NCH - 1):
                    o = (h * TT + c // 2) * P
                    ins = pe.matmul(bank(0, 2)[:, SLOT[c] * GDV:(SLOT[c] + 1) * GDV],
                                    k_outT[:].rearrange("p a b -> p (a b)")[half(c), o:o + P],
                                    values(h, c // 2, 0)[half(c), :], start=True, stop=True)
                ins.then_inc(u_mm, 1)
                pe.wait_ge(s_done, h + 1)
                if h >= 2:
                    pe.wait_ge(o_evac, h - 1)
                for a in range(TT):
                    o = bank(2 + h % 2)[:, a * GDV:(a + 1) * GDV]
                    for c in (2 * a, 2 * a + 1):
                        pe.matmul(o[half(c), :], q_in[:, h, c * CH:(c + 1) * CH], states[:, h % 2, c, :], start=True, stop=False)
                    ins = pe.matmul(o, a_gla[:, h, a * P:(a + 1) * P], values(h, a, 0), start=False, stop=True)
                ins.then_inc(o_mm, 1)

            for h in range(RH):
                for a in range(TT):
                    o = (h * TT + a) * P
                    for s in range(2):
                        t = slice(a * P, (a + 1) * P)
                        ins = pe.matmul(bank(0, 2)[:, o:o + P], rot[:, RH + h, s, t], rot[:, h, s, t], start=s == 0, stop=s == 1)
            ins.then_inc(rs_mm, 1)
            pe.wait_ge(rkt_sb, RH)
            pe.wait_ge(ra_done, 1)
            for h in range(RH):
                if h:
                    pe.wait_ge(rs_done, h)
                for c in range(NCH - 1):
                    for s in range(2):
                        o = (SLOT[c] * 2 + s) * GDV
                        ins = pe.matmul(bank(4, 3)[:, o:o + GDV], rkT[half(c), h, c // 2, s * P:(s + 1) * P],
                                        values(h, c // 2, 1)[half(c), :], start=True, stop=True)
                ins.then_inc(ru_mm, 1)
                pe.wait_ge(rs_done, h + 1)
                pe.wait_ge(o_evac if h < 2 else ro_evac, GH if h < 2 else h - 1)
                for a in range(TT):
                    o = bank(2 + h % 2)[:, a * RDV:(a + 1) * RDV]
                    for c in (2 * a, 2 * a + 1):
                        for s in range(2):
                            pe.matmul(o[half(c), :], rq_dec[:, h, s, c * CH:(c + 1) * CH], states[:, s, c, :], start=s == 0, stop=False)
                    ins = pe.matmul(o, a_ret[:, h * TT + a, :], values(h, a, 1), start=False, stop=True)
                ins.then_inc(ro_mm, 1)

            pe.wait_ge(mix_done, 2)
            transposed(o_sb, 1, by_tile)
            pe.wait_ge(tr_lo, 16)
            pe.wait_ge(ro_evac, RH)
            for g in range(B_END, O_END):
                steps_t(g, g % 2)
            pe.wait_ge(h1p_done, 2)
            transposed(h1_perm, 2, by_tile)
            pe.wait_ge(tr_lo, 24)
            with pe.Fori(O_END // 2, Q_END // 2) as j:
                for par in range(2):
                    steps_n(j * 2 + par, par)
            pe.wait_ge(sk_in, 16)
            for c in range(4):
                for k in range(4):
                    ins = pe.transpose(bank(4 + c)[:, k * P:(k + 1) * P], sk_raw[:, 4 * c + k, :], ident)
                ins.then_inc(sk_mm, 1)
            pe.wait_ge(sk_sb, 4)
            pe.wait_ge(acc_free, 2 + Q_END)
            for a in range(TT):
                for r in range(2 * PH):
                    ins = pe.matmul(bank(4 * a, 4)[:, r * NK:(r + 1) * NK], qT[:, r, a * P:(a + 1) * P], skT[:, r, :], start=True, stop=True)
                ins.then_inc(score_mm, 1)
            pe.wait_ge(score_sb, 2)

            pe.sem_inc(uparts_free, 4)

            def u_tile(ii, s, first=False, spreads=False):
                i = ii * 2 + s
                if not first:
                    pe.wait_ge(gelu_done, i - 1)
                for f in range(4):
                    pe.wait_ge(ulo_done, ii * 8 + 4 * s + f + 1)
                    for k in range(4):
                        c = slice(k * P, (k + 1) * P)
                        kt = 4 * f + k
                        ins = three(bank(s)[:, 0:T], u_hi[:, f, c], u_lo[:, f, c], xT_hi[:, kt, :], xT_lo[:, kt, :], kt == 0, kt == KT - 1)
                    ins.then_inc(uparts_free, 1)
                if spreads:
                    q = i - U_ONES
                    pe.wait_ge(hot_done, q + 1)
                    pe.wait_ge(spread_free, q + 1)
                    for k in range(4):
                        ins = pe.matmul(bank(2 + s)[:, k * P:(k + 1) * P], hot_j[:, s, k, :], hot_i[:, s, k, :], start=True, stop=True)
                    ins.then_inc(spread_mm, 1)

            for s in range(2):
                u_tile(0, s, first=True)
            with pe.Fori(1, U_ROUTE // 2) as ii:
                for s in range(2):
                    u_tile(ii, s)
            pe.wait_ge(ijg_done, 1)
            for s in range(3):
                for a in range(TT):
                    o = (s * TT + a) * P
                    ins = pe.transpose(bank(4, 2)[:, o:o + P], ijg[:, s, a, :], ident)
            ins.then_inc(ijg_mm, 1)
            with pe.Fori(U_ROUTE // 2, U_ONES // 2) as ii:
                for s in range(2):
                    u_tile(ii, s)
            pe.sem_inc(spread_free, 2)
            with pe.Fori(U_ONES // 2, P // 2) as ii:
                for s in range(2):
                    u_tile(ii, s, spreads=True)

            pe.sem_inc(vparts_free, 2)
            pe.wait_ge(gelu_free, 2 + P - U_ONES)

            def v_tile(i, s, start=False, stop=False):
                pe.wait_ge(vraw_free, 4 + i + 1)
                for a in range(TT):
                    t = slice(a * P, (a + 1) * P)
                    mh, ml = m_hi[:, s % 2, t], m_lo[:, s % 2, t]
                    for p, (m, v) in enumerate(((mh, v_hi), (mh, v_lo), (ml, v_hi))):
                        for c in range(4):
                            ins = pe.matmul(bank(4 * a + c), m, v[:, s % 2, c * 512:(c + 1) * 512], start=start and p == 0, stop=stop and p == 2)
                ins.then_inc(vparts_free, 1)

            for i in range(4):
                v_tile(i, i, start=i == 0)
            with pe.Fori(1, P // 4 - 1) as ii:
                for s in range(4):
                    v_tile(ii * 4 + s, s)
            for i in range(P - 4, P):
                v_tile(i, i % 4, stop=i == P - 1)


_INS = ["x", "w_in", "w_gla_gate_up", "b_gla_gate", "gla_norm_g", "ret_norm_g", "w_out", "ln1_g", "ln1_b",
        "w_peer_q", "peer_subkeys", "peer_u", "peer_v", "ln2_g", "ln2_b"]


def kernel(**inputs):
    import concourse.bacc as bacc
    from concourse.bass_utils import run_bass_kernel_spmd

    nc = bacc.Bacc("TRN2", target_bir_lowering=False, num_devices=1)
    keep_c, mix_c = constants()
    arrays, args = {}, []
    for name, a in [(n, inputs[n]) for n in _INS] + [("keep_c", keep_c), ("mix_c", mix_c)]:
        a = np.ascontiguousarray(a)
        arrays[f"in_{name}"] = a
        args.append(nc.dram_tensor(f"in_{name}", a.shape, mybir.dt.from_np(a.dtype), kind="ExternalInput").ap())
    args.append(nc.dram_tensor("out_0", (1, T, D), F32, kind="ExternalOutput").ap())
    build(nc, *args)
    r = run_bass_kernel_spmd(nc, [arrays], core_ids=[0])
    return r.results[0]["out_0"]
```

```python
import numpy as np
from contextlib import ExitStack
import concourse.bass as bass
from concourse import mybir

F32 = mybir.dt.float32
F32R = mybir.dt.float32r
U32 = mybir.dt.uint32
ALU = mybir.AluOpType
ACT = mybir.ActivationFunctionType
AX = mybir.AxisListType

P = 128
T, D = 256, 2048
TT, KT = T // P, D // P
CH = 64
NCH = T // CH
GH, GDK, GDV = 4, 128, 256
RH, RDK, RDV = 4, 256, 256
RANK = 16
PH, NK, TOPK = 8, 128, 16
COL = 512
EPS = 1e-5
ALPHA = 2 ** 0.25
LOW = -3.0e38

GQ, GV, GLR = 0, 1024, 3072
RQ, RV = GLR + RANK, GLR + RANK + 2048
U_ROUTE, U_ONES = 48, 64
A_END, V_END, B_END, O_END, Q_END = 6, 10, 14, 18, 22
STEPS = 8
VRING = 8
RING, HI_RING = 8, 4
LEVELS = 6
SLOT = (0, 2, 1)

LOG_GAMMA = np.log(1.0 - 2.0 ** (-5.0 - np.arange(RH, dtype=np.float32))).astype(np.float32)
CHUNK_DECAY = np.exp(LOG_GAMMA * CH).astype(np.float32)

KEEP = {"ident": P, "iota": P, "iota16": TOPK, "one": 1}
MIX = {"cos": T, "sin": T, "scan": T, "masks": (LEVELS + 1) * P, "dintra": RH * P, "qdec": RH * T, "kdec": RH}


def constants():
    c = {}
    c["ident"] = np.eye(P, dtype=np.float32)
    c["iota"] = np.broadcast_to(np.arange(P, dtype=np.float32), (P, P))
    c["iota16"] = np.broadcast_to(np.arange(TOPK, dtype=np.float32), (P, TOPK))
    c["one"] = np.ones((P, 1))
    half = RDK // 2
    inv = np.float32(10000.0) ** (-np.arange(half, dtype=np.float32) / np.float32(half))
    ang = np.arange(T, dtype=np.float32)[None, :] * inv.astype(np.float32)[:, None]
    c["cos"], c["sin"] = np.cos(ang), np.sin(ang)
    t = np.arange(T)
    c["scan"] = np.broadcast_to((t % CH != 0).astype(np.float32), (P, T))
    m, n = np.meshgrid(np.arange(P), np.arange(P), indexing="ij")
    masks = [(m // (CH >> l) == n // (CH >> l)) & (m // (CH >> (l + 1)) != n // (CH >> (l + 1))) for l in range(LEVELS)]
    c["masks"] = np.concatenate([*masks, m == n], axis=1)
    same = m // CH == n // CH
    scale = np.float32(RDK ** -0.5)
    c["dintra"] = np.concatenate([np.where(same, np.exp(g * np.abs(m - n).astype(np.float32)), 0) * scale for g in LOG_GAMMA], axis=1)
    i = (t % CH).astype(np.float32)
    c["qdec"] = np.concatenate([np.broadcast_to(np.exp(g * (i + 1)), (P, T)) for g in LOG_GAMMA], axis=1)
    c["kdec"] = np.stack([np.exp(g * (CH - 1 - i[:P])) * scale for g in LOG_GAMMA], axis=1)
    pack = lambda names: np.ascontiguousarray(np.concatenate([c[k].astype(np.float32) for k in names], axis=1))
    return pack(KEEP), pack(MIX)


def build(nc, x, w_in, w_up, b_gate, gla_g, ret_g, w_out, ln1_g, ln1_b, w_q, subkeys, peer_u, peer_v,
          ln2_g, ln2_b, keep_c, mix_c, out):
    ctx = ExitStack()
    with ctx:
        sem = lambda name: ctx.enter_context(nc.semaphore(name))

        base = -(-nc.sbuf_base // 64) * 64
        K = 1024

        def at(name, off, shape, dt=F32):
            return nc.alloc_sbuf_tensor_at(name, shape, dt, offset=base + off)

        BIG, HT, WRK, CST = 0, 128 * K, 160 * K, 200 * K
        act_w = at("act_w", BIG, [P, P, T])
        xT_hi, xT_lo = at("xT_hi", HT, [P, KT, T], F32R), at("xT_lo", HT + 16 * K, [P, KT, T], F32R)
        raw = at("raw", BIG, [P, RING, 2 * COL])
        w_lo = at("w_lo", BIG, [P, RING, 2 * COL], F32R)
        w_hi = at("w_hi", BIG + 32 * K, [P, HI_RING, 2 * COL], F32R)
        proj_v = at("proj_v", BIG + 64 * K, [P, TT, 4 * COL])
        swish = at("swish", BIG + 80 * K, [P, TT, D])
        proj_n = at("proj_n", BIG + 96 * K, [P, 24, T])
        mixc = at("mixc", WRK, [P, sum(MIX.values())])
        x_sb = at("x_sb", WRK + 13 * K, [P, TT, D])
        o_sb = at("o_sb", WRK + 13 * K, [P, TT, D])
        gains = at("gains", BIG + 96 * K, [P, D])
        glr_raw = at("glr_raw", BIG + 80 * K, [P, KT, P])
        glr_hi = at("glr_hi", BIG + 64 * K, [P, KT, P], F32R)
        glr_lo = at("glr_lo", BIG + 72 * K, [P, KT, P], F32R)
        wup = at("wup", WRK + 37 * K, [P, GH * GDK])
        small = at("small", CST + 17 * K // 4, [P, 256])
        keepc = at("keepc", CST, [P, sum(KEEP.values())])
        b_cum, lvl_e, k_out, a_gla = (at(n, BIG + (48 + 4 * i) * K, [P, 4, T]) for i, n in enumerate(("b_cum", "lvl_e", "k_out", "a_gla")))
        lvl_tmp = at("lvl_tmp", BIG + 56 * K, [P, 8, P])
        lvl_q, lvl_k = at("lvl_q", BIG + 120 * K, [P, 4, T]), at("lvl_k", BIG + 124 * K, [P, 4, T])
        states = at("states", BIG + 120 * K, [P, 2, NCH, GDV])
        q_in, k_outT = at("q_in", WRK + 29 * K, [P, 4, T]), at("k_outT", WRK + 33 * K, [P, 4, T])
        rkT = at("rkT", BIG + 112 * K, [P, RH, TT, RDK])
        a_ret = at("a_ret", BIG + 48 * K, [P, RH * TT, P])
        rot_tmp = at("rot_tmp", BIG + 52 * K, [P, 2, 2, T])
        sig = at("sig", BIG + 56 * K, [P, TT, COL])
        y_sb = o_sb
        ln_g = at("ln_g", BIG + 64 * K, [P, D])
        ln_b = at("ln_b", BIG + 72 * K, [P, D])
        x_again = at("x_again", BIG + 104 * K, [P, TT, D])
        h1_perm = at("h1_perm", BIG + 80 * K, [P, TT, D])
        qT = at("qT", BIG + 64 * K, [P, 2 * PH, T])
        sk_raw = at("sk_raw", BIG + 96 * K, [P, 2 * PH, P])
        skT = at("skT", BIG + 104 * K, [P, 2 * PH, P])
        scores = at("scores", BIG + 80 * K, [P, TT, 2 * PH, NK])
        scores2 = at("scores2", BIG + 64 * K, [P, TT, 2 * PH, NK])
        cand = at("cand", BIG + 96 * K, [P, TT * PH, TOPK * TOPK])
        cand2 = at("cand2", BIG + 80 * K, [P, TT * PH, TOPK * TOPK])
        pick = at("pick", BIG + 64 * K, [P, TT * PH * TOPK, TOPK])
        vals = at("vals", BIG + 112 * K, [P, TT, 2 * PH, TOPK])
        idx_u = at("idx_u", BIG + 114 * K, [P, TT, 2 * PH, TOPK], U32)
        idx_f = at("idx_f", BIG + 116 * K, [P, TT, PH, 2, TOPK])
        tops = at("tops", BIG + 118 * K, [P, TT * PH, TOPK])
        sel_u = at("sel_u", BIG + 119 * K, [P, TT * PH, TOPK], U32)
        sel_ab = at("sel_ab", BIG + 120 * K, [P, 2, TT * PH, TOPK], U32)
        sel_f = at("sel_f", BIG + 122 * K, [P, 2, TT * PH, TOPK])
        ijg = at("ijg", BIG + 124 * K, [P, 3, TT, P])
        ijgT = at("ijgT", CST + 5 * K // 4, [P, 3, T])
        u_raw = at("u_raw", WRK, [P, 2, 4 * COL])
        u_t = at("u_t", WRK + 16 * K, [P, 4, 4 * P])
        u_lo = at("u_lo", WRK + 16 * K, [P, 4, 4 * P], F32R)
        u_hi = at("u_hi", WRK + 24 * K, [P, 4, 4 * P], F32R)
        gelu_sb = at("gelu_sb", CST + 21 * K // 4, [P, 2, T])
        hot_j = at("hot_j", WRK + 32 * K, [P, 2, 4, P])
        hot_i = at("hot_i", WRK + 36 * K, [P, 2, 4, P])
        HALF = D // 2
        v_raw = at("v_raw", WRK, [P, 8, HALF])
        v_lo = at("v_lo", WRK, [P, 8, HALF], F32R)
        v_hi = at("v_hi", HT, [P, 4, HALF], F32R)
        m_hi = at("m_hi", CST + 21 * K // 4, [P, 2, T], F32R)
        m_lo = at("m_lo", CST + 5 * K // 4, [P, 2, T], F32R)
        h1_again = at("h1_again", HT + 16 * K, [P, TT, D])
        ln2g_sb = at("ln2g_sb", WRK + 32 * K, [P, D])
        ln2b_sb = at("ln2b_sb", BIG, [P, D])
        h1_dram = nc.dram_tensor("h1_dram", [T, D], F32, kind="Internal").ap()

        def cols(tensor, table, name):
            off = 0
            for k, n in table.items():
                if k == name:
                    return tensor[:, off:off + n]
                off += n

        ident = cols(keepc, KEEP, "ident")
        iota = cols(keepc, KEEP, "iota")
        one = cols(keepc, KEEP, "one")
        iota16 = cols(keepc, KEEP, "iota16")
        mc = lambda name: cols(mixc, MIX, name)

        bias4 = small[:, 0:4]
        stat6 = small[:, 8:8 + 96].rearrange("p (n s) -> p n s", s=6)
        mv = small[:, 104:136].rearrange("p (n s) -> p n s", s=2)
        rstd = small[:, 136:152]
        power = small[:, 152:168]
        var16 = small[:, 168:184]
        last_e = small[:, 184:200]
        gmax = small[:, 200:216]
        wup_sb = wup[0:RANK, :]
        glrT = at("glrT", CST + 5 * K // 4, [P, T])

        ps = ctx.enter_context(nc.psum_tensor("ps", [P, 8, 512], F32))

        def bank(i, n=1):
            return ps[:, i:i + n, :].rearrange("p a b -> p (a b)")

        keep_in, mix_in, glrw_in, wup_in = sem("keep_in"), sem("mix_in"), sem("glrw_in"), sem("wup_in")
        x_in = [sem(f"x_in{i}") for i in range(4)]
        raw_in = [sem(f"raw_in{i}") for i in range(RING)]
        step_free, hi_done, lo_done, acc_free = sem("step_free"), sem("hi_done"), sem("lo_done"), sem("acc_free")
        tr_done, tr_hi, tr_lo = sem("tr_done"), sem("tr_hi"), sem("tr_lo")
        glrw_hi, glrw_lo, glr_done, glrT_done, logit_done = (sem(n) for n in ("glrw_hi", "glrw_lo", "glr_done", "glrT_done", "logit_done"))
        neg_min, logsig_act, b_done, decay_act, decay_d, decay_done = (sem(n) for n in ("neg_min", "logsig_act", "b_done", "decay_act", "decay_d", "decay_done"))
        lvl_diff, lvl_exp, lvl_ready, lvl_mm, lvl_acc = (sem(n) for n in ("lvl_diff", "lvl_exp", "lvl_ready", "lvl_mm", "lvl_acc"))
        kt_mm, kt_sb, u_mm, s_done, o_mm, o_evac = (sem(n) for n in ("kt_mm", "kt_sb", "u_mm", "s_done", "o_mm", "o_evac"))
        rot_done, rkt_mm, rkt_sb, rs_mm, ra_done, rq_done, ru_mm, rs_done, ro_mm, ro_evac = (
            sem(n) for n in ("rot_done", "rkt_mm", "rkt_sb", "rs_mm", "ra_done", "rq_done", "ru_mm", "rs_done", "ro_mm", "ro_evac"))
        sig_done, stat_done, rstd_done, mix_done, gains_in = (sem(n) for n in ("sig_done", "stat_done", "rstd_done", "mix_done", "gains_in"))
        x2_in, ln1_in, h1_done, h1_out = sem("x2_in"), sem("ln1_in"), sem("h1_done"), sem("h1_out")
        h1p_done = sem("h1p_done")
        sk_in, sk_mm, sk_sb, score_mm, score_sb = (sem(n) for n in ("sk_in", "sk_mm", "sk_sb", "score_mm", "score_sb"))
        soft_d, soft_e, ijg_done, ijg_mm, ijg_sb = (sem(n) for n in ("soft_d", "soft_e", "ijg_done", "ijg_mm", "ijg_sb"))
        u_in = [sem("u_in0"), sem("u_in1")]
        ut_done, uhi_done, ulo_done, uparts_free, gelu_done, gelu_free = (
            sem(n) for n in ("ut_done", "uhi_done", "ulo_done", "uparts_free", "gelu_done", "gelu_free"))
        hot_done, spread_mm, spread_free = sem("hot_done"), sem("spread_mm"), sem("spread_free")
        v_in = [sem(f"v_in{i}") for i in range(4)]
        v_hi_done, v_lo_done, v_free, sum_done = sem("v_hi_done"), sem("v_lo_done"), sem("v_free"), sem("sum_done")
        last_in, y_done, out_done = sem("last_in"), sem("y_done"), sem("out_done")
        ln_stat, ln_rstd = sem("ln_stat"), sem("ln_rstd")

        win = w_in[0]
        w_rows = lambda w, k: w[2 * k * P:2 * (k + 1) * P, :].rearrange("(k p) n -> p k n", p=P)
        wq_rows = w_q[0].rearrange("(q f l) n -> q l f n", q=4, f=KT)
        u_rows = peer_u[0].rearrange("(i b l) (q d) -> i q l b d", b=4, l=32, q=4)
        v_rows = peer_v[0].rearrange("(i j) d -> i j d", j=P)

        def raw_count(g):
            return 16 * (g + 1) if not isinstance(g, int) or g < O_END else 16 * O_END + 64 * (g + 1 - O_END)

        def used(g, k=STEPS - 1):
            return RING + STEPS * g + k + 1

        block = ctx.enter_context(nc.Block())

        @block.sync
        def _(sp):
            def load_step(g, k, w, col):
                sp.wait_ge(step_free, STEPS * g + k + 1)
                sp.dma_start(raw[:, k, :].rearrange("p (k n) -> p k n", k=2), w_rows(w, k)[:, :, bass.ds(col, COL)]).then_inc(raw_in[k], 16)

            def load(g, w, col):
                for k in range(STEPS):
                    load_step(g, k, w, col)

            sp.sem_inc(step_free, RING)
            sp.dma_start(keepc[:], keep_c).then_inc(keep_in, 16)
            for b in range(4):
                c = slice(b * COL, (b + 1) * COL)
                sp.dma_start(x_sb[:, :, c], x[0].rearrange("(a p) d -> p a d", p=P)[:, :, c]).then_inc(x_in[b], 16)
                for k in (2 * b, 2 * b + 1):
                    load_step(0, k, win, GQ)
            sp.dma_start(glr_raw[:], win[:, GLR:GLR + P].rearrange("(k p) n -> p k n", p=P)).then_inc(glrw_in, 16)
            sp.dma_start(wup_sb, w_up[0]).then_inc(wup_in, 16)
            with nc.allow_non_contiguous_dma(reason="512 bias values, one channel a partition"):
                sp.dma_start(bias4, b_gate[0].rearrange("(h p) -> p h", p=P)).then_inc(wup_in, 16)
            load(1, win, GQ + COL)
            sp.dma_start(mixc[:], mix_c).then_inc(mix_in, 16)
            with sp.Fori(2, A_END) as g:
                load(g, win, RQ + (g - 2) * COL)
            for g in range(A_END, B_END):
                half, first = divmod(g - A_END, 4)
                load(g, win, (GV if first < 2 else RV) + 2 * COL * half + COL * (first % 2))
                if g == A_END + 2:
                    sp.wait_ge(lvl_acc, LEVELS + 1)
                    sp.dma_start(gains[:, 0:D // 2], gla_g[0:1, :].to_broadcast([P, D // 2])).then_inc(gains_in, 16)
                    sp.dma_start(gains[:, D // 2:], ret_g[0:1, :].to_broadcast([P, D // 2])).then_inc(gains_in, 16)
            sp.wait_ge(ro_mm, RH)
            sp.dma_start(x_again[:], x[0].rearrange("(a p) d -> p a d", p=P)).then_inc(x2_in, 16)
            sp.dma_start(ln_g[:], ln1_g[0:1, :].to_broadcast([P, D])).then_inc(ln1_in, 16)
            sp.dma_start(ln_b[:], ln1_b[0:1, :].to_broadcast([P, D])).then_inc(ln1_in, 16)
            with sp.Fori(B_END, O_END) as g:
                load(g, w_out[0], (g - B_END) * COL)
            sp.wait_ge(mix_done, 4)
            sp.dma_start(sk_raw[:], subkeys[0].rearrange("h s k d -> k (h s) d")).then_inc(sk_in, 16)
            for g in range(O_END, Q_END):
                col = (g - O_END) * COL
                for k in range(STEPS):
                    sp.wait_ge(step_free, STEPS * g + k + 1)
                    for q in range(4):
                        sp.dma_start(raw[32 * q:32 * q + 32, k, :].rearrange("p (k n) -> p k n", k=2),
                                     wq_rows[q][:, 2 * k:2 * k + 2, col:col + COL]).then_inc(raw_in[k], 16)
                if g == O_END:
                    sp.wait_ge(h1_done, 8)
                    sp.dma_start(h1_dram.rearrange("(a p) d -> p a d", p=P), y_sb[:]).then_inc(h1_out, 16)
            sp.wait_ge(h1_out, 16)
            sp.wait_ge(tr_lo, 24)
            def load_u(ii, s):
                for q in range(4):
                    sp.dma_start(u_raw[32 * q:32 * q + 32, s, :].rearrange("p (b d) -> p b d", b=4),
                                 u_rows[bass.ds(ii * 2 + s, 1), q].rearrange("i l b d -> l (i b) d")).then_inc(u_in[s], 16)

            load_u(0, 0)
            load_u(0, 1)
            with sp.Fori(1, P // 2) as ii:
                for s in range(2):
                    sp.wait_ge(ut_done, ii * 8 + 4 * s - 4)
                    load_u(ii, s)
            sp.sem_inc(v_free, VRING)

            def load_v(i, s):
                sp.dma_start(v_raw[:, 2 * s:2 * s + 2, :].rearrange("p a b -> p (a b)"), v_rows[bass.ds(i, 1)].rearrange("i j d -> j (i d)")).then_inc(v_in[s], 16)

            for s in range(2):
                sp.wait_ge(ut_done, 4 * (P - 1) + 4 * s)
                load_v(s, s)
            sp.wait_ge(uparts_free, 4 + 4 * P)
            for s in range(2, 4):
                load_v(s, s)
            sp.dma_start(h1_again[:], h1_dram.rearrange("(a p) d -> p a d", p=P)).then_inc(last_in, 16)
            sp.wait_ge(spread_mm, 2 + P - U_ONES)
            sp.dma_start(ln2g_sb[:], ln2_g[0:1, :].to_broadcast([P, D])).then_inc(last_in, 16)
            with sp.Fori(1, P // 4) as ii:
                for s in range(4):
                    sp.wait_ge(v_free, ii * 8 + 2 * s + 2)
                    load_v(ii * 4 + s, s)
            sp.dma_start(ln2b_sb[:], ln2_b[0:1, :].to_broadcast([P, D])).then_inc(last_in, 16)
            for a in range(TT):
                for b in range(4):
                    c = slice(b * COL, (b + 1) * COL)
                    sp.wait_ge(y_done, 4 * a + b + 1)
                    sp.dma_start(out[0, a * P:(a + 1) * P, c], h1_again[:, a, c]).then_inc(out_done, 16)
            sp.wait_ge(out_done, 16 * TT * 4)

        def act_turn(act, use, c):
            act.wait_ge(tr_done, use * 8 + c + 1)
            act.activation(xT_hi[:, 2 * c:2 * c + 2, :].rearrange("p a b -> p (a b)"), bank(4 + c % 4), ACT.Copy).then_inc(tr_hi, 1)

        @block.scalar
        def _(act):
            def hi_steps(g, ks):
                for k in ks:
                    act.wait_ge(raw_in[k], raw_count(g))
                    act.wait_ge(step_free, used(g, k - HI_RING))
                    act.activation(w_hi[:, k % HI_RING, :], raw[:, k, :], ACT.Copy).then_inc(hi_done, 1)

            def evac_n(g, dst, tile):
                act.wait_ge(step_free, used(g))
                act.activation(dst[:, tile:tile + 4, :], bank(2 * (g % 2), 2).rearrange("p (a b) -> p a b", a=4), ACT.Copy).then_inc(acc_free, 1)

            def evac_t(g):
                act.wait_ge(step_free, used(g))
                act.activation(proj_v[:, :, (g - A_END) * COL:(g - A_END + 1) * COL], ps[:, 2 * (g % 2):2 * (g % 2) + 2, :], ACT.Copy).then_inc(acc_free, 1)

            def gate(g):
                act.wait_ge(step_free, used(g))
                if g > V_END:
                    act.wait_ge(acc_free, 2 + g)
                act.activation(sig[:], ps[:, 2 * (g % 2):2 * (g % 2) + 2, :], ACT.Sigmoid).then_inc(sig_done, 1)

            def level_exp(l):
                act.wait_ge(lvl_diff, l + 1)
                act.activation(lvl_e[:], lvl_e[:], ACT.Abs)
                act.drain()
                act.activation(lvl_e[:], lvl_e[:], ACT.Exp, scale=-1.0).then_inc(lvl_exp, 1)

            def evac_gla(h):
                act.wait_ge(o_mm, h + 1)
                act.activation(o_sb[:, :, h * GDV:(h + 1) * GDV], bank(6 + h % 2).rearrange("p (a e) -> p a e", a=TT), ACT.Copy).then_inc(o_evac, 1)

            def evac_ret(h):
                act.wait_ge(ro_mm, h + 1)
                act.activation(o_sb[:, :, K + h * RDV:K + (h + 1) * RDV], bank(7).rearrange("p (a e) -> p a e", a=TT), ACT.Copy).then_inc(ro_evac, 1)

            def later_turns(g, use):
                for k in range(4, STEPS):
                    hi_steps(g, (k,))
                    act_turn(act, use, k - 1)
                act_turn(act, use, 7)

            hi_steps(0, range(4))
            for c in range(3):
                act_turn(act, 0, c)
            later_turns(0, 0)
            act.wait_ge(glrw_in, 16)
            act.activation(glr_hi[:], glr_raw[:], ACT.Copy).then_inc(glrw_hi, 1)
            hi_steps(1, range(4))
            evac_n(0, proj_n, 0)
            hi_steps(1, (4,))
            act.wait_ge(glr_done, 1)
            act.activation(glrT[0:RANK, :], bank(4)[0:RANK, 0:T], ACT.Copy).then_inc(glrT_done, 1)
            hi_steps(1, (5, 6))
            act.wait_ge(logit_done, 1)
            act.wait_ge(wup_in, 32)
            for h in range(GH):
                act.activation(lvl_e[:, h, :], bank(5, 2)[:, h * T:(h + 1) * T], ACT.Abs, bias=bias4[:, h:h + 1])
            act.drain()
            hi_steps(1, (7,))
            act.activation(lvl_q[:], lvl_e[:], ACT.Exp, scale=-1.0)
            act.drain()
            act.activation(lvl_k[:], lvl_q[:], ACT.Ln, bias=1.0).then_inc(logsig_act, 1)
            hi_steps(2, range(4))
            evac_n(1, proj_n, 4)
            hi_steps(2, (4, 5))
            act.wait_ge(b_done, 1)
            act.activation(lvl_e[:], b_cum[:], ACT.Exp).then_inc(decay_act, 1)
            act.wait_ge(decay_d, 1)
            act.activation(lvl_k[:], lvl_q[:], ACT.Exp).then_inc(decay_act, 1)
            hi_steps(2, (6, 7))
            for g in range(3, A_END + 1):
                hi_steps(g, (0,))
                if g > 3:
                    level_exp(2 * g - 7)
                hi_steps(g, (1, 2, 3))
                evac_n(g - 1, proj_n, 4 * (g - 1))
                if g == 3:
                    act.wait_ge(kt_mm, 1)
                    act.activation(k_outT[:].rearrange("p a b -> p (a b)"), bank(4, 2), ACT.Copy).then_inc(kt_sb, 1)
                hi_steps(g, (4,))
                if g < A_END:
                    level_exp(2 * g - 6)
                hi_steps(g, (5, 6, 7))
            for g in range(A_END + 1, B_END):
                hi_steps(g, (0,))
                if g >= V_END:
                    h = 2 * (g - V_END) + 1
                    evac_gla(h) if h < GH else evac_ret(h - GH)
                hi_steps(g, (1, 2, 3))
                evac_t(g - 1) if g <= V_END else gate(g - 1)
                hi_steps(g, (4,))
                if V_END - 1 <= g < B_END - 1:
                    h = 2 * (g - V_END) + 2
                    evac_gla(h) if h < GH else evac_ret(h - GH)
                hi_steps(g, (5, 6, 7))
            hi_steps(B_END, range(4))
            act_turn(act, 1, 0)
            act_turn(act, 1, 1)
            gate(B_END - 1)
            act_turn(act, 1, 2)
            later_turns(B_END, 1)
            for g in range(B_END + 1, O_END):
                hi_steps(g, range(STEPS))
            hi_steps(O_END, range(4))
            for b in range(4):
                for a in range(TT):
                    act.wait_ge(h1_done, 2 * b + a + 1)
                    act.activation(h1_perm[:, a, :].rearrange("p (f q l) -> p q f l", f=KT, q=4)[:, :, 4 * b:4 * b + 4, :],
                                   y_sb[:, a, :].rearrange("p (q f l) -> p q f l", f=KT, q=4)[:, :, 4 * b:4 * b + 4, :], ACT.Copy).then_inc(h1p_done, 1)
                if b:
                    act_turn(act, 2, b - 1)
            later_turns(O_END, 2)
            for g in range(O_END + 1, Q_END):
                hi_steps(g, range(4))
                evac_n(g - 1, qT, 4 * (g - 1 - O_END))
                hi_steps(g, range(4, STEPS))
            evac_n(Q_END - 1, qT, 4 * (Q_END - 1 - O_END))
            for c in range(4):
                act.wait_ge(sk_mm, c + 1)
                act.activation(skT[:, 4 * c:4 * c + 4, :].rearrange("p a b -> p (a b)"), bank(4 + c), ACT.Copy).then_inc(sk_sb, 1)
            for a in range(TT):
                act.wait_ge(score_mm, a + 1)
                act.activation(scores[:, a].rearrange("p a b -> p (a b)"), bank(4 * a, 4), ACT.Copy).then_inc(score_sb, 1)

            def gelu(i, par, far):
                act.wait_ge(uparts_free, 4 * i + 8)
                if far:
                    act.wait_ge(gelu_free, i - U_ONES + 1)
                    act.activation(gelu_sb[:, par, :], bank(par)[:, 0:T], ACT.Gelu).then_inc(gelu_done, 1)
                else:
                    act.activation(act_w[:, bass.ds(i, 1), :].rearrange("p a t -> p (a t)"), bank(par)[:, 0:T], ACT.Gelu).then_inc(gelu_done, 1)

            def u_tile(i, par, evac=True, far=False):
                for f in range(4):
                    act.wait_ge(ut_done, 4 * i + f + 1)
                    act.activation(u_hi[:, f, :], u_t[:, f, :], ACT.Copy).then_inc(uhi_done, 1)
                if evac:
                    gelu(i - 1, 1 - par, far)

            u_tile(0, 0, evac=False)
            u_tile(1, 1)
            with act.Fori(1, (U_ROUTE - 12) // 2) as ii:
                for s in range(2):
                    u_tile(ii * 2 + s, s)
            act.wait_ge(soft_d, 1)
            act.activation(tops[:], tops[:], ACT.Exp).then_inc(soft_e, 1)
            with act.Fori((U_ROUTE - 12) // 2, U_ROUTE // 2) as ii:
                for s in range(2):
                    u_tile(ii * 2 + s, s)
            act.wait_ge(ijg_mm, 1)
            act.activation(ijgT[:].rearrange("p a b -> p (a b)"), bank(4, 2)[:, 0:3 * T], ACT.Copy).then_inc(ijg_sb, 1)
            with act.Fori(U_ROUTE // 2, U_ONES // 2) as ii:
                for s in range(2):
                    u_tile(ii * 2 + s, s)
            act.sem_inc(gelu_free, 2)
            u_tile(U_ONES, 0)
            u_tile(U_ONES + 1, 1, far=True)
            with act.Fori(U_ONES // 2 + 1, P // 2) as ii:
                for s in range(2):
                    u_tile(ii * 2 + s, s, far=True)
            gelu(P - 1, 1, True)

            act.wait_ge(gelu_free, 2 + P - U_ONES)
            with act.Fori(0, P // 4) as ii:
                for s in range(4):
                    act.wait_ge(v_in[s], ii * 16 + 16)
                    act.wait_ge(v_free, ii * 8 + 2 * s + 5)
                    act.activation(v_hi[:, 2 * (s % 2), :], v_raw[:, 2 * s, :], ACT.Copy)
                    act.wait_ge(v_free, ii * 8 + 2 * s + 6)
                    act.activation(m_hi[:, s % 2, :], act_w[:, bass.ds(ii * 4 + s, 1), :].rearrange("p a t -> p (a t)"), ACT.Copy).then_inc(v_hi_done, 1)
                    act.activation(v_hi[:, 2 * (s % 2) + 1, :], v_raw[:, 2 * s + 1, :], ACT.Copy).then_inc(v_hi_done, 1)

        def cols_of(y, b):
            return y.rearrange("p (q b m) -> p q b m", q=4, b=4)[:, :, b, :]

        def stat_block(dve, y, c):
            for a in range(TT):
                dve.bn_stats(stat6[:, 4 * a + c, :], y[:, a, c * COL:(c + 1) * COL])

        def norm_scale(dve):
            dve.drain()
            for a in range(TT):
                dve.bn_aggr(mv[:, a, :], stat6[:, 4 * a:4 * a + 4, :])
            dve.drain()
            dve.tensor_scalar(var16[:, 0:TT], mv[:, 0:TT, 1], EPS, None, ALU.add).then_inc(ln_stat, 1)
            dve.wait_ge(ln_rstd, 1)

        def norm_apply(dve, o, gain, shift, a, done):
            dve.scalar_tensor_tensor(o, o, mv[:, a, 0:1], gain, ALU.subtract, ALU.mult)
            dve.drain()
            dve.scalar_tensor_tensor(o, o, rstd[:, a:a + 1], shift, ALU.mult, ALU.add).then_inc(done, 1)

        def turn_lo(dve, use, c):
            dve.wait_ge(tr_hi, use * 8 + c + 1)
            sl = slice(2 * c, 2 * c + 2)
            dve.tensor_tensor(xT_lo[:, sl, :].rearrange("p a b -> p (a b)"), bank(4 + c % 4),
                              xT_hi[:, sl, :].rearrange("p a b -> p (a b)").bitcast(F32), ALU.subtract).then_inc(tr_lo, 1)

        @block.vector
        def _(dve):
            dve.memset(power[:], -0.5)
            for c in range(8):
                turn_lo(dve, 0, c)
            dve.wait_ge(glrw_hi, 1)
            dve.tensor_tensor(glr_lo[:], glr_raw[:], glr_hi[:].bitcast(F32), ALU.subtract).then_inc(glrw_lo, 1)

            dve.wait_ge(logit_done, 1)
            dve.wait_ge(wup_in, 32)
            dve.wait_ge(logsig_act, 1)
            for h in range(GH):
                dve.tensor_scalar(k_out[:, h, :], bank(5, 2)[:, h * T:(h + 1) * T], bias4[:, h:h + 1], 0.0, ALU.add, ALU.min)
            dve.wait_ge(mix_in, 16)
            dve.drain()
            dve.tensor_tensor(k_out[:], k_out[:], lvl_k[:], ALU.subtract)
            dve.drain()
            for h in range(GH):
                dve.tensor_tensor_scan(b_cum[:, h, :], mc("scan"), k_out[:, h, :], 0.0, ALU.mult, ALU.add)
            dve.drain()
            dve.tensor_scalar(b_cum[:], b_cum[:], 1.0 / 16.0, None, ALU.mult).then_inc(b_done, 1)
            dve.drain()
            chunks = lambda t: t[:].rearrange("p h (c n) -> p (h c) n", n=CH)
            dve.tensor_tensor(chunks(lvl_q), chunks(b_cum)[:, :, CH - 1:CH].to_broadcast([P, GH * NCH, CH]), chunks(b_cum), ALU.subtract).then_inc(decay_d, 1)
            gq, gk = proj_n[:, 0:4, :], proj_n[:, 4:8, :]
            dve.wait_ge(acc_free, 2 + 2)
            dve.tensor_scalar(gq, gq, float(np.float32(GDK ** -0.5)), None, ALU.mult)
            dve.wait_ge(decay_act, 2)
            dve.drain()
            dve.tensor_tensor(k_out[:], gk, lvl_k[:], ALU.mult).then_inc(decay_done, 1)
            dve.tensor_copy(last_e, chunks(lvl_e)[:, :, CH - 1])
            dve.tensor_tensor(q_in[:], gq, lvl_e[:], ALU.mult)
            dve.drain()
            masks = mc("masks").rearrange("p (l n) -> p l n", l=LEVELS + 1)

            def gather(n):
                dve.wait_ge(lvl_mm, n + 1)
                m = n - 1 if n else LEVELS
                m8 = masks[:, m:m + 1, :].to_broadcast([P, 8, P])
                s = bank(6 - 2 * (n % 2), 2).rearrange("p (a b) -> p a b", a=8)
                a8 = a_gla[:].rearrange("p h (a b) -> p (h a) b", b=P)
                if n == 0:
                    dve.tensor_tensor(a8, s, m8, ALU.mult).then_inc(lvl_acc, 1)
                else:
                    dve.wait_ge(lvl_acc, n)
                    dve.tensor_tensor(lvl_tmp[:], s, m8, ALU.mult)
                    dve.drain()
                    dve.tensor_tensor(a8, a8, lvl_tmp[:], ALU.add).then_inc(lvl_acc, 1)

            for l in range(LEVELS):
                m = CH >> (l + 1)
                blocks = lambda t: t[:].rearrange("p h (c n) -> p (h c) n", n=2 * m)
                bb = blocks(b_cum)
                if l:
                    dve.wait_ge(lvl_ready, l)
                dve.tensor_tensor(blocks(lvl_e), bb, bb[:, :, m - 1:m].to_broadcast([P, GH * T // (2 * m), 2 * m]), ALU.subtract).then_inc(lvl_diff, 1)
                gather(l)
                dve.wait_ge(lvl_exp, l + 1)
                dve.tensor_tensor(lvl_q[:], gq, lvl_e[:], ALU.mult)
                dve.tensor_tensor(lvl_k[:], gk, lvl_e[:], ALU.mult).then_inc(lvl_ready, 1)

            dve.wait_ge(acc_free, 2 + A_END)
            both = proj_n[:, 8:24, :].rearrange("p (h s) t -> p h s t", s=2)
            cos2, sin2 = (mc(n).unsqueeze(1).to_broadcast([P, 2, T]) for n in ("cos", "sin"))
            dve.wait_ge(lvl_ready, LEVELS)
            for h in range(0, 2 * RH, 2):
                t1, t2 = both[:, h:h + 2, 0, :], both[:, h:h + 2, 1, :]
                dve.tensor_tensor(rot_tmp[:, :, 0, :], t2, sin2, ALU.mult)
                dve.tensor_tensor(rot_tmp[:, :, 1, :], t1, sin2, ALU.mult)
                dve.drain()
                dve.tensor_tensor(t1, t1, cos2, ALU.mult)
                dve.tensor_tensor(t2, t2, cos2, ALU.mult)
                dve.drain()
                dve.tensor_tensor(t1, t1, rot_tmp[:, :, 0, :], ALU.subtract)
                dve.tensor_tensor(t2, t2, rot_tmp[:, :, 1, :], ALU.add).then_inc(rot_done, 1)
                dve.drain()
                if h == 2:
                    gather(LEVELS)

            kdec = mc("kdec")
            dintra = mc("dintra").rearrange("p (h n) -> p h n", h=RH)
            qdec = mc("qdec").rearrange("p (h t) -> p h t", h=RH).unsqueeze(2).to_broadcast([P, RH, 2, T])
            a4 = a_ret[:].rearrange("p (h a) n -> p h a n", h=RH)
            dve.wait_ge(rs_mm, 1)
            dve.tensor_tensor(a4, bank(4, 2).rearrange("p (h a n) -> p h a n", h=RH, a=TT), dintra.unsqueeze(2).to_broadcast([P, RH, TT, P]), ALU.mult).then_inc(ra_done, 1)
            for h in range(RH):
                dve.wait_ge(rkt_mm, h + 1)
                dve.tensor_scalar(rkT[:, h].rearrange("p a d -> p (a d)"), bank(4 + (h + 2) % 4), kdec[:, h:h + 1], None, ALU.mult).then_inc(rkt_sb, 1)
                if h == 1:
                    dve.tensor_tensor(both[:, 0:RH], both[:, 0:RH], qdec, ALU.mult).then_inc(rq_done, 1)

            def head_stats(h):
                for a in range(TT):
                    dve.bn_stats(stat6[:, a * 8 + h, :], o_sb[:, a, h * GDV:(h + 1) * GDV])

            def gla_states(h):
                dve.wait_ge(u_mm, h + 1)
                if h >= 2:
                    dve.wait_ge(o_mm, h - 1)
                s = states[:, h % 2]
                u = lambda c: bank(4, 2)[:, SLOT[c] * GDV:(SLOT[c] + 1) * GDV]
                dve.tensor_copy(s[:, 1, :], u(0))
                for c in (1, 2):
                    dve.drain()
                    ins = dve.scalar_tensor_tensor(s[:, c + 1, :], s[:, c, :], last_e[:, h * NCH + c:h * NCH + c + 1], u(c), ALU.mult, ALU.add)
                ins.then_inc(s_done, 1)

            def ret_states(h):
                dve.wait_ge(ru_mm, h + 1)
                dve.wait_ge(o_mm if h == 0 else ro_mm, GH if h == 0 else h)
                u6 = bank(4, 3).rearrange("p (c s e) -> p c s e", c=3, s=2)
                dve.tensor_copy(states[:, :, 1, :], u6[:, SLOT[0]])
                for c in (1, 2):
                    dve.drain()
                    ins = dve.scalar_tensor_tensor(states[:, :, c + 1, :], states[:, :, c, :], float(CHUNK_DECAY[h]), u6[:, SLOT[c]], ALU.mult, ALU.add)
                ins.then_inc(rs_done, 1)

            def swish_block(g):
                n = g - V_END
                dve.wait_ge(sig_done, n + 1)
                dve.tensor_tensor(swish[:, :, n * COL:(n + 1) * COL], ps[:, 2 * (g % 2):2 * (g % 2) + 2, :], sig[:], ALU.mult).then_inc(acc_free, 1)

            def mix_block(n):
                c = slice(n * COL, (n + 1) * COL)
                dve.tensor_tensor(o_sb[:, :, c], o_sb[:, :, c], swish[:, :, c], ALU.mult).then_inc(mix_done, 1)

            dve.memset(states[:, :, 0, :], 0.0)
            for h in range(GH):
                gla_states(h)
            ret_states(0)
            swish_block(V_END)
            for h in range(GH):
                dve.wait_ge(o_evac, h + 1)
                head_stats(h)
            for h in range(1, RH):
                ret_states(h)
                if h == 2:
                    swish_block(V_END + 1)
                dve.wait_ge(ro_evac, h)
                head_stats(GH + h - 1)
            swish_block(V_END + 2)
            dve.wait_ge(ro_evac, RH)
            head_stats(7)
            dve.drain()
            for n in range(16):
                dve.bn_aggr(mv[:, n, :], stat6[:, n:n + 1, :])
            dve.drain()
            v16 = var16[:].rearrange("p (a h) -> p a h", a=TT)
            mva = mv[:].rearrange("p (a h) s -> p a h s", a=TT)
            dve.tensor_tensor(v16[:, :, 0:4], mva[:, :, 0:4, 0], mva[:, :, 0:4, 0], ALU.mult)
            dve.tensor_copy(v16[:, :, 4:8], mva[:, :, 4:8, 1])
            dve.drain()
            dve.tensor_tensor(v16[:, :, 0:4], v16[:, :, 0:4], mva[:, :, 0:4, 1], ALU.add)
            dve.drain()
            dve.tensor_scalar(var16[:], var16[:], EPS, None, ALU.add).then_inc(stat_done, 1)
            dve.wait_ge(gains_in, 32)
            dve.wait_ge(rstd_done, 1)
            for a in range(TT):
                for h in range(8):
                    n = a * 8 + h
                    o = o_sb[:, a, h * GDV:(h + 1) * GDV]
                    if h < GH:
                        dve.tensor_scalar(o, o, rstd[:, n:n + 1], None, ALU.mult)
                    else:
                        dve.tensor_scalar(o, o, mv[:, n, 0:1], rstd[:, n:n + 1], ALU.subtract, ALU.mult)
            dve.drain()
            for a in range(TT):
                dve.tensor_tensor(o_sb[:, a, :], o_sb[:, a, :], gains[:], ALU.mult)
            dve.drain()
            for n in range(3):
                mix_block(n)
            turn_lo(dve, 1, 0)
            turn_lo(dve, 1, 1)
            swish_block(B_END - 1)
            dve.drain()
            mix_block(3)
            for c in range(2, 8):
                turn_lo(dve, 1, c)

            dve.wait_ge(x2_in, 16)
            dve.wait_ge(ln1_in, 32)
            for g in range(B_END, O_END):
                c = slice((g - B_END) * COL, (g - B_END + 1) * COL)
                dve.wait_ge(step_free, used(g))
                dve.scalar_tensor_tensor(y_sb[:, :, c], x_again[:, :, c], float(ALPHA),
                                         ps[:, 2 * (g % 2):2 * (g % 2) + 2, :], ALU.mult, ALU.add).then_inc(acc_free, 1)
                dve.drain()
                stat_block(dve, y_sb, g - B_END)
            norm_scale(dve)
            for b in range(4):
                for a in range(TT):
                    norm_apply(dve, cols_of(y_sb[:, a, :], b), cols_of(ln_g[:], b), cols_of(ln_b[:], b), a, h1_done)
                if b:
                    turn_lo(dve, 2, b - 1)
            for c in range(3, 8):
                turn_lo(dve, 2, c)

            def u_quarter(ii, s, f):
                if f == 0:
                    dve.wait_ge(u_in[s], ii * 64 + 64)
                dve.wait_ge(uparts_free, ii * 8 + 4 * s + f + 1)
                dve.transpose(u_t[:, f, :].rearrange("p (f b l) -> p b f l", f=4, b=4),
                              u_raw[:, s, :].rearrange("p (b f l) -> p b f l", b=4, l=32)[:, :, 4 * f:4 * f + 4, :]).then_inc(ut_done, 1)

            def route_best(stage, part):
                a, rows = part // 4, range(4 * (part % 4), 4 * (part % 4) + 4)
                sums = range(2 * part, 2 * part + 2)
                dve.drain()
                if stage == 0:
                    if part % 4 == 0:
                        dve.wait_ge(score_sb, a + 1)
                    for r in rows:
                        dve.max(vals[:, a, r, 0:8], scores[:, a, r, :])
                elif stage == 1:
                    for r in rows:
                        dve.max_index(idx_u[:, a, r, 0:8], vals[:, a, r, 0:8], scores[:, a, r, :])
                        dve.match_replace(scores2[:, a, r, :], vals[:, a, r, 0:8], scores[:, a, r, :], LOW)
                elif stage == 2:
                    for r in rows:
                        dve.max(vals[:, a, r, 8:16], scores2[:, a, r, :])
                elif stage == 3:
                    v = vals[:, a].rearrange("p (h s) k -> p h s k", s=2)
                    for r in rows:
                        dve.max_index(idx_u[:, a, r, 8:16], vals[:, a, r, 8:16], scores2[:, a, r, :])
                    for n in sums:
                        h = n % PH
                        dve.tensor_tensor(cand[:, n, :].rearrange("p (a b) -> p a b", a=TOPK),
                                          v[:, h, 0, :].unsqueeze(2).to_broadcast([P, TOPK, TOPK]),
                                          v[:, h, 1, :].unsqueeze(1).to_broadcast([P, TOPK, TOPK]), ALU.add)
                elif stage == 4:
                    for n in sums:
                        dve.max(tops[:, n, 0:8], cand[:, n, :])
                elif stage == 5:
                    for n in sums:
                        dve.max_index(sel_u[:, n, 0:8], tops[:, n, 0:8], cand[:, n, :])
                        dve.match_replace(cand2[:, n, :], tops[:, n, 0:8], cand[:, n, :], LOW)
                elif stage == 6:
                    for n in sums:
                        dve.max(tops[:, n, 8:16], cand2[:, n, :])
                else:
                    for n in sums:
                        dve.max_index(sel_u[:, n, 8:16], tops[:, n, 8:16], cand2[:, n, :])

            def route_split():
                dve.drain()
                dve.tensor_copy(gmax[:], tops[:, :, 0])
                dve.tensor_copy(idx_f[:].rearrange("p a h s k -> p (a h s k)"), idx_u[:].rearrange("p a r k -> p (a r k)"))
                dve.tensor_scalar(sel_ab[:, 0], sel_u[:], 4, None, ALU.logical_shift_right)
                dve.tensor_scalar(sel_ab[:, 1], sel_u[:], 15, None, ALU.bitwise_and)
                dve.drain()
                dve.tensor_tensor(tops[:], tops[:], gmax[:].unsqueeze(2).to_broadcast([P, TT * PH, TOPK]), ALU.subtract).then_inc(soft_d, 1)
                dve.tensor_copy(sel_f[:], sel_ab[:])

            def route_pick(s, a, stage):
                rows = slice(a * P, (a + 1) * P)
                dve.drain()
                if stage == 0:
                    dve.tensor_tensor(pick[:, rows], sel_f[:, s, a * PH:(a + 1) * PH].rearrange("p n k -> p (n k)").unsqueeze(2).to_broadcast([P, P, TOPK]),
                                      iota16.unsqueeze(1).to_broadcast([P, P, TOPK]), ALU.is_equal)
                elif stage == 1:
                    p4 = pick[:, rows].rearrange("p (h k) a -> p h k a", h=PH)
                    dve.tensor_tensor(p4, p4, idx_f[:, a, :, s, :].unsqueeze(2).to_broadcast([P, PH, TOPK, TOPK]), ALU.mult)
                else:
                    dve.tensor_reduce(ijg[:, s, a], pick[:, rows], AX.X, ALU.add)

            def route_gates():
                dve.wait_ge(soft_e, 1)
                dve.drain()
                dve.tensor_reduce(gmax[:], tops[:], AX.X, ALU.add)
                dve.drain()
                dve.reciprocal(rstd[:], gmax[:])
                dve.drain()
                dve.tensor_tensor(ijg[:, 2].rearrange("p a (h k) -> p (a h) k", k=TOPK), tops[:],
                                  rstd[:].unsqueeze(2).to_broadcast([P, TT * PH, TOPK]), ALU.mult).then_inc(ijg_done, 1)

            for i in range(U_ROUTE):
                for f in range(4):
                    u_quarter(i // 2, i % 2, f)
                    if i < 32 and f % 2:
                        route_best(i // 4, 2 * (i % 4) + f // 2)
                if i == 32:
                    route_split()
                elif 32 < i < 45:
                    route_pick((i - 33) // 6, (i - 33) // 3 % 2, (i - 33) % 3)
                elif i == 45:
                    route_gates()
            dve.wait_ge(ijg_sb, 1)
            with dve.Fori(U_ROUTE // 2, U_ONES // 2) as ii:
                for s in range(2):
                    for f in range(4):
                        u_quarter(ii, s, f)
                    dve.tensor_copy(act_w[:, bass.ds(U_ONES + (ii * 2 + s - U_ROUTE) * 4, 4), :], one.unsqueeze(2).to_broadcast([P, 4, T]))

            grid = act_w[:].rearrange("p i t -> p t i")

            def hot(q, r, ks):
                for k in ks:
                    if k == 0:
                        dve.wait_ge(spread_mm, q + 1)
                    t = bass.ds(q * 4 + k, 1)
                    dve.tensor_scalar(hot_j[:, r, k, :], iota, ijgT[:, 1, t], None, ALU.is_equal)
                    ins = dve.tensor_scalar(hot_i[:, r, k, :], iota, ijgT[:, 0, t], ijgT[:, 2, t], ALU.is_equal, ALU.mult)
                if ks[-1] == 3:
                    ins.then_inc(hot_done, 1)

            def spread(q, r):
                dve.drain()
                dve.wait_ge(spread_mm, 2 + q + 1)
                g4 = grid[:, bass.ds(q * 4, 4), :]
                dve.tensor_tensor(g4, g4, bank(2 + r).rearrange("p (t i) -> p t i", t=4), ALU.mult).then_inc(spread_free, 1)

            def weigh(i, s):
                dve.drain()
                dve.wait_ge(gelu_done, i + 1)
                row = act_w[:, bass.ds(i, 1), :].rearrange("p a t -> p (a t)")
                dve.tensor_tensor(row, row, gelu_sb[:, s, :], ALU.mult).then_inc(gelu_free, 1)

            def u_spread_tile(ii, s, first=False):
                q = ii * 2 + s - U_ONES
                u_quarter(ii, s, 0)
                hot(q, s, (0, 1))
                u_quarter(ii, s, 1)
                hot(q, s, (2, 3))
                u_quarter(ii, s, 2)
                if first and s == 1:
                    dve.wait_ge(gelu_done, U_ONES)
                if not (first and s == 0):
                    spread(q - 1, 1 - s)
                u_quarter(ii, s, 3)
                if not first:
                    weigh(ii * 2 + s - 2, s)

            dve.sem_inc(spread_mm, 2)
            for s in range(2):
                u_spread_tile(U_ONES // 2, s, first=True)
            with dve.Fori(U_ONES // 2 + 1, P // 2) as ii:
                for s in range(2):
                    u_spread_tile(ii, s)
            spread(P - U_ONES - 1, 1)
            weigh(P - 2, 0)
            weigh(P - 1, 1)

            with dve.Fori(0, P // 4) as ii:
                for s in range(4):
                    dve.wait_ge(v_hi_done, ii * 8 + 2 * s + 1)
                    dve.tensor_tensor(m_lo[:, s % 2, :], act_w[:, bass.ds(ii * 4 + s, 1), :].rearrange("p a t -> p (a t)"), m_hi[:, s % 2, :].bitcast(F32), ALU.subtract)
                    for h in range(2):
                        if h:
                            dve.wait_ge(v_hi_done, ii * 8 + 2 * s + 2)
                        dve.tensor_tensor(v_lo[:, 2 * s + h, :], v_raw[:, 2 * s + h, :], v_hi[:, 2 * (s % 2) + h, :].bitcast(F32), ALU.subtract).then_inc(v_lo_done, 1)
            dve.wait_ge(last_in, 48)

            def last_sum(a):
                dve.wait_ge(sum_done, a + 1)
                dve.scalar_tensor_tensor(h1_again[:, a, :], h1_again[:, a, :], float(ALPHA), bank(4 * a, 4), ALU.mult, ALU.add)
                dve.drain()
                for c in range(4):
                    dve.bn_stats(stat6[:, 4 * a + c, :], h1_again[:, a, c * COL:(c + 1) * COL])
                dve.drain()
                dve.bn_aggr(mv[:, a, :], stat6[:, 4 * a:4 * a + 4, :])
                dve.drain()
                dve.tensor_scalar(var16[:, a:a + 1], mv[:, a:a + 1, 1], EPS, None, ALU.add).then_inc(ln_stat, 1)

            last_sum(0)
            last_sum(1)
            for a in range(TT):
                dve.wait_ge(ln_rstd, 2 + a)
                for b in range(4):
                    c = slice(b * COL, (b + 1) * COL)
                    norm_apply(dve, h1_again[:, a, c], ln2g_sb[:, c], ln2b_sb[:, c], a, y_done)

        @block.gpsimd
        def _(pool):
            def lo_steps(g, ks):
                for k in ks:
                    pool.wait_ge(hi_done, STEPS * g + k + 1)
                    pool.tensor_tensor(w_lo[:, k, :], raw[:, k, :], w_hi[:, k % HI_RING, :].bitcast(F32), ALU.subtract).then_inc(lo_done, 1)

            def ln_power(n, c):
                pool.wait_ge(ln_stat, n)
                pool.tensor_tensor(rstd[:, c], var16[:, c], power[:, c], ALU.pow).then_inc(ln_rstd, 1)

            with pool.Fori(0, B_END - 1) as g:
                lo_steps(g, range(STEPS))
            lo_steps(B_END - 1, range(4))
            pool.wait_ge(stat_done, 1)
            pool.tensor_tensor(rstd[:], var16[:], power[:], ALU.pow).then_inc(rstd_done, 1)
            lo_steps(B_END - 1, range(4, STEPS))
            with pool.Fori(B_END, O_END) as g:
                lo_steps(g, range(STEPS))
            lo_steps(O_END, range(4))
            ln_power(1, slice(0, TT))
            lo_steps(O_END, range(4, STEPS))
            with pool.Fori(O_END + 1, Q_END) as g:
                lo_steps(g, range(STEPS))
            with pool.Fori(0, P) as i:
                for f in range(4):
                    pool.wait_ge(uhi_done, i * 4 + f + 1)
                    pool.tensor_tensor(u_lo[:, f, :], u_t[:, f, :], u_hi[:, f, :].bitcast(F32), ALU.subtract).then_inc(ulo_done, 1)
            for a in range(TT):
                ln_power(2 + a, slice(a, a + 1))

        @block.tensor
        def _(pe):
            by_tile = lambda s, a, k: s[:, a, k * P:(k + 1) * P]

            def turn(src, use, c, ready, n):
                q = use * 8 + c
                pe.wait_ge(ready, n)
                if c >= 4:
                    pe.wait_ge(tr_lo, q - 3)
                for k in range(2):
                    for a in range(TT):
                        o = (k * TT + a) * P
                        ins = pe.transpose(bank(4 + c % 4)[:, o:o + P], by_tile(src, a, 2 * c + k), ident)
                ins.then_inc(tr_done, 1)

            def three(o, lh, ll, rh, rl, start, stop, lint=False):
                pe.matmul(o, lh, rh, start=start, stop=False, skip_group_check=lint)
                pe.matmul(o, lh, rl, start=False, stop=False, skip_group_check=lint)
                return pe.matmul(o, ll, rh, start=False, stop=stop, skip_group_check=lint)

            def steps_n(g, ks=range(STEPS)):
                for k in ks:
                    if k == 0:
                        pe.wait_ge(acc_free, g + 1)
                    pe.wait_ge(lo_done, STEPS * g + k + 1)
                    for kt in (2 * k, 2 * k + 1):
                        for n in range(4):
                            c = slice(kt % 2 * COL + n * P, kt % 2 * COL + (n + 1) * P)
                            o = ps[:, 2 * (g % 2) + n // 2, (n % 2) * T:(n % 2 + 1) * T]
                            ins = three(o, w_hi[:, k % HI_RING, c], w_lo[:, k, c], xT_hi[:, kt, :], xT_lo[:, kt, :],
                                        kt == 0 and n % 2 == 0, kt == KT - 1, lint=True)
                    ins.then_inc(step_free, 1)

            def steps_t(g, ks=range(STEPS)):
                for k in ks:
                    if k == 0:
                        pe.wait_ge(acc_free, g + 1)
                    pe.wait_ge(lo_done, STEPS * g + k + 1)
                    for kt in (2 * k, 2 * k + 1):
                        c = slice(kt % 2 * COL, (kt % 2 + 1) * COL)
                        for a in range(TT):
                            t = slice(a * P, (a + 1) * P)
                            ins = three(ps[:, 2 * (g % 2) + a, :], xT_hi[:, kt, t], xT_lo[:, kt, t], w_hi[:, k % HI_RING, c], w_lo[:, k, c],
                                        kt == 0, kt == KT - 1)
                    ins.then_inc(step_free, 1)

            def turned_group(g, steps, src, use, ready):
                for c in range(3):
                    turn(src, use, c, *ready(c))
                for k in range(STEPS):
                    pe.wait_ge(tr_lo, 8 * use + k + 1)
                    steps(g, (k,))
                    if k + 3 < 8:
                        turn(src, use, k + 3, *ready(k + 3))

            pe.sem_inc(acc_free, 2)
            pe.wait_ge(keep_in, 16)
            turned_group(0, steps_n, x_sb, 0, lambda c: (x_in[c // 2], 16))
            pe.wait_ge(glrw_lo, 1)
            for kt in range(KT):
                ins = three(bank(4)[:, 0:T], glr_hi[:, kt, :], glr_lo[:, kt, :], xT_hi[:, kt, :], xT_lo[:, kt, :], kt == 0, kt == KT - 1)
            ins.then_inc(glr_done, 1)
            steps_n(1, range(3))
            pe.wait_ge(wup_in, 32)
            pe.wait_ge(glrT_done, 1)
            for h in range(GH):
                ins = pe.matmul(bank(5, 2)[:, h * T:(h + 1) * T], wup_sb[:, h * P:(h + 1) * P], glrT[0:RANK, :], start=True, stop=True)
            ins.then_inc(logit_done, 1)
            steps_n(1, range(3, STEPS))
            steps_n(2)

            head_t = lambda t, h, a: t[:, h, a * P:(a + 1) * P]
            pe.wait_ge(decay_done, 1)
            for h in range(GH):
                for a in range(TT):
                    o = (h * TT + a) * P
                    ins = pe.transpose(bank(4, 2)[:, o:o + P], head_t(k_out, h, a), ident)
            ins.then_inc(kt_mm, 1)

            def level(n):
                if n:
                    pe.wait_ge(lvl_ready, n)
                if n == 1:
                    pe.wait_ge(kt_sb, 1)
                if n >= 2:
                    pe.wait_ge(lvl_acc, n - 1)
                kk, qq = (lvl_k, lvl_q) if n else (proj_n[:, 4:8, :], proj_n[:, 0:4, :])
                for h in range(GH):
                    for a in range(TT):
                        o = (h * TT + a) * P
                        ins = pe.matmul(bank(6 - 2 * (n % 2), 2)[:, o:o + P], head_t(kk, h, a), head_t(qq, h, a), start=True, stop=True)
                ins.then_inc(lvl_mm, 1)

            level(0)
            for g in range(3, A_END):
                for half in range(2):
                    steps_n(g, range(4 * half, 4 * half + 4))
                    level(2 * (g - 3) + half + 1)

            rq, rk = (proj_n[:, n:n + 8, :].rearrange("p (h s) t -> p h s t", s=2) for n in (8, 16))

            def turn_keys(h):
                for a in range(TT):
                    for s in range(2):
                        o = (a * 2 + s) * P
                        ins = pe.transpose(bank(4 + (h + 2) % 4)[:, o:o + P], rk[:, h, s, a * P:(a + 1) * P], ident)
                ins.then_inc(rkt_mm, 1)

            def values(h, a, ret):
                return proj_v[:, a, K * ret + h * GDV:K * ret + (h + 1) * GDV]

            def half(c):
                return slice(CH * (c % 2), CH * (c % 2) + CH)

            def gla_u(h):
                if h:
                    pe.wait_ge(s_done, h)
                for c in range(NCH - 1):
                    o = (h * TT + c // 2) * P
                    ins = pe.matmul(bank(4, 2)[:, SLOT[c] * GDV:(SLOT[c] + 1) * GDV],
                                    k_outT[:].rearrange("p a b -> p (a b)")[half(c), o:o + P],
                                    values(h, c // 2, 0)[half(c), :], start=True, stop=True)
                ins.then_inc(u_mm, 1)

            def gla_o(h):
                pe.wait_ge(s_done, h + 1)
                if h >= 2:
                    pe.wait_ge(o_evac, h - 1)
                for a in range(TT):
                    o = bank(6 + h % 2)[:, a * GDV:(a + 1) * GDV]
                    for c in (2 * a, 2 * a + 1):
                        pe.matmul(o[half(c), :], q_in[:, h, c * CH:(c + 1) * CH], states[:, h % 2, c, :], start=True, stop=False)
                    ins = pe.matmul(o, a_gla[:, h, a * P:(a + 1) * P], values(h, a, 0), start=False, stop=True)
                ins.then_inc(o_mm, 1)

            def ret_u(h):
                if h:
                    pe.wait_ge(rs_done, h)
                else:
                    pe.wait_ge(o_evac, 3)
                for c in range(NCH - 1):
                    for s in range(2):
                        o = (SLOT[c] * 2 + s) * GDV
                        ins = pe.matmul(bank(4, 3)[:, o:o + GDV], rkT[half(c), h, c // 2, s * P:(s + 1) * P],
                                        values(h, c // 2, 1)[half(c), :], start=True, stop=True)
                ins.then_inc(ru_mm, 1)

            def ret_o(h):
                pe.wait_ge(rs_done, h + 1)
                pe.wait_ge(ro_evac if h else o_evac, h if h else GH)
                for a in range(TT):
                    o = bank(7)[:, a * RDV:(a + 1) * RDV]
                    for c in (2 * a, 2 * a + 1):
                        for s in range(2):
                            pe.matmul(o[half(c), :], rq[:, h, s, c * CH:(c + 1) * CH], states[:, s, c, :], start=s == 0, stop=False)
                    ins = pe.matmul(o, a_ret[:, h * TT + a, :], values(h, a, 1), start=False, stop=True)
                ins.then_inc(ro_mm, 1)

            steps_t(A_END)
            steps_t(A_END + 1, range(4))
            pe.wait_ge(rot_done, RH)
            pe.wait_ge(lvl_acc, LEVELS + 1)
            for h in range(RH):
                for a in range(TT):
                    o = (h * TT + a) * P
                    t = slice(a * P, (a + 1) * P)
                    for s in range(2):
                        ins = pe.matmul(bank(4, 2)[:, o:o + P], rk[:, h, s, t], rq[:, h, s, t], start=s == 0, stop=s == 1)
            ins.then_inc(rs_mm, 1)
            turn_keys(0)
            turn_keys(1)
            steps_t(A_END + 1, range(4, STEPS))
            pe.wait_ge(ra_done, 1)
            turn_keys(2)
            turn_keys(3)
            steps_t(A_END + 2, range(4))
            pe.wait_ge(rkt_sb, RH)
            pe.wait_ge(rq_done, 1)
            gla_u(0)
            steps_t(A_END + 2, range(4, STEPS))
            gla_o(0)
            gla_u(1)
            steps_t(A_END + 3, range(4))
            gla_o(1)
            gla_u(2)
            steps_t(A_END + 3, range(4, STEPS))
            gla_o(2)
            gla_u(3)
            steps_t(V_END, range(4))
            gla_o(3)
            ret_u(0)
            steps_t(V_END, range(4, STEPS))
            ret_o(0)
            ret_u(1)
            steps_t(V_END + 1, range(4))
            ret_o(1)
            ret_u(2)
            steps_t(V_END + 1, range(4, STEPS))
            ret_o(2)
            ret_u(3)
            steps_t(V_END + 2, range(4))
            ret_o(3)
            steps_t(V_END + 2, range(4, STEPS))
            steps_t(V_END + 3)

            turned_group(B_END, steps_t, o_sb, 1, lambda c: (mix_done, c // 2 + 1))
            for g in range(B_END + 1, O_END):
                steps_t(g)
            turned_group(O_END, steps_n, h1_perm, 2, lambda c: (h1p_done, 2 * (c // 2) + 2))
            for g in range(O_END + 1, Q_END):
                steps_n(g)
            pe.wait_ge(sk_in, 16)
            for c in range(4):
                for k in range(4):
                    ins = pe.transpose(bank(4 + c)[:, k * P:(k + 1) * P], sk_raw[:, 4 * c + k, :], ident)
                ins.then_inc(sk_mm, 1)
            pe.wait_ge(sk_sb, 4)
            pe.wait_ge(acc_free, 2 + Q_END)
            for a in range(TT):
                for r in range(2 * PH):
                    ins = pe.matmul(bank(4 * a, 4)[:, r * NK:(r + 1) * NK], qT[:, r, a * P:(a + 1) * P], skT[:, r, :], start=True, stop=True)
                ins.then_inc(score_mm, 1)
            pe.wait_ge(score_sb, 2)

            pe.sem_inc(uparts_free, 4)

            def u_tile(ii, s, first=False, spreads=False):
                i = ii * 2 + s
                if not first:
                    pe.wait_ge(gelu_done, i - 1)
                for f in range(4):
                    pe.wait_ge(ulo_done, ii * 8 + 4 * s + f + 1)
                    for k in range(4):
                        c = slice(k * P, (k + 1) * P)
                        kt = 4 * f + k
                        ins = three(bank(s)[:, 0:T], u_hi[:, f, c], u_lo[:, f, c], xT_hi[:, kt, :], xT_lo[:, kt, :], kt == 0, kt == KT - 1)
                    ins.then_inc(uparts_free, 1)
                if spreads:
                    q = i - U_ONES
                    pe.wait_ge(hot_done, q + 1)
                    pe.wait_ge(spread_free, q + 1)
                    for k in range(4):
                        ins = pe.matmul(bank(2 + s)[:, k * P:(k + 1) * P], hot_j[:, s, k, :], hot_i[:, s, k, :], start=True, stop=True)
                    ins.then_inc(spread_mm, 1)

            for s in range(2):
                u_tile(0, s, first=True)
            with pe.Fori(1, U_ROUTE // 2) as ii:
                for s in range(2):
                    u_tile(ii, s)
            pe.wait_ge(ijg_done, 1)
            for s in range(3):
                for a in range(TT):
                    o = (s * TT + a) * P
                    ins = pe.transpose(bank(4, 2)[:, o:o + P], ijg[:, s, a, :], ident)
            ins.then_inc(ijg_mm, 1)
            with pe.Fori(U_ROUTE // 2, U_ONES // 2) as ii:
                for s in range(2):
                    u_tile(ii, s)
            pe.sem_inc(spread_free, 2)
            with pe.Fori(U_ONES // 2, P // 2) as ii:
                for s in range(2):
                    u_tile(ii, s, spreads=True)

            def v_products(s, h, a, start=False, stop=False):
                t = slice(a * P, (a + 1) * P)
                mh, ml = m_hi[:, s % 2, t], m_lo[:, s % 2, t]
                vh, vl = v_hi[:, 2 * (s % 2) + h, :], v_lo[:, 2 * s + h, :]
                for p, (m, v) in enumerate(((mh, vh), (mh, vl), (ml, vh))):
                    for c in range(2):
                        ins = pe.matmul(bank(4 * a + 2 * h + c), m, v[:, c * 512:(c + 1) * 512], start=start and p == 0, stop=stop and p == 2)
                return ins

            def v_tile(i, s, start=False):
                for h in range(2):
                    pe.wait_ge(v_lo_done, 2 * i + h + 1)
                    for a in range(TT):
                        ins = v_products(s, h, a, start=start)
                    ins.then_inc(v_free, 1)

            pe.wait_ge(spread_free, 2 + P - U_ONES)
            for i in range(4):
                v_tile(i, i, start=i == 0)
            with pe.Fori(1, P // 4 - 1) as ii:
                for s in range(4):
                    v_tile(ii * 4 + s, s)
            v_tile(P - 4, 0)
            v_tile(P - 3, 1)
            pe.wait_ge(v_lo_done, 2 * P)
            for a in range(TT):
                for i in (P - 2, P - 1):
                    for h in range(2):
                        ins = v_products(i % 4, h, a, stop=i == P - 1)
                ins.then_inc(sum_done, 1)


_INS = ["x", "w_in", "w_gla_gate_up", "b_gla_gate", "gla_norm_g", "ret_norm_g", "w_out", "ln1_g", "ln1_b",
        "w_peer_q", "peer_subkeys", "peer_u", "peer_v", "ln2_g", "ln2_b"]


def kernel(**inputs):
    import concourse.bacc as bacc
    from concourse.bass_utils import run_bass_kernel_spmd

    nc = bacc.Bacc("TRN2", target_bir_lowering=False, num_devices=1)
    keep_c, mix_c = constants()
    arrays, args = {}, []
    for name, a in [(n, inputs[n]) for n in _INS] + [("keep_c", keep_c), ("mix_c", mix_c)]:
        a = np.ascontiguousarray(a)
        arrays[f"in_{name}"] = a
        args.append(nc.dram_tensor(f"in_{name}", a.shape, mybir.dt.from_np(a.dtype), kind="ExternalInput").ap())
    args.append(nc.dram_tensor("out_0", (1, T, D), F32, kind="ExternalOutput").ap())
    build(nc, *args)
    r = run_bass_kernel_spmd(nc, [arrays], core_ids=[0])
    return r.results[0]["out_0"]
```

```python
import numpy as np
from contextlib import ExitStack
import concourse.bass as bass
from concourse import mybir

F32 = mybir.dt.float32
F32R = mybir.dt.float32r
U32 = mybir.dt.uint32
ALU = mybir.AluOpType
ACT = mybir.ActivationFunctionType
AX = mybir.AxisListType

P = 128
T, D = 256, 2048
TT, KT = T // P, D // P
CH = 64
NCH = T // CH
GH, GDK, GDV = 4, 128, 256
RH, RDK, RDV = 4, 256, 256
RANK = 16
PH, NK, TOPK = 8, 128, 16
COL = 512
EPS = 1e-5
ALPHA = 2 ** 0.25
LOW = -3.0e38

GQ, GV, GLR = 0, 1024, 3072
RQ, RV = GLR + RANK, GLR + RANK + 2048
U_ROUTE, U_ONES = 40, 64
A_END, V_END, B_END, O_END, Q_END = 6, 10, 14, 18, 22
STEPS = 8
VRING = 8
LEAD = 3
RING, HI_RING = 8, 4
LEVELS = 6

LOG_GAMMA = np.log(1.0 - 2.0 ** (-5.0 - np.arange(RH, dtype=np.float32))).astype(np.float32)

KEEP = {"ident": P, "iota": P, "iota16": TOPK, "one": 1}
MIX = {"cos": T, "sin": T, "scan": T, "masks": (LEVELS + 1) * P, "decay": 3 * RH * P}


def constants():
    c = {}
    c["ident"] = np.eye(P, dtype=np.float32)
    c["iota"] = np.broadcast_to(np.arange(P, dtype=np.float32), (P, P))
    c["iota16"] = np.broadcast_to(np.arange(TOPK, dtype=np.float32), (P, TOPK))
    c["one"] = np.ones((P, 1))
    half = RDK // 2
    inv = np.float32(10000.0) ** (-np.arange(half, dtype=np.float32) / np.float32(half))
    ang = np.arange(T, dtype=np.float32)[None, :] * inv.astype(np.float32)[:, None]
    c["cos"], c["sin"] = np.cos(ang), np.sin(ang)
    t = np.arange(T)
    c["scan"] = np.broadcast_to((t % CH != 0).astype(np.float32), (P, T))
    m, n = np.meshgrid(np.arange(P), np.arange(P), indexing="ij")
    masks = [(m // (CH >> l) == n // (CH >> l)) & (m // (CH >> (l + 1)) != n // (CH >> (l + 1))) for l in range(LEVELS)]
    c["masks"] = np.concatenate([*masks, m == n], axis=1)
    scale = np.float32(RDK ** -0.5)
    tiles = lambda g: [np.where(m // CH <= n // CH, np.exp(g * np.abs(m - n).astype(np.float32)), 0) * scale] * 2 + \
        [np.exp(g * (P + n - m).astype(np.float32)) * scale]
    c["decay"] = np.concatenate([b for g in LOG_GAMMA for b in tiles(g)], axis=1)
    pack = lambda names: np.ascontiguousarray(np.concatenate([c[k].astype(np.float32) for k in names], axis=1))
    return pack(KEEP), pack(MIX)


def build(nc, x, w_in, w_up, b_gate, gla_g, ret_g, w_out, ln1_g, ln1_b, w_q, subkeys, peer_u, peer_v,
          ln2_g, ln2_b, keep_c, mix_c, out):
    ctx = ExitStack()
    with ctx:
        sem = lambda name: ctx.enter_context(nc.semaphore(name))

        base = -(-nc.sbuf_base // 64) * 64
        K = 1024

        def at(name, off, shape, dt=F32):
            return nc.alloc_sbuf_tensor_at(name, shape, dt, offset=base + off)

        BIG, HT, WRK, CST = 0, 128 * K, 160 * K, 200 * K
        act_w = at("act_w", BIG, [P, P, T])
        xT_hi, xT_lo = at("xT_hi", HT, [P, KT, T], F32R), at("xT_lo", HT + 16 * K, [P, KT, T], F32R)
        raw = at("raw", BIG, [P, RING, 2 * COL])
        w_lo = at("w_lo", BIG, [P, RING, 2 * COL], F32R)
        w_hi = at("w_hi", BIG + 32 * K, [P, HI_RING, 2 * COL], F32R)
        proj_v = at("proj_v", BIG + 64 * K, [P, TT, 4 * COL])
        swish = at("swish", BIG + 80 * K, [P, TT, D])
        proj_n = at("proj_n", BIG + 96 * K, [P, 24, T])
        mixc = at("mixc", WRK, [P, sum(MIX.values())])
        x_sb = at("x_sb", WRK + 13 * K, [P, TT, D])
        o_sb = at("o_sb", WRK + 13 * K, [P, TT, D])
        gains = at("gains", BIG + 96 * K, [P, D])
        glr_raw = at("glr_raw", BIG + 80 * K, [P, KT, P])
        glr_hi = at("glr_hi", BIG + 64 * K, [P, KT, P], F32R)
        glr_lo = at("glr_lo", BIG + 72 * K, [P, KT, P], F32R)
        wup = at("wup", WRK + 37 * K, [P, GH * GDK])
        small = at("small", CST + 17 * K // 4, [P, 256])
        keepc = at("keepc", CST, [P, sum(KEEP.values())])
        b_cum, lvl_e, k_out, a_gla = (at(n, BIG + (48 + 4 * i) * K, [P, 4, T]) for i, n in enumerate(("b_cum", "lvl_e", "k_out", "a_gla")))
        lvl_tmp = at("lvl_tmp", BIG + 56 * K, [P, 8, P])
        lvl_q, lvl_k = at("lvl_q", BIG + 120 * K, [P, 4, T]), at("lvl_k", BIG + 124 * K, [P, 4, T])
        q_in = at("q_in", WRK + 29 * K, [P, 4, T])
        a_far = at("a_far", WRK + 33 * K, [P, GH, P])
        q_far = at("q_far", WRK + 35 * K, [P, GH, 4, CH])
        a_ret = at("a_ret", BIG + 48 * K, [P, RH, 3, P])
        rot_tmp = at("rot_tmp", BIG + 52 * K, [P, 2, 2, T])
        sig = at("sig", BIG + 56 * K, [P, TT, COL])
        y_sb = o_sb
        ln_g = at("ln_g", BIG + 64 * K, [P, D])
        ln_b = at("ln_b", BIG + 72 * K, [P, D])
        x_again = at("x_again", BIG + 112 * K, [P, TT, D])
        h1_perm = at("h1_perm", BIG + 80 * K, [P, TT, D])
        qT = at("qT", BIG + 64 * K, [P, 2 * PH, T])
        sk_raw = at("sk_raw", BIG + 96 * K, [P, 2 * PH, P])
        skT = at("skT", BIG + 104 * K, [P, 2 * PH, P])
        scores = at("scores", BIG + 80 * K, [P, TT, 2 * PH, NK])
        scores2 = at("scores2", BIG + 48 * K, [P, TT, 2 * PH, NK])
        cand = at("cand", BIG + 48 * K, [P, TT * PH, TOPK * TOPK])
        cand2 = at("cand2", BIG + 80 * K, [P, TT * PH, TOPK * TOPK])
        pick = at("pick", BIG + 64 * K, [P, TT * PH * TOPK, TOPK])
        vals = at("vals", BIG + 112 * K, [P, TT, 2 * PH, TOPK])
        idx_u = at("idx_u", BIG + 114 * K, [P, TT, 2 * PH, TOPK], U32)
        idx_f = at("idx_f", BIG + 116 * K, [P, TT, PH, 2, TOPK])
        tops = at("tops", BIG + 118 * K, [P, TT * PH, TOPK])
        sel_u = at("sel_u", BIG + 119 * K, [P, TT * PH, TOPK], U32)
        sel_ab = at("sel_ab", BIG + 120 * K, [P, 2, TT * PH, TOPK], U32)
        sel_f = at("sel_f", BIG + 122 * K, [P, 2, TT * PH, TOPK])
        ijg = at("ijg", BIG + 124 * K, [P, 3, TT, P])
        ijgT = at("ijgT", CST + 5 * K // 4, [P, 3, T])
        u_raw = at("u_raw", WRK, [P, 2, 4 * COL])
        u_t = at("u_t", WRK + 16 * K, [P, 4, 4 * P])
        u_lo = at("u_lo", WRK + 16 * K, [P, 4, 4 * P], F32R)
        u_hi = at("u_hi", WRK + 24 * K, [P, 4, 4 * P], F32R)
        gelu_sb = at("gelu_sb", CST + 21 * K // 4, [P, 2, T])
        hot_j = at("hot_j", WRK + 32 * K, [P, 2, 4, P])
        hot_i = at("hot_i", WRK + 36 * K, [P, 2, 4, P])
        HALF = D // 2
        v_raw = at("v_raw", WRK, [P, VRING, HALF])
        v_lo = at("v_lo", WRK, [P, VRING, HALF], F32R)
        v_hi = at("v_hi", HT, [P, 4, HALF], F32R)
        m_hi = at("m_hi", CST + 21 * K // 4, [P, 2, T], F32R)
        m_lo = at("m_lo", CST + 5 * K // 4, [P, 2, T], F32R)
        v_hi4 = at("v_hi4", BIG + 32 * K, [P, 8, HALF], F32R)
        m_hi4, m_lo4 = at("m_hi4", BIG + 64 * K, [P, 4, T], F32R), at("m_lo4", BIG + 68 * K, [P, 4, T], F32R)
        h1_again = at("h1_again", HT + 16 * K, [P, TT, D])
        ln2g_sb = at("ln2g_sb", WRK + 32 * K, [P, D])
        ln2b_sb = at("ln2b_sb", BIG, [P, D])
        h1_dram = nc.dram_tensor("h1_dram", [T, D], F32, kind="Internal").ap()

        def cols(tensor, table, name):
            off = 0
            for k, n in table.items():
                if k == name:
                    return tensor[:, off:off + n]
                off += n

        ident = cols(keepc, KEEP, "ident")
        iota = cols(keepc, KEEP, "iota")
        one = cols(keepc, KEEP, "one")
        iota16 = cols(keepc, KEEP, "iota16")
        mc = lambda name: cols(mixc, MIX, name)

        bias4 = small[:, 0:4]
        stat6 = small[:, 8:8 + 96].rearrange("p (n s) -> p n s", s=6)
        mv = small[:, 104:136].rearrange("p (n s) -> p n s", s=2)
        rstd = small[:, 136:152]
        power = small[:, 152:168]
        var16 = small[:, 168:184]
        last_e = small[:, 184:200]
        gmax = small[:, 200:216]
        wup_sb = wup[0:RANK, :]
        glrT = at("glrT", CST + 5 * K // 4, [P, T])

        ps = ctx.enter_context(nc.psum_tensor("ps", [P, 8, 512], F32))

        def bank(i, n=1):
            return ps[:, i:i + n, :].rearrange("p a b -> p (a b)")

        keep_in, mix_in, glrw_in, wup_in = sem("keep_in"), sem("mix_in"), sem("glrw_in"), sem("wup_in")
        x_in = [sem(f"x_in{i}") for i in range(4)]
        raw_in = [sem(f"raw_in{i}") for i in range(RING)]
        step_free, hi_done, lo_done, acc_free = sem("step_free"), sem("hi_done"), sem("lo_done"), sem("acc_free")
        tr_done, tr_hi, tr_lo = sem("tr_done"), sem("tr_hi"), sem("tr_lo")
        glrw_hi, glrw_lo, glr_done, glrT_done, logit_done = (sem(n) for n in ("glrw_hi", "glrw_lo", "glr_done", "glrT_done", "logit_done"))
        logsig_act, b_done, decay_act, decay_d, decay_done = (sem(n) for n in ("logsig_act", "b_done", "decay_act", "decay_d", "decay_done"))
        lvl_diff, lvl_exp, lvl_ready, lvl_mm, lvl_acc = (sem(n) for n in ("lvl_diff", "lvl_exp", "lvl_ready", "lvl_mm", "lvl_acc"))
        far_sb, o_mm, o_evac = sem("far_sb"), sem("o_mm"), sem("o_evac")
        rot_done, rs_mm, ra_done, ro_mm, ro_evac = (sem(n) for n in ("rot_done", "rs_mm", "ra_done", "ro_mm", "ro_evac"))
        sig_done, stat_done, rstd_done, mix_done, gains_in = (sem(n) for n in ("sig_done", "stat_done", "rstd_done", "mix_done", "gains_in"))
        x2_in, ln1_in, h1_done, h1_out = sem("x2_in"), sem("ln1_in"), sem("h1_done"), sem("h1_out")
        h1p_done = sem("h1p_done")
        sk_in, sk_mm, sk_sb, score_mm, score_sb = (sem(n) for n in ("sk_in", "sk_mm", "sk_sb", "score_mm", "score_sb"))
        soft_d, soft_e, ijg_done, ijg_mm, ijg_sb = (sem(n) for n in ("soft_d", "soft_e", "ijg_done", "ijg_mm", "ijg_sb"))
        u_in = [sem("u_in0"), sem("u_in1")]
        ut_done, uhi_done, ulo_done, uparts_free, gelu_done, gelu_free = (
            sem(n) for n in ("ut_done", "uhi_done", "ulo_done", "uparts_free", "gelu_done", "gelu_free"))
        hot_done, spread_mm, spread_free = sem("hot_done"), sem("spread_mm"), sem("spread_free")
        v_in = [sem(f"v_in{i}") for i in range(4)]
        v_hi_done, m_hi_done, v_lo_done, v_free, sum_done = sem("v_hi_done"), sem("m_hi_done"), sem("v_lo_done"), sem("v_free"), sem("sum_done")
        last_in, y_done, out_done = sem("last_in"), sem("y_done"), sem("out_done")
        ln_stat, ln_rstd = sem("ln_stat"), sem("ln_rstd")

        win = w_in[0]
        w_rows = lambda w, k: w[2 * k * P:2 * (k + 1) * P, :].rearrange("(k p) n -> p k n", p=P)
        wq_rows = w_q[0].rearrange("(q f l) n -> q l f n", q=4, f=KT)
        u_rows = peer_u[0].rearrange("(i b l) (q d) -> i q l b d", b=4, l=32, q=4)
        v_rows = peer_v[0].rearrange("(i j) d -> i j d", j=P)

        def raw_count(g):
            return 16 * (g + 1) if not isinstance(g, int) or g < O_END else 16 * O_END + 64 * (g + 1 - O_END)

        def used(g, k=STEPS - 1):
            return RING + STEPS * g + k + 1

        block = ctx.enter_context(nc.Block())

        @block.sync
        def _(sp):
            def load_step(g, k, w, col):
                sp.wait_ge(step_free, STEPS * g + k + 1)
                sp.dma_start(raw[:, k, :].rearrange("p (k n) -> p k n", k=2), w_rows(w, k)[:, :, bass.ds(col, COL)]).then_inc(raw_in[k], 16)

            def load(g, w, col):
                for k in range(STEPS):
                    load_step(g, k, w, col)

            sp.sem_inc(step_free, RING)
            sp.dma_start(keepc[:], keep_c).then_inc(keep_in, 16)
            for b in range(4):
                c = slice(b * COL, (b + 1) * COL)
                load_step(0, 2 * b, win, GQ)
                sp.dma_start(x_sb[:, :, c], x[0].rearrange("(a p) d -> p a d", p=P)[:, :, c]).then_inc(x_in[b], 16)
                load_step(0, 2 * b + 1, win, GQ)
            sp.dma_start(glr_raw[:], win[:, GLR:GLR + P].rearrange("(k p) n -> p k n", p=P)).then_inc(glrw_in, 16)
            sp.dma_start(wup_sb, w_up[0]).then_inc(wup_in, 16)
            with nc.allow_non_contiguous_dma(reason="512 bias values, one channel a partition"):
                sp.dma_start(bias4, b_gate[0].rearrange("(h p) -> p h", p=P)).then_inc(wup_in, 16)
            load(1, win, GQ + COL)
            sp.dma_start(mixc[:], mix_c).then_inc(mix_in, 16)
            with sp.Fori(2, A_END) as g:
                load(g, win, RQ + (g - 2) * COL)
            for g in range(A_END, B_END):
                half, first = divmod(g - A_END, 4)
                load(g, win, (GV if first < 2 else RV) + 2 * COL * half + COL * (first % 2))
                if g == V_END + 1:
                    sp.wait_ge(ro_mm, RH)
                    sp.dma_start(x_again[:], x[0].rearrange("(a p) d -> p a d", p=P)).then_inc(x2_in, 16)
                    sp.dma_start(ln_g[:], ln1_g[0:1, :].to_broadcast([P, D])).then_inc(ln1_in, 16)
                    sp.dma_start(ln_b[:], ln1_b[0:1, :].to_broadcast([P, D])).then_inc(ln1_in, 16)
                if g == A_END + 2:
                    sp.wait_ge(lvl_acc, LEVELS + 1)
                    sp.dma_start(gains[:, 0:D // 2], gla_g[0:1, :].to_broadcast([P, D // 2])).then_inc(gains_in, 16)
                    sp.dma_start(gains[:, D // 2:], ret_g[0:1, :].to_broadcast([P, D // 2])).then_inc(gains_in, 16)
            with sp.Fori(B_END, O_END) as g:
                load(g, w_out[0], (g - B_END) * COL)
            sp.wait_ge(mix_done, 4)
            sp.dma_start(sk_raw[:], subkeys[0].rearrange("h s k d -> k (h s) d")).then_inc(sk_in, 16)
            for g in range(O_END, Q_END):
                col = (g - O_END) * COL
                for k in range(STEPS):
                    sp.wait_ge(step_free, STEPS * g + k + 1)
                    for q in range(4):
                        sp.dma_start(raw[32 * q:32 * q + 32, k, :].rearrange("p (k n) -> p k n", k=2),
                                     wq_rows[q][:, 2 * k:2 * k + 2, col:col + COL]).then_inc(raw_in[k], 16)
                if g == O_END:
                    sp.wait_ge(h1_done, 8)
                    sp.dma_start(h1_dram.rearrange("(a p) d -> p a d", p=P), y_sb[:]).then_inc(h1_out, 16)
            sp.wait_ge(h1_out, 16)
            sp.wait_ge(tr_lo, 24)
            def load_u(ii, s):
                for q in range(4):
                    sp.dma_start(u_raw[32 * q:32 * q + 32, s, :].rearrange("p (b d) -> p b d", b=4),
                                 u_rows[bass.ds(ii * 2 + s, 1), q].rearrange("i l b d -> l (i b) d")).then_inc(u_in[s], 16)

            load_u(0, 0)
            load_u(0, 1)
            with sp.Fori(1, P // 2) as ii:
                for s in range(2):
                    sp.wait_ge(ut_done, ii * 8 + 4 * s - 4)
                    load_u(ii, s)
            sp.sem_inc(v_free, VRING)

            def load_v(i, s):
                sp.dma_start(v_raw[:, 2 * s:2 * s + 2, :].rearrange("p a b -> p (a b)"), v_rows[bass.ds(i, 1)].rearrange("i j d -> j (i d)")).then_inc(v_in[s], 16)

            for s in range(2):
                sp.wait_ge(ut_done, 4 * (P - 1) + 4 * s)
                load_v(s, s)
            sp.wait_ge(uparts_free, 4 + 4 * P)
            for s in range(2, 4):
                load_v(s, s)
            sp.dma_start(h1_again[:], h1_dram.rearrange("(a p) d -> p a d", p=P)).then_inc(last_in, 16)
            sp.wait_ge(spread_mm, 2 + P - U_ONES)
            sp.dma_start(ln2g_sb[:], ln2_g[0:1, :].to_broadcast([P, D])).then_inc(last_in, 16)
            with sp.Fori(1, P // 4) as ii:
                for s in range(4):
                    sp.wait_ge(v_free, ii * 8 + 2 * s + 2)
                    load_v(ii * 4 + s, s)
            sp.dma_start(ln2b_sb[:], ln2_b[0:1, :].to_broadcast([P, D])).then_inc(last_in, 16)
            for a in range(TT):
                for b in range(4):
                    c = slice(b * COL, (b + 1) * COL)
                    sp.wait_ge(y_done, 4 * a + b + 1)
                    sp.dma_start(out[0, a * P:(a + 1) * P, c], h1_again[:, a, c]).then_inc(out_done, 16)
            sp.wait_ge(out_done, 16 * TT * 4)

        def act_turn(act, use, c):
            act.wait_ge(tr_done, use * 8 + c + 1)
            act.activation(xT_hi[:, 2 * c:2 * c + 2, :].rearrange("p a b -> p (a b)"), bank(4 + c % 4), ACT.Copy).then_inc(tr_hi, 1)

        @block.scalar
        def _(act):
            def hi_steps(g, ks):
                for k in ks:
                    act.wait_ge(raw_in[k], raw_count(g))
                    act.wait_ge(step_free, used(g, k - HI_RING))
                    act.activation(w_hi[:, k % HI_RING, :], raw[:, k, :], ACT.Copy).then_inc(hi_done, 1)

            def evac_n(g, dst, tile):
                act.wait_ge(step_free, used(g))
                act.activation(dst[:, tile:tile + 4, :], bank(2 * (g % 2), 2).rearrange("p (a b) -> p a b", a=4), ACT.Copy).then_inc(acc_free, 1)

            def evac_t(g):
                act.wait_ge(step_free, used(g))
                act.activation(proj_v[:, :, (g - A_END) * COL:(g - A_END + 1) * COL], ps[:, 2 * (g % 2):2 * (g % 2) + 2, :], ACT.Copy).then_inc(acc_free, 1)

            def gate(g):
                act.wait_ge(step_free, used(g))
                if g > V_END:
                    act.wait_ge(acc_free, 2 + g)
                act.activation(sig[:], ps[:, 2 * (g % 2):2 * (g % 2) + 2, :], ACT.Sigmoid).then_inc(sig_done, 1)

            def level_exp(l):
                act.wait_ge(lvl_diff, l + 1)
                act.activation(lvl_e[:], lvl_e[:], ACT.Abs)
                act.drain()
                act.activation(lvl_e[:], lvl_e[:], ACT.Exp, scale=-1.0).then_inc(lvl_exp, 1)

            def evac_gla(h):
                act.wait_ge(o_mm, h + 1)
                act.activation(o_sb[:, :, h * GDV:(h + 1) * GDV], bank(4 + h).rearrange("p (a e) -> p a e", a=TT), ACT.Copy).then_inc(o_evac, 1)

            def evac_ret(h):
                act.wait_ge(ro_mm, h + 1)
                act.activation(o_sb[:, :, K + h * RDV:K + (h + 1) * RDV], bank(4 + h).rearrange("p (a e) -> p a e", a=TT), ACT.Copy).then_inc(ro_evac, 1)

            def heads_out(g, h):
                if g == V_END - 1:
                    evac_gla(h)
                    evac_gla(h + 1)
                elif g == V_END + 1:
                    evac_ret(h)
                    evac_ret(h + 1)

            def later_turns(g, use, lead=LEAD):
                for k in range(4, STEPS):
                    hi_steps(g, (k,))
                    act_turn(act, use, k - 4 + lead)
                for c in range(4 + lead, 8):
                    act_turn(act, use, c)

            for c in range(2):
                hi_steps(0, (c,))
                act_turn(act, 0, c)
            hi_steps(0, (2, 3))
            later_turns(0, 0, lead=2)
            act.wait_ge(glrw_in, 16)
            act.activation(glr_hi[:], glr_raw[:], ACT.Copy).then_inc(glrw_hi, 1)
            hi_steps(1, range(4))
            evac_n(0, proj_n, 0)
            hi_steps(1, (4,))
            act.wait_ge(glr_done, 1)
            act.activation(glrT[0:RANK, :], bank(4)[0:RANK, 0:T], ACT.Copy).then_inc(glrT_done, 1)
            hi_steps(1, (5, 6))
            act.wait_ge(logit_done, 1)
            act.wait_ge(wup_in, 32)
            for h in range(GH):
                act.activation(lvl_e[:, h, :], bank(5, 2)[:, h * T:(h + 1) * T], ACT.Abs, bias=bias4[:, h:h + 1])
            act.drain()
            hi_steps(1, (7,))
            act.activation(lvl_q[:], lvl_e[:], ACT.Exp, scale=-1.0)
            act.drain()
            act.activation(lvl_k[:], lvl_q[:], ACT.Ln, bias=1.0).then_inc(logsig_act, 1)
            hi_steps(2, range(4))
            evac_n(1, proj_n, 4)
            hi_steps(2, (4, 5))
            act.wait_ge(b_done, 1)
            act.activation(lvl_e[:], b_cum[:], ACT.Exp).then_inc(decay_act, 1)
            act.wait_ge(decay_d, 1)
            act.activation(lvl_k[:], lvl_q[:], ACT.Exp).then_inc(decay_act, 1)
            hi_steps(2, (6, 7))
            for g in range(3, A_END + 1):
                hi_steps(g, (0,))
                if g > 3:
                    level_exp(2 * g - 7)
                hi_steps(g, (1, 2, 3))
                evac_n(g - 1, proj_n, 4 * (g - 1))
                hi_steps(g, (4,))
                if g < A_END:
                    level_exp(2 * g - 6)
                hi_steps(g, (5, 6, 7))
            for g in range(A_END + 1, B_END):
                hi_steps(g, (0,))
                heads_out(g, 0)
                hi_steps(g, (1, 2, 3))
                evac_t(g - 1) if g <= V_END else gate(g - 1)
                hi_steps(g, (4,))
                heads_out(g, 2)
                hi_steps(g, (5, 6, 7))
            hi_steps(B_END, range(4))
            act_turn(act, 1, 0)
            act_turn(act, 1, 1)
            gate(B_END - 1)
            act_turn(act, 1, 2)
            later_turns(B_END, 1)
            for g in range(B_END + 1, O_END):
                hi_steps(g, range(STEPS))
            hi_steps(O_END, range(4))
            for c in range(4):
                act.wait_ge(sk_mm, c + 1)
                act.activation(skT[:, 4 * c:4 * c + 4, :].rearrange("p a b -> p (a b)"), bank(4 + c), ACT.Copy).then_inc(sk_sb, 1)
            for b in range(4):
                for a in range(TT):
                    act.wait_ge(h1_done, 2 * b + a + 1)
                    act.activation(h1_perm[:, a, :].rearrange("p (f q l) -> p q f l", f=KT, q=4)[:, :, 4 * b:4 * b + 4, :],
                                   y_sb[:, a, :].rearrange("p (q f l) -> p q f l", f=KT, q=4)[:, :, 4 * b:4 * b + 4, :], ACT.Copy).then_inc(h1p_done, 1)
                if b < LEAD:
                    act_turn(act, 2, b)
            later_turns(O_END, 2)
            def evac_scores(n):
                act.wait_ge(score_mm, n + 1)
                act.activation(scores[:, :, 4 * n:4 * n + 4, :].rearrange("p a r k -> p a (r k)"), ps[:, 4 + 2 * (n % 2):6 + 2 * (n % 2), :], ACT.Copy).then_inc(score_sb, 1)

            for g in range(O_END + 1, Q_END):
                hi_steps(g, (0,))
                if g > O_END + 1:
                    evac_scores(g - O_END - 2)
                hi_steps(g, (1, 2, 3))
                evac_n(g - 1, qT, 4 * (g - 1 - O_END))
                hi_steps(g, range(4, STEPS))
            evac_scores(2)

            def gelu(i, par, far):
                act.wait_ge(uparts_free, 4 * i + 8)
                if far:
                    act.wait_ge(gelu_free, i - U_ONES + 1)
                    act.activation(gelu_sb[:, par, :], bank(par)[:, 0:T], ACT.Gelu).then_inc(gelu_done, 1)
                else:
                    act.activation(act_w[:, bass.ds(i, 1), :].rearrange("p a t -> p (a t)"), bank(par)[:, 0:T], ACT.Gelu).then_inc(gelu_done, 1)

            def u_tile(i, par, evac=True, far=False):
                for f in range(4):
                    act.wait_ge(ut_done, 4 * i + f + 1)
                    act.activation(u_hi[:, f, :], u_t[:, f, :], ACT.Copy).then_inc(uhi_done, 1)
                if evac:
                    gelu(i - 1, 1 - par, far)

            u_tile(0, 0, evac=False)
            evac_n(Q_END - 1, qT, 4 * (Q_END - 1 - O_END))
            u_tile(1, 1)
            evac_scores(3)
            with act.Fori(1, (U_ROUTE - 12) // 2) as ii:
                for s in range(2):
                    u_tile(ii * 2 + s, s)
            act.wait_ge(soft_d, 1)
            act.activation(tops[:], tops[:], ACT.Exp).then_inc(soft_e, 1)
            with act.Fori((U_ROUTE - 12) // 2, U_ROUTE // 2) as ii:
                for s in range(2):
                    u_tile(ii * 2 + s, s)
            act.wait_ge(ijg_mm, 1)
            act.activation(ijgT[:].rearrange("p a b -> p (a b)"), bank(4, 2)[:, 0:3 * T], ACT.Copy).then_inc(ijg_sb, 1)
            with act.Fori(U_ROUTE // 2, U_ONES // 2) as ii:
                for s in range(2):
                    u_tile(ii * 2 + s, s)
            act.sem_inc(gelu_free, 2)
            u_tile(U_ONES, 0)
            u_tile(U_ONES + 1, 1, far=True)
            with act.Fori(U_ONES // 2 + 1, P // 2) as ii:
                for s in range(2):
                    u_tile(ii * 2 + s, s, far=True)
            gelu(P - 1, 1, True)

            def v_high(ii, s, first=False, last=False):
                vh = [v_hi4[:, 2 * s + h, :] if last else v_hi[:, 2 * (s % 2) + h, :] for h in range(2)]
                act.wait_ge(v_in[s], ii * 16 + 16)
                if not last:
                    act.wait_ge(v_free, ii * 8 + 2 * s + 5)
                act.activation(vh[0], v_raw[:, 2 * s, :], ACT.Copy).then_inc(v_hi_done, 1)
                if not last:
                    act.wait_ge(v_free, ii * 8 + 2 * s + 6)
                if first:
                    act.wait_ge(gelu_free, 2 + P - U_ONES)
                act.activation(m_hi4[:, s, :] if last else m_hi[:, s % 2, :],
                               act_w[:, bass.ds(ii * 4 + s, 1), :].rearrange("p a t -> p (a t)"), ACT.Copy).then_inc(m_hi_done, 1)
                act.activation(vh[1], v_raw[:, 2 * s + 1, :], ACT.Copy).then_inc(v_hi_done, 1)

            act.wait_ge(uparts_free, 4 + 4 * P)
            for s in range(4):
                v_high(0, s, first=s == 0)
            with act.Fori(1, P // 4 - 1) as ii:
                for s in range(4):
                    v_high(ii, s)
            for s in range(4):
                v_high(P // 4 - 1, s, last=True)

        def cols_of(y, b):
            return y.rearrange("p (q b m) -> p q b m", q=4, b=4)[:, :, b, :]

        def stat_block(dve, y, c):
            for a in range(TT):
                dve.bn_stats(stat6[:, 4 * a + c, :], y[:, a, c * COL:(c + 1) * COL])

        def norm_scale(dve):
            dve.drain()
            for a in range(TT):
                dve.bn_aggr(mv[:, a, :], stat6[:, 4 * a:4 * a + 4, :])
            dve.drain()
            dve.tensor_scalar(var16[:, 0:TT], mv[:, 0:TT, 1], EPS, None, ALU.add).then_inc(ln_stat, 1)
            dve.wait_ge(ln_rstd, 1)

        def norm_apply(dve, o, gain, shift, a, done):
            dve.scalar_tensor_tensor(o, o, mv[:, a, 0:1], gain, ALU.subtract, ALU.mult)
            dve.drain()
            dve.scalar_tensor_tensor(o, o, rstd[:, a:a + 1], shift, ALU.mult, ALU.add).then_inc(done, 1)

        def turn_lo(dve, use, c):
            dve.wait_ge(tr_hi, use * 8 + c + 1)
            sl = slice(2 * c, 2 * c + 2)
            dve.tensor_tensor(xT_lo[:, sl, :].rearrange("p a b -> p (a b)"), bank(4 + c % 4),
                              xT_hi[:, sl, :].rearrange("p a b -> p (a b)").bitcast(F32), ALU.subtract).then_inc(tr_lo, 1)

        @block.vector
        def _(dve):
            dve.memset(power[:], -0.5)
            for c in range(8):
                turn_lo(dve, 0, c)
            dve.wait_ge(glrw_hi, 1)
            dve.tensor_tensor(glr_lo[:], glr_raw[:], glr_hi[:].bitcast(F32), ALU.subtract).then_inc(glrw_lo, 1)

            dve.wait_ge(logit_done, 1)
            dve.wait_ge(wup_in, 32)
            dve.wait_ge(logsig_act, 1)
            for h in range(GH):
                dve.tensor_scalar(k_out[:, h, :], bank(5, 2)[:, h * T:(h + 1) * T], bias4[:, h:h + 1], 0.0, ALU.add, ALU.min)
            dve.wait_ge(mix_in, 16)
            dve.drain()
            dve.tensor_tensor(k_out[:], k_out[:], lvl_k[:], ALU.subtract)
            dve.drain()
            for h in range(GH):
                dve.tensor_tensor_scan(b_cum[:, h, :], mc("scan"), k_out[:, h, :], 0.0, ALU.mult, ALU.add)
            dve.drain()
            dve.tensor_scalar(b_cum[:], b_cum[:], 1.0 / 16.0, None, ALU.mult).then_inc(b_done, 1)
            dve.drain()
            chunks = lambda t: t[:].rearrange("p h (c n) -> p (h c) n", n=CH)
            dve.tensor_tensor(chunks(lvl_q), chunks(b_cum)[:, :, CH - 1:CH].to_broadcast([P, GH * NCH, CH]), chunks(b_cum), ALU.subtract).then_inc(decay_d, 1)
            gq, gk = proj_n[:, 0:4, :], proj_n[:, 4:8, :]
            dve.wait_ge(acc_free, 2 + 2)
            dve.tensor_scalar(gq, gq, float(np.float32(GDK ** -0.5)), None, ALU.mult)
            dve.wait_ge(decay_act, 2)
            dve.drain()
            dve.tensor_copy(last_e, chunks(lvl_e)[:, :, CH - 1])
            dve.tensor_tensor(q_in[:], gq, lvl_e[:], ALU.mult)
            dve.tensor_tensor(k_out[:], gk, lvl_k[:], ALU.mult)
            dve.drain()
            whole = lambda c: last_e.rearrange("p (h c) -> p h c", c=NCH)[:, :, c:c + 1]
            dve.tensor_copy(q_far[:, :, 0, :], q_in[:, :, 2 * CH:3 * CH])
            dve.tensor_tensor(q_far[:, :, 1, :], q_in[:, :, 3 * CH:4 * CH], whole(2).to_broadcast([P, GH, CH]), ALU.mult)
            dve.drain()
            dve.tensor_tensor(q_far[:, :, 2:4, :].rearrange("p h c n -> p h (c n)"), q_far[:, :, 0:2, :].rearrange("p h c n -> p h (c n)"),
                              whole(1).to_broadcast([P, GH, 2 * CH]), ALU.mult).then_inc(decay_done, 1)
            dve.drain()
            masks = mc("masks").rearrange("p (l n) -> p l n", l=LEVELS + 1)

            def gather(n):
                dve.wait_ge(lvl_mm, n + 1)
                m = n - 1 if n else LEVELS
                m8 = masks[:, m:m + 1, :].to_broadcast([P, 8, P])
                s = bank(6 - 2 * (n % 2), 2).rearrange("p (a b) -> p a b", a=8)
                a8 = a_gla[:].rearrange("p h (a b) -> p (h a) b", b=P)
                if n == 0:
                    dve.tensor_tensor(a8, s, m8, ALU.mult).then_inc(lvl_acc, 1)
                    dve.drain()
                    dve.tensor_copy(a8[0:CH, :, CH:P], bank(4)[0:CH, :].rearrange("p (a b) -> p a b", a=8))
                    dve.tensor_copy(a_far[:].rearrange("p h n -> p (h n)"), bank(5)).then_inc(far_sb, 1)
                else:
                    dve.wait_ge(lvl_acc, n)
                    dve.tensor_tensor(lvl_tmp[:], s, m8, ALU.mult)
                    dve.drain()
                    dve.tensor_tensor(a8, a8, lvl_tmp[:], ALU.add).then_inc(lvl_acc, 1)

            for l in range(LEVELS):
                m = CH >> (l + 1)
                blocks = lambda t: t[:].rearrange("p h (c n) -> p (h c) n", n=2 * m)
                bb = blocks(b_cum)
                if l:
                    dve.wait_ge(lvl_ready, l)
                dve.tensor_tensor(blocks(lvl_e), bb, bb[:, :, m - 1:m].to_broadcast([P, GH * T // (2 * m), 2 * m]), ALU.subtract).then_inc(lvl_diff, 1)
                gather(l)
                dve.wait_ge(lvl_exp, l + 1)
                dve.tensor_tensor(lvl_q[:], gq, lvl_e[:], ALU.mult)
                dve.tensor_tensor(lvl_k[:], gk, lvl_e[:], ALU.mult).then_inc(lvl_ready, 1)

            dve.wait_ge(acc_free, 2 + A_END)
            both = proj_n[:, 8:24, :].rearrange("p (h s) t -> p h s t", s=2)
            cos2, sin2 = (mc(n).unsqueeze(1).to_broadcast([P, 2, T]) for n in ("cos", "sin"))
            dve.wait_ge(lvl_ready, LEVELS)
            for h in range(0, 2 * RH, 2):
                t1, t2 = both[:, h:h + 2, 0, :], both[:, h:h + 2, 1, :]
                dve.tensor_tensor(rot_tmp[:, :, 0, :], t2, sin2, ALU.mult)
                dve.tensor_tensor(rot_tmp[:, :, 1, :], t1, sin2, ALU.mult)
                dve.drain()
                dve.tensor_tensor(t1, t1, cos2, ALU.mult)
                dve.tensor_tensor(t2, t2, cos2, ALU.mult)
                dve.drain()
                dve.tensor_tensor(t1, t1, rot_tmp[:, :, 0, :], ALU.subtract)
                dve.tensor_tensor(t2, t2, rot_tmp[:, :, 1, :], ALU.add).then_inc(rot_done, 1)
                dve.drain()
                if h == 2:
                    gather(LEVELS)

            decay = mc("decay").rearrange("p (h a n) -> p h (a n)", h=RH, a=3)
            for h in (0, 2):
                dve.wait_ge(rs_mm, h // 2 + 1)
                dve.tensor_tensor(a_ret[:, h:h + 2].rearrange("p h a n -> p h (a n)"), bank(4 + h, 2)[:, 0:6 * P].rearrange("p (h n) -> p h n", h=2),
                                  decay[:, h:h + 2, :], ALU.mult).then_inc(ra_done, 1)

            def head_stats(h):
                for a in range(TT):
                    dve.bn_stats(stat6[:, a * 8 + h, :], o_sb[:, a, h * GDV:(h + 1) * GDV])

            def swish_block(g):
                n = g - V_END
                dve.wait_ge(sig_done, n + 1)
                dve.tensor_tensor(swish[:, :, n * COL:(n + 1) * COL], ps[:, 2 * (g % 2):2 * (g % 2) + 2, :], sig[:], ALU.mult).then_inc(acc_free, 1)

            def mix_block(n):
                c = slice(n * COL, (n + 1) * COL)
                dve.tensor_tensor(o_sb[:, :, c], o_sb[:, :, c], swish[:, :, c], ALU.mult).then_inc(mix_done, 1)

            for h in range(GH):
                dve.wait_ge(o_evac, h + 1)
                head_stats(h)
            swish_block(V_END)
            for h in range(RH):
                dve.wait_ge(ro_evac, h + 1)
                head_stats(GH + h)
            dve.drain()
            for n in range(16):
                dve.bn_aggr(mv[:, n, :], stat6[:, n:n + 1, :])
            dve.drain()
            v16 = var16[:].rearrange("p (a h) -> p a h", a=TT)
            mva = mv[:].rearrange("p (a h) s -> p a h s", a=TT)
            dve.tensor_tensor(v16[:, :, 0:4], mva[:, :, 0:4, 0], mva[:, :, 0:4, 0], ALU.mult)
            dve.tensor_copy(v16[:, :, 4:8], mva[:, :, 4:8, 1])
            dve.drain()
            dve.tensor_tensor(v16[:, :, 0:4], v16[:, :, 0:4], mva[:, :, 0:4, 1], ALU.add)
            dve.drain()
            dve.tensor_scalar(var16[:], var16[:], EPS, None, ALU.add).then_inc(stat_done, 1)
            dve.wait_ge(gains_in, 32)
            dve.wait_ge(rstd_done, 1)
            for a in range(TT):
                for h in range(8):
                    n = a * 8 + h
                    o = o_sb[:, a, h * GDV:(h + 1) * GDV]
                    if h < GH:
                        dve.tensor_scalar(o, o, rstd[:, n:n + 1], None, ALU.mult)
                    else:
                        dve.tensor_scalar(o, o, mv[:, n, 0:1], rstd[:, n:n + 1], ALU.subtract, ALU.mult)
            dve.drain()
            for a in range(TT):
                dve.tensor_tensor(o_sb[:, a, :], o_sb[:, a, :], gains[:], ALU.mult)
            dve.drain()
            for n in range(3):
                if n:
                    swish_block(V_END + n)
                    dve.drain()
                mix_block(n)
            turn_lo(dve, 1, 0)
            turn_lo(dve, 1, 1)
            swish_block(B_END - 1)
            dve.drain()
            mix_block(3)
            for c in range(2, 8):
                turn_lo(dve, 1, c)

            dve.wait_ge(x2_in, 16)
            dve.wait_ge(ln1_in, 32)
            for g in range(B_END, O_END):
                c = slice((g - B_END) * COL, (g - B_END + 1) * COL)
                dve.wait_ge(step_free, used(g))
                dve.scalar_tensor_tensor(y_sb[:, :, c], x_again[:, :, c], float(ALPHA),
                                         ps[:, 2 * (g % 2):2 * (g % 2) + 2, :], ALU.mult, ALU.add).then_inc(acc_free, 1)
                dve.drain()
                stat_block(dve, y_sb, g - B_END)
            norm_scale(dve)
            for b in range(4):
                for a in range(TT):
                    norm_apply(dve, cols_of(y_sb[:, a, :], b), cols_of(ln_g[:], b), cols_of(ln_b[:], b), a, h1_done)
                if b:
                    turn_lo(dve, 2, b - 1)
            for c in range(3, 8):
                turn_lo(dve, 2, c)

            def u_quarter(ii, s, f):
                if f == 0:
                    dve.wait_ge(u_in[s], ii * 64 + 64)
                dve.wait_ge(uparts_free, ii * 8 + 4 * s + f + 1)
                dve.transpose(u_t[:, f, :].rearrange("p (f b l) -> p b f l", f=4, b=4),
                              u_raw[:, s, :].rearrange("p (b f l) -> p b f l", b=4, l=32)[:, :, 4 * f:4 * f + 4, :]).then_inc(ut_done, 1)

            def route_best(stage, part):
                a, rows = part // 4, range(4 * (part % 4), 4 * (part % 4) + 4)
                sums = range(2 * part, 2 * part + 2)
                dve.drain()
                if stage == 0:
                    dve.wait_ge(score_sb, part % 4 + 1)
                    for r in rows:
                        dve.max(vals[:, a, r, 0:8], scores[:, a, r, :])
                elif stage == 1:
                    for r in rows:
                        dve.max_index(idx_u[:, a, r, 0:8], vals[:, a, r, 0:8], scores[:, a, r, :])
                        dve.match_replace(scores2[:, a, r, :], vals[:, a, r, 0:8], scores[:, a, r, :], LOW)
                elif stage == 2:
                    for r in rows:
                        dve.max(vals[:, a, r, 8:16], scores2[:, a, r, :])
                elif stage == 3:
                    v = vals[:, a].rearrange("p (h s) k -> p h s k", s=2)
                    for r in rows:
                        dve.max_index(idx_u[:, a, r, 8:16], vals[:, a, r, 8:16], scores2[:, a, r, :])
                    dve.drain()
                    for n in sums:
                        h = n % PH
                        dve.tensor_tensor(cand[:, n, :].rearrange("p (a b) -> p a b", a=TOPK),
                                          v[:, h, 0, :].unsqueeze(2).to_broadcast([P, TOPK, TOPK]),
                                          v[:, h, 1, :].unsqueeze(1).to_broadcast([P, TOPK, TOPK]), ALU.add)
                elif stage == 4:
                    for n in sums:
                        dve.max(tops[:, n, 0:8], cand[:, n, :])
                elif stage == 5:
                    for n in sums:
                        dve.max_index(sel_u[:, n, 0:8], tops[:, n, 0:8], cand[:, n, :])
                        dve.match_replace(cand2[:, n, :], tops[:, n, 0:8], cand[:, n, :], LOW)
                elif stage == 6:
                    for n in sums:
                        dve.max(tops[:, n, 8:16], cand2[:, n, :])
                else:
                    for n in sums:
                        dve.max_index(sel_u[:, n, 8:16], tops[:, n, 8:16], cand2[:, n, :])

            def route_split():
                dve.drain()
                dve.tensor_copy(gmax[:], tops[:, :, 0])
                dve.tensor_copy(idx_f[:].rearrange("p a h s k -> p (a h s k)"), idx_u[:].rearrange("p a r k -> p (a r k)"))
                dve.tensor_scalar(sel_ab[:, 0], sel_u[:], 4, None, ALU.logical_shift_right)
                dve.tensor_scalar(sel_ab[:, 1], sel_u[:], 15, None, ALU.bitwise_and)
                dve.drain()
                dve.tensor_tensor(tops[:], tops[:], gmax[:].unsqueeze(2).to_broadcast([P, TT * PH, TOPK]), ALU.subtract).then_inc(soft_d, 1)
                dve.tensor_copy(sel_f[:], sel_ab[:])

            def route_pick(s, a, stage, part):
                h0 = 4 * part
                rows = slice(a * P + h0 * TOPK, a * P + (h0 + 4) * TOPK)
                p4 = pick[:, rows].rearrange("p (h k) a -> p h k a", h=4)
                dve.drain()
                if stage == 0:
                    dve.tensor_tensor(pick[:, rows], sel_f[:, s, a * PH + h0:a * PH + h0 + 4].rearrange("p n k -> p (n k)").unsqueeze(2).to_broadcast([P, 4 * TOPK, TOPK]),
                                      iota16.unsqueeze(1).to_broadcast([P, 4 * TOPK, TOPK]), ALU.is_equal)
                elif stage == 1:
                    dve.tensor_tensor(p4, p4, idx_f[:, a, h0:h0 + 4, s, :].unsqueeze(2).to_broadcast([P, 4, TOPK, TOPK]), ALU.mult)
                else:
                    dve.tensor_reduce(ijg[:, s, a, h0 * TOPK:(h0 + 4) * TOPK], pick[:, rows], AX.X, ALU.add).then_inc(ijg_done, 1)

            def route_gates():
                dve.wait_ge(soft_e, 1)
                dve.drain()
                dve.tensor_reduce(gmax[:], tops[:], AX.X, ALU.add)
                dve.drain()
                dve.reciprocal(rstd[:], gmax[:])
                dve.drain()
                dve.tensor_tensor(ijg[:, 2].rearrange("p a (h k) -> p (a h) k", k=TOPK), tops[:],
                                  rstd[:].unsqueeze(2).to_broadcast([P, TT * PH, TOPK]), ALU.mult).then_inc(ijg_done, 1)

            for m in range(2):
                for stage in range(8):
                    for a in range(TT):
                        route_best(stage, 4 * a + m)
            for i in range(U_ROUTE):
                for f in range(4):
                    u_quarter(i // 2, i % 2, f)
                    if i < 24 and i % 3 < 2 and f % 2:
                        n = i // 3 * 2 + i % 3
                        route_best(n % 8, 4 * (f // 2) + 2 + n // 8)
                    elif 24 < i < 37 and f % 2:
                        route_pick((i - 25) // 6, (i - 25) // 3 % 2, (i - 25) % 3, f // 2)
                if i == 24:
                    route_split()
                elif i == 30:
                    route_gates()
            dve.wait_ge(ijg_sb, 1)
            with dve.Fori(U_ROUTE // 2, U_ROUTE // 2 + 8) as ii:
                for s in range(2):
                    for f in range(4):
                        u_quarter(ii, s, f)
                    dve.tensor_copy(act_w[:, bass.ds(U_ONES + (ii * 2 + s - U_ROUTE) * 4, 4), :], one.unsqueeze(2).to_broadcast([P, 4, T]))
            with dve.Fori(U_ROUTE // 2 + 8, U_ONES // 2) as ii:
                for s in range(2):
                    for f in range(4):
                        u_quarter(ii, s, f)

            grid = act_w[:].rearrange("p i t -> p t i")

            def hot(q, r, ks):
                for k in ks:
                    if k == 0:
                        dve.wait_ge(spread_mm, q + 1)
                    t = bass.ds(q * 4 + k, 1)
                    dve.tensor_scalar(hot_j[:, r, k, :], iota, ijgT[:, 1, t], None, ALU.is_equal)
                    ins = dve.tensor_scalar(hot_i[:, r, k, :], iota, ijgT[:, 0, t], ijgT[:, 2, t], ALU.is_equal, ALU.mult)
                if ks[-1] == 3:
                    ins.then_inc(hot_done, 1)

            def spread(q, r):
                dve.drain()
                dve.wait_ge(spread_mm, 2 + q + 1)
                g4 = grid[:, bass.ds(q * 4, 4), :]
                dve.tensor_tensor(g4, g4, bank(2 + r).rearrange("p (t i) -> p t i", t=4), ALU.mult).then_inc(spread_free, 1)

            def weigh(i, s):
                dve.drain()
                dve.wait_ge(gelu_done, i + 1)
                row = act_w[:, bass.ds(i, 1), :].rearrange("p a t -> p (a t)")
                dve.tensor_tensor(row, row, gelu_sb[:, s, :], ALU.mult).then_inc(gelu_free, 1)

            def u_spread_tile(ii, s, first=False):
                q = ii * 2 + s - U_ONES
                u_quarter(ii, s, 0)
                hot(q, s, (0, 1))
                u_quarter(ii, s, 1)
                hot(q, s, (2, 3))
                u_quarter(ii, s, 2)
                if first and s == 1:
                    dve.wait_ge(gelu_done, U_ONES)
                if not (first and s == 0):
                    spread(q - 1, 1 - s)
                u_quarter(ii, s, 3)
                if not first:
                    weigh(ii * 2 + s - 2, s)

            dve.sem_inc(spread_mm, 2)
            for s in range(2):
                u_spread_tile(U_ONES // 2, s, first=True)
            with dve.Fori(U_ONES // 2 + 1, P // 2) as ii:
                for s in range(2):
                    u_spread_tile(ii, s)
            weigh(P - 2, 0)
            spread(P - U_ONES - 1, 1)
            weigh(P - 1, 1)

            def v_low(ii, s, last=False):
                vh = [v_hi4[:, 2 * s + h, :] if last else v_hi[:, 2 * (s % 2) + h, :] for h in range(2)]
                mh, ml = (m_hi4[:, s, :], m_lo4[:, s, :]) if last else (m_hi[:, s % 2, :], m_lo[:, s % 2, :])
                dve.wait_ge(v_hi_done, ii * 8 + 2 * s + 1)
                dve.tensor_tensor(v_lo[:, 2 * s, :], v_raw[:, 2 * s, :], vh[0].bitcast(F32), ALU.subtract)
                dve.wait_ge(m_hi_done, ii * 4 + s + 1)
                dve.tensor_tensor(ml, act_w[:, bass.ds(ii * 4 + s, 1), :].rearrange("p a t -> p (a t)"), mh.bitcast(F32), ALU.subtract).then_inc(v_lo_done, 1)
                dve.wait_ge(v_hi_done, ii * 8 + 2 * s + 2)
                dve.tensor_tensor(v_lo[:, 2 * s + 1, :], v_raw[:, 2 * s + 1, :], vh[1].bitcast(F32), ALU.subtract).then_inc(v_lo_done, 1)

            with dve.Fori(0, P // 4 - 1) as ii:
                for s in range(4):
                    v_low(ii, s)
            for s in range(4):
                v_low(P // 4 - 1, s, last=True)
            dve.wait_ge(last_in, 48)

            def last_sum(a):
                for h in range(2):
                    c = slice(h * HALF, (h + 1) * HALF)
                    dve.wait_ge(sum_done, 2 * a + h + 1)
                    dve.scalar_tensor_tensor(h1_again[:, a, c], h1_again[:, a, c], float(ALPHA), bank(4 * a + 2 * h, 2), ALU.mult, ALU.add)
                dve.drain()
                for c in range(4):
                    dve.bn_stats(stat6[:, 4 * a + c, :], h1_again[:, a, c * COL:(c + 1) * COL])
                dve.drain()
                dve.bn_aggr(mv[:, a, :], stat6[:, 4 * a:4 * a + 4, :])
                dve.drain()
                dve.tensor_scalar(var16[:, a:a + 1], mv[:, a:a + 1, 1], EPS, None, ALU.add).then_inc(ln_stat, 1)

            for a in range(TT):
                last_sum(a)
                dve.wait_ge(ln_rstd, 2 + a)
                for b in range(4):
                    c = slice(b * COL, (b + 1) * COL)
                    norm_apply(dve, h1_again[:, a, c], ln2g_sb[:, c], ln2b_sb[:, c], a, y_done)

        @block.gpsimd
        def _(pool):
            def lo_steps(g, ks):
                for k in ks:
                    pool.wait_ge(hi_done, STEPS * g + k + 1)
                    pool.tensor_tensor(w_lo[:, k, :], raw[:, k, :], w_hi[:, k % HI_RING, :].bitcast(F32), ALU.subtract).then_inc(lo_done, 1)

            def ln_power(n, c):
                pool.wait_ge(ln_stat, n)
                pool.tensor_tensor(rstd[:, c], var16[:, c], power[:, c], ALU.pow).then_inc(ln_rstd, 1)

            with pool.Fori(0, B_END - 2) as g:
                lo_steps(g, range(STEPS))
            lo_steps(B_END - 2, range(4))
            pool.wait_ge(stat_done, 1)
            pool.tensor_tensor(rstd[:], var16[:], power[:], ALU.pow).then_inc(rstd_done, 1)
            lo_steps(B_END - 2, range(4, STEPS))
            with pool.Fori(B_END - 1, O_END) as g:
                lo_steps(g, range(STEPS))
            lo_steps(O_END, range(4))
            ln_power(1, slice(0, TT))
            lo_steps(O_END, range(4, STEPS))
            with pool.Fori(O_END + 1, Q_END) as g:
                lo_steps(g, range(STEPS))
            with pool.Fori(0, P) as i:
                for f in range(4):
                    pool.wait_ge(uhi_done, i * 4 + f + 1)
                    pool.tensor_tensor(u_lo[:, f, :], u_t[:, f, :], u_hi[:, f, :].bitcast(F32), ALU.subtract).then_inc(ulo_done, 1)
            for a in range(TT):
                ln_power(2 + a, slice(a, a + 1))

        @block.tensor
        def _(pe):
            by_tile = lambda s, a, k: s[:, a, k * P:(k + 1) * P]

            def turn(src, use, c, ready, n):
                q = use * 8 + c
                pe.wait_ge(ready, n)
                if c >= 4:
                    pe.wait_ge(tr_lo, q - 3)
                for k in range(2):
                    for a in range(TT):
                        o = (k * TT + a) * P
                        ins = pe.transpose(bank(4 + c % 4)[:, o:o + P], by_tile(src, a, 2 * c + k), ident)
                ins.then_inc(tr_done, 1)

            def three(o, lh, ll, rh, rl, start, stop, lint=False):
                pe.matmul(o, lh, rh, start=start, stop=False, skip_group_check=lint)
                pe.matmul(o, lh, rl, start=False, stop=False, skip_group_check=lint)
                return pe.matmul(o, ll, rh, start=False, stop=stop, skip_group_check=lint)

            def steps_n(g, ks=range(STEPS)):
                for k in ks:
                    if k == 0:
                        pe.wait_ge(acc_free, g + 1)
                    pe.wait_ge(lo_done, STEPS * g + k + 1)
                    for kt in (2 * k, 2 * k + 1):
                        for n in range(4):
                            c = slice(kt % 2 * COL + n * P, kt % 2 * COL + (n + 1) * P)
                            o = ps[:, 2 * (g % 2) + n // 2, (n % 2) * T:(n % 2 + 1) * T]
                            ins = three(o, w_hi[:, k % HI_RING, c], w_lo[:, k, c], xT_hi[:, kt, :], xT_lo[:, kt, :],
                                        kt == 0 and n % 2 == 0, kt == KT - 1, lint=True)
                    ins.then_inc(step_free, 1)

            def steps_t(g, ks=range(STEPS)):
                for k in ks:
                    if k == 0:
                        pe.wait_ge(acc_free, g + 1)
                    pe.wait_ge(lo_done, STEPS * g + k + 1)
                    for kt in (2 * k, 2 * k + 1):
                        c = slice(kt % 2 * COL, (kt % 2 + 1) * COL)
                        for a in range(TT):
                            t = slice(a * P, (a + 1) * P)
                            ins = three(ps[:, 2 * (g % 2) + a, :], xT_hi[:, kt, t], xT_lo[:, kt, t], w_hi[:, k % HI_RING, c], w_lo[:, k, c],
                                        kt == 0, kt == KT - 1)
                    ins.then_inc(step_free, 1)

            def turned_group(g, steps, src, use, ready, lead=LEAD):
                for c in range(lead):
                    turn(src, use, c, *ready(c))
                for k in range(STEPS):
                    pe.wait_ge(tr_lo, 8 * use + k + 1)
                    steps(g, (k,))
                    if k + lead < 8:
                        turn(src, use, k + lead, *ready(k + lead))

            pe.sem_inc(acc_free, 2)
            pe.wait_ge(keep_in, 16)
            turned_group(0, steps_n, x_sb, 0, lambda c: (x_in[c // 2], 16), lead=2)
            pe.wait_ge(glrw_lo, 1)
            for kt in range(KT):
                ins = three(bank(4)[:, 0:T], glr_hi[:, kt, :], glr_lo[:, kt, :], xT_hi[:, kt, :], xT_lo[:, kt, :], kt == 0, kt == KT - 1)
            ins.then_inc(glr_done, 1)
            steps_n(1, range(3))
            pe.wait_ge(wup_in, 32)
            pe.wait_ge(glrT_done, 1)
            for h in range(GH):
                ins = pe.matmul(bank(5, 2)[:, h * T:(h + 1) * T], wup_sb[:, h * P:(h + 1) * P], glrT[0:RANK, :], start=True, stop=True)
            ins.then_inc(logit_done, 1)
            steps_n(1, range(3, STEPS))
            steps_n(2)

            head_t = lambda t, h, a: t[:, h, a * P:(a + 1) * P]
            pe.wait_ge(decay_done, 1)
            chunk = lambda t, h, c: t[:, h, c * CH:(c + 1) * CH]
            for h in range(GH):
                for a in range(TT):
                    pe.matmul(bank(4)[0:CH, (h * TT + a) * CH:(h * TT + a + 1) * CH], chunk(k_out, h, 2 * a), chunk(q_in, h, 2 * a + 1), start=True, stop=True)
                for c in range(2):
                    pe.matmul(bank(5)[c * CH:(c + 1) * CH, h * P:(h + 1) * P], chunk(k_out, h, c),
                              q_far[:, h, 2 - 2 * c:4 - 2 * c, :].rearrange("p c n -> p (c n)"), start=True, stop=True)

            def level(n):
                if n:
                    pe.wait_ge(lvl_ready, n)
                if n == 1:
                    pe.wait_ge(far_sb, 1)
                if n >= 2:
                    pe.wait_ge(lvl_acc, n - 1)
                kk, qq = (lvl_k, lvl_q) if n else (proj_n[:, 4:8, :], proj_n[:, 0:4, :])
                for h in range(GH):
                    for a in range(TT):
                        o = (h * TT + a) * P
                        ins = pe.matmul(bank(6 - 2 * (n % 2), 2)[:, o:o + P], head_t(kk, h, a), head_t(qq, h, a), start=True, stop=True)
                ins.then_inc(lvl_mm, 1)

            level(0)
            for g in range(3, A_END):
                for half in range(2):
                    steps_n(g, range(4 * half, 4 * half + 4))
                    level(2 * (g - 3) + half + 1)

            rq, rk = (proj_n[:, n:n + 8, :].rearrange("p (h s) t -> p h s t", s=2) for n in (8, 16))

            def ret_scores(h):
                for b, (keys, queries) in enumerate(((0, 0), (1, 1), (0, 1))):
                    o = ((h % 2) * 3 + b) * P
                    for s in range(2):
                        ins = pe.matmul(bank(4 + 2 * (h // 2), 2)[:, o:o + P], rk[:, h, s, keys * P:(keys + 1) * P],
                                        rq[:, h, s, queries * P:(queries + 1) * P], start=s == 0, stop=s == 1)
                return ins

            def head_out(h, near, far, ret):
                v = [proj_v[:, a, K * ret + h * GDV:K * ret + (h + 1) * GDV] for a in range(TT)]
                o = [bank(4 + h)[:, a * GDV:(a + 1) * GDV] for a in range(TT)]
                pe.matmul(o[0], near(h, 0), v[0], start=True, stop=True)
                pe.matmul(o[1], near(h, 1), v[1], start=True, stop=False)
                return pe.matmul(o[1], far(h), v[0], start=False, stop=True)

            def gla_out(h):
                head_out(h, lambda h, a: head_t(a_gla, h, a), lambda h: a_far[:, h, :], 0).then_inc(o_mm, 1)

            def ret_out(h):
                pe.wait_ge(o_evac, h + 1)
                head_out(h, lambda h, a: a_ret[:, h, a, :], lambda h: a_ret[:, h, 2, :], 1).then_inc(ro_mm, 1)

            steps_t(A_END)
            steps_t(A_END + 1, range(4))
            pe.wait_ge(rot_done, RH)
            pe.wait_ge(lvl_acc, LEVELS + 1)
            for h in (0, 2):
                ret_scores(h)
                ret_scores(h + 1).then_inc(rs_mm, 1)
            steps_t(A_END + 1, range(4, STEPS))
            steps_t(A_END + 2, range(4))
            pe.wait_ge(ra_done, 2)
            gla_out(0)
            gla_out(1)
            steps_t(A_END + 2, range(4, STEPS))
            gla_out(2)
            gla_out(3)
            steps_t(A_END + 3)
            steps_t(V_END, range(4))
            ret_out(0)
            ret_out(1)
            steps_t(V_END, range(4, STEPS))
            ret_out(2)
            ret_out(3)
            for g in range(V_END + 1, B_END):
                steps_t(g)

            turned_group(B_END, steps_t, o_sb, 1, lambda c: (mix_done, c // 2 + 1))
            for g in range(B_END + 1, O_END):
                steps_t(g)
            pe.wait_ge(sk_in, 16)
            for c in range(4):
                for k in range(4):
                    ins = pe.transpose(bank(4 + c)[:, k * P:(k + 1) * P], sk_raw[:, 4 * c + k, :], ident)
                ins.then_inc(sk_mm, 1)
            pe.wait_ge(sk_sb, 4)
            turned_group(O_END, steps_n, h1_perm, 2, lambda c: (h1p_done, 2 * (c // 2) + 2))

            def query_scores(n):
                pe.wait_ge(acc_free, 2 + O_END + n + 1)
                if n >= 2:
                    pe.wait_ge(score_sb, n - 1)
                for a in range(TT):
                    for k in range(4):
                        r = 4 * n + k
                        ins = pe.matmul(bank(4 + 2 * (n % 2) + a)[:, k * NK:(k + 1) * NK], qT[:, r, a * P:(a + 1) * P], skT[:, r, :], start=True, stop=True)
                ins.then_inc(score_mm, 1)

            for g in range(O_END + 1, Q_END):
                steps_n(g, range(4))
                if g == O_END + 1:
                    pe.wait_ge(tr_lo, 24)
                query_scores(g - O_END - 1)
                steps_n(g, range(4, STEPS))
            pe.sem_inc(uparts_free, 4)

            def spread(q, s):
                pe.wait_ge(hot_done, q + 1)
                pe.wait_ge(spread_free, q + 1)
                for k in range(4):
                    ins = pe.matmul(bank(2 + s)[:, k * P:(k + 1) * P], hot_j[:, s, k, :], hot_i[:, s, k, :], start=True, stop=True)
                ins.then_inc(spread_mm, 1)

            def u_tile(ii, s, first=False, spreads=False):
                i = ii * 2 + s
                if not first:
                    pe.wait_ge(gelu_done, i - 1)
                for f in range(4):
                    if spreads and f == 3:
                        spread(i - U_ONES, s)
                    pe.wait_ge(ulo_done, ii * 8 + 4 * s + f + 1)
                    for k in range(4):
                        c = slice(k * P, (k + 1) * P)
                        kt = 4 * f + k
                        ins = three(bank(s)[:, 0:T], u_hi[:, f, c], u_lo[:, f, c], xT_hi[:, kt, :], xT_lo[:, kt, :], kt == 0, kt == KT - 1)
                    ins.then_inc(uparts_free, 1)

            u_tile(0, 0, first=True)
            query_scores(3)
            u_tile(0, 1, first=True)
            with pe.Fori(1, U_ROUTE // 2 - 1) as ii:
                for s in range(2):
                    u_tile(ii, s)
            pe.wait_ge(ijg_done, 8 + 1)
            for s in range(3):
                for a in range(TT):
                    o = (s * TT + a) * P
                    ins = pe.transpose(bank(4, 2)[:, o:o + P], ijg[:, s, a, :], ident)
            ins.then_inc(ijg_mm, 1)
            with pe.Fori(U_ROUTE // 2 - 1, U_ONES // 2) as ii:
                for s in range(2):
                    u_tile(ii, s)
            pe.sem_inc(spread_free, 2)
            with pe.Fori(U_ONES // 2, P // 2) as ii:
                for s in range(2):
                    u_tile(ii, s, spreads=True)

            def v_products(s, h, a, start=False, last=False, stop=False):
                t = slice(a * P, (a + 1) * P)
                mh, ml = (m_hi4[:, s, t], m_lo4[:, s, t]) if last else (m_hi[:, s % 2, t], m_lo[:, s % 2, t])
                vh, vl = v_hi4[:, 2 * s + h, :] if last else v_hi[:, 2 * (s % 2) + h, :], v_lo[:, 2 * s + h, :]
                for p, (m, v) in enumerate(((mh, vh), (mh, vl), (ml, vh))):
                    for c in range(2):
                        ins = pe.matmul(bank(4 * a + 2 * h + c), m, v[:, c * 512:(c + 1) * 512], start=start and p == 0, stop=stop and p == 2)
                return ins

            def v_tile(i, s, start=False):
                for h in range(2):
                    pe.wait_ge(v_lo_done, 2 * i + h + 1)
                    for a in range(TT):
                        ins = v_products(s, h, a, start=start)
                    ins.then_inc(v_free, 1)

            pe.wait_ge(spread_free, 2 + P - U_ONES)
            for i in range(4):
                v_tile(i, i, start=i == 0)
            with pe.Fori(1, P // 4 - 1) as ii:
                for s in range(4):
                    v_tile(ii * 4 + s, s)
            for a in range(TT):
                for s in range(4):
                    for h in range(2):
                        if a == 0:
                            pe.wait_ge(v_lo_done, 2 * (P - 4 + s) + h + 1)
                        ins = v_products(s, h, a, last=True, stop=s == 3)
                        if s == 3:
                            ins.then_inc(sum_done, 1)


_INS = ["x", "w_in", "w_gla_gate_up", "b_gla_gate", "gla_norm_g", "ret_norm_g", "w_out", "ln1_g", "ln1_b",
        "w_peer_q", "peer_subkeys", "peer_u", "peer_v", "ln2_g", "ln2_b"]


def kernel(**inputs):
    import concourse.bacc as bacc
    from concourse.bass_utils import run_bass_kernel_spmd

    nc = bacc.Bacc("TRN2", target_bir_lowering=False, num_devices=1)
    keep_c, mix_c = constants()
    arrays, args = {}, []
    for name, a in [(n, inputs[n]) for n in _INS] + [("keep_c", keep_c), ("mix_c", mix_c)]:
        a = np.ascontiguousarray(a)
        arrays[f"in_{name}"] = a
        args.append(nc.dram_tensor(f"in_{name}", a.shape, mybir.dt.from_np(a.dtype), kind="ExternalInput").ap())
    args.append(nc.dram_tensor("out_0", (1, T, D), F32, kind="ExternalOutput").ap())
    build(nc, *args)
    r = run_bass_kernel_spmd(nc, [arrays], core_ids=[0])
    return r.results[0]["out_0"]
```
